# Optimizing a Trainium2 kernel written in Bass

```python
import math
import jax, jax.numpy as jnp
from jax import lax
import numpy as np

D_MODEL = 1024
BATCH = 1
SEQ = 512
DEPTH = 1

CHUNK = 64
Q_BLOCK = 128
PLE_DIM = 256
D_MIX = D_MODEL
D_ATTN = D_MIX // 2
D_CONV = D_MIX - D_ATTN
N_HEADS_A = 4
HEAD_DIM_V = D_ATTN // N_HEADS_A
HEAD_DIM_QK = HEAD_DIM_V // 2
CONV_WIDTH = 3
N_IN_PARTS = 8
D_IN = 4 * D_ATTN + 4 * D_CONV
EPS = 1e-6
SUBLN_EPS = 1e-5


def rms_norm(x, gain, eps=EPS):
    xf = x.astype(jnp.float32)
    y = xf * lax.rsqrt(jnp.mean(xf * xf, axis=-1, keepdims=True) + eps)
    return (y * gain.astype(jnp.float32)).astype(x.dtype)

def alibi_slopes(n_heads):
    return jnp.exp2(-8.0 * jnp.arange(1, n_heads + 1, dtype=jnp.float32) / n_heads)

def diff_attention(q, k, v, lam, slopes):
    seq = q.shape[1]
    scale = HEAD_DIM_QK ** -0.5
    outs = []
    for q0 in range(0, seq, Q_BLOCK):
        k_end = q0 + Q_BLOCK
        t = jnp.arange(q0, k_end)
        s = jnp.arange(k_end)
        scores = jnp.einsum('bqhmd,bkhmd->bhmqk', q[:, q0:k_end], k[:, :k_end]).astype(jnp.float32) * scale
        dist = jnp.abs(t[:, None] - s[None, :]).astype(jnp.float32)
        allowed = (s[None, :] // CHUNK) <= (t[:, None] // CHUNK)
        bias = jnp.where(allowed[None], -slopes[:, None, None] * dist[None], -jnp.inf)
        probs = jax.nn.softmax(scores + bias[None, :, None], axis=-1)
        weights = probs[:, :, 0] - lam * probs[:, :, 1]
        outs.append(jnp.einsum('bhqk,bkhd->bqhd', weights.astype(v.dtype), v[:, :k_end]))
    return jnp.concatenate(outs, axis=1)

def first_inputs(seed: int = 0) -> dict:
    key = jax.random.key(seed)
    ks = jax.random.split(key, 16)
    f32 = jnp.float32
    x = jax.random.normal(ks[0], (BATCH, SEQ, D_MODEL), f32)
    p = jax.random.normal(ks[1], (DEPTH, BATCH, SEQ, PLE_DIM), f32)
    pre_norm_gain = 1.0 + 0.02 * jax.random.normal(ks[2], (DEPTH, D_MODEL), f32)
    w_in = jax.random.normal(ks[3], (DEPTH, D_MODEL, D_IN), f32) * D_MODEL ** -0.5
    lambda_q1 = 0.1 * jax.random.normal(ks[4], (DEPTH, HEAD_DIM_QK), f32)
    lambda_k1 = 0.1 * jax.random.normal(ks[5], (DEPTH, HEAD_DIM_QK), f32)
    lambda_q2 = 0.1 * jax.random.normal(ks[6], (DEPTH, HEAD_DIM_QK), f32)
    lambda_k2 = 0.1 * jax.random.normal(ks[7], (DEPTH, HEAD_DIM_QK), f32)
    subln_gain = 1.0 + 0.02 * jax.random.normal(ks[8], (DEPTH, HEAD_DIM_V), f32)
    conv_w = jax.random.normal(ks[9], (DEPTH, CONV_WIDTH, D_CONV), f32) * CONV_WIDTH ** -0.5
    w_out = jax.random.normal(ks[10], (DEPTH, D_MIX, D_MODEL), f32) * D_MIX ** -0.5
    post_norm_gain = 1.0 + 0.02 * jax.random.normal(ks[11], (DEPTH, D_MODEL), f32)
    w_ple_proj = jax.random.normal(ks[12], (DEPTH, PLE_DIM, D_MODEL), f32) * PLE_DIM ** -0.5
    ple_norm_gain = 1.0 + 0.02 * jax.random.normal(ks[13], (DEPTH, D_MODEL), f32)
    w_ple_gate = jax.random.normal(ks[14], (DEPTH, D_MODEL, D_MODEL), f32) * D_MODEL ** -0.5
    return {"x": x, "p": p, "pre_norm_gain": pre_norm_gain, "w_in": w_in,
            "lambda_q1": lambda_q1, "lambda_k1": lambda_k1, "lambda_q2": lambda_q2,
            "lambda_k2": lambda_k2, "subln_gain": subln_gain, "conv_w": conv_w,
            "w_out": w_out, "post_norm_gain": post_norm_gain, "w_ple_proj": w_ple_proj,
            "ple_norm_gain": ple_norm_gain, "w_ple_gate": w_ple_gate}

def first_block(x, p, pre_norm_gain, w_in, lambda_q1, lambda_k1, lambda_q2, lambda_k2,
              subln_gain, conv_w, w_out, post_norm_gain, w_ple_proj, ple_norm_gain, w_ple_gate):
    bsz, seq, _ = x.shape
    slopes = alibi_slopes(N_HEADS_A)
    for i in range(DEPTH):
        lambda_init = 0.8 - 0.6 * math.exp(-0.3 * i)
        h = rms_norm(x, pre_norm_gain[i])
        proj = h @ w_in[i]
        q, k, v, z_a, b_gate, c_gate, u, z_c = jnp.split(proj, N_IN_PARTS, axis=-1)

        q = q.reshape(bsz, seq, N_HEADS_A, 2, HEAD_DIM_QK)
        k = k.reshape(bsz, seq, N_HEADS_A, 2, HEAD_DIM_QK)
        v = v.reshape(bsz, seq, N_HEADS_A, HEAD_DIM_V)
        lam = (jnp.exp(jnp.sum((lambda_q1[i] * lambda_k1[i]).astype(jnp.float32)))
               - jnp.exp(jnp.sum((lambda_q2[i] * lambda_k2[i]).astype(jnp.float32)))
               + lambda_init)
        attn = diff_attention(q, k, v, lam, slopes)
        attn = rms_norm(attn, subln_gain[i], SUBLN_EPS) * (1.0 - lambda_init)
        attn = attn.reshape(bsz, seq, D_ATTN) * jax.nn.silu(z_a)

        g = c_gate * u
        g_pad = jnp.pad(g, ((0, 0), (CONV_WIDTH - 1, 0), (0, 0)))
        conv = conv_w[i, 0] * g_pad[:, 0:seq]
        for j in range(1, CONV_WIDTH):
            conv = conv + conv_w[i, j] * g_pad[:, j:j + seq]
        conv_out = b_gate * conv * jax.nn.silu(z_c)

        mixed = jnp.concatenate([attn, conv_out], axis=-1) @ w_out[i]
        x = x + rms_norm(mixed, post_norm_gain[i])

        e = rms_norm(p[i] @ w_ple_proj[i], ple_norm_gain[i])
        x = x + jax.nn.sigmoid(x @ w_ple_gate[i]) * e
    return x


DEPTH_2 = 2

N_MIXERS = 2
FOURIER_GROUPS = 4
FOURIER_GROUP_DIM = D_MODEL // FOURIER_GROUPS
RET_HEADS = 4
RET_QK_DIM = D_MODEL // RET_HEADS
RET_V_DIM = 2 * RET_QK_DIM
RET_CHUNK = 128
ROPE_BASE = 10000.0
D_FF = -(-8 * D_MODEL // (3 * 256)) * 256


def rmsnorm(x, g):
    xf = x.astype(jnp.float32)
    y = xf * lax.rsqrt(jnp.mean(xf * xf, axis=-1, keepdims=True) + EPS)
    return (y * g.astype(jnp.float32)).astype(x.dtype)

def modulate(h, shift, scale):
    return h * (1.0 + scale[:, None, :]) + shift[:, None, :]

def fourier_mixer(h, w_o):
    B, S, D = h.shape
    hg = h.astype(jnp.float32).reshape(B, S, FOURIER_GROUPS, FOURIER_GROUP_DIM)
    f = jnp.fft.fftn(hg, axes=(1, 3), norm="ortho").real.astype(h.dtype)
    return f.reshape(B, S, D) @ w_o

def rotary(x, pos):
    half = x.shape[-1] // 2
    inv_freq = ROPE_BASE ** (-jnp.arange(half, dtype=jnp.float32) / half)
    ang = pos[:, None] * inv_freq[None, :]
    cos, sin = jnp.cos(ang), jnp.sin(ang)
    x1, x2 = x[..., :half], x[..., half:]
    return jnp.concatenate([x1 * cos - x2 * sin, x1 * sin + x2 * cos], axis=-1)

def chunk_retention(q, k, v, log_gamma, inclusive):
    B, H, S, dk = q.shape
    dv = v.shape[-1]
    C = RET_CHUNK
    N = S // C
    to_chunks = lambda a: jnp.moveaxis(a.reshape(B, H, N, C, a.shape[-1]), 2, 0)
    qc, kc, vc = to_chunks(q), to_chunks(k), to_chunks(v)

    t = jnp.arange(C)
    diff = t[:, None] - t[None, :]
    mask = (diff >= 0) if inclusive else (diff > 0)
    lg = log_gamma.astype(jnp.float32)[:, None, None]
    dmask = jnp.where(mask, jnp.exp(jnp.where(mask, diff, 0).astype(jnp.float32) * lg), 0.0)
    tf = t.astype(jnp.float32)[None, :, None]
    q_decay = jnp.exp((tf + 1.0) * lg)
    k_decay = jnp.exp((C - 1.0 - tf) * lg)
    chunk_decay = jnp.exp(C * lg)

    def step(R, xs):
        qb, kb, vb = xs
        scores = jnp.einsum('bhtd,bhsd->bhts', qb, kb) * dmask
        inner = jnp.einsum('bhts,bhsv->bhtv', scores, vb)
        cross = jnp.einsum('bhtd,bhdv->bhtv', qb, R) * q_decay
        R = R * chunk_decay + jnp.einsum('bhsd,bhsv->bhdv', kb * k_decay, vb)
        return R, inner + cross

    R0 = jnp.zeros((B, H, dk, dv), jnp.float32)
    _, out = lax.scan(step, R0, (qc, kc, vc))
    return jnp.moveaxis(out, 0, 2).reshape(B, H, S, dv)

def retention_mixer(h, w_in, w_out, log_g_fwd, log_g_bwd):
    B, S, _ = h.shape
    H, dk, dv = RET_HEADS, RET_QK_DIM, RET_V_DIM
    proj = h @ w_in
    q, k, v, g = jnp.split(proj, [H * dk, 2 * H * dk, 2 * H * dk + H * dv], axis=-1)
    heads = lambda a, d: a.astype(jnp.float32).reshape(B, S, H, d).transpose(0, 2, 1, 3)
    pos = jnp.arange(S, dtype=jnp.float32)
    q = rotary(heads(q, dk), pos)
    k = rotary(heads(k, dk), pos) * (dk ** -0.5)
    v = heads(v, dv)
    y_fwd = chunk_retention(q, k, v, log_g_fwd, True)
    flip = lambda a: jnp.flip(a, axis=2)
    y_bwd = flip(chunk_retention(flip(q), flip(k), flip(v), log_g_bwd, False))
    y = y_fwd + y_bwd
    mu = jnp.mean(y, axis=-1, keepdims=True)
    var = jnp.mean(jnp.square(y - mu), axis=-1, keepdims=True)
    y = (y - mu) * lax.rsqrt(var + EPS)
    y = y.transpose(0, 2, 1, 3).reshape(B, S, H * dv).astype(h.dtype)
    return (jax.nn.silu(g) * y) @ w_out

def swiglu(h, w_in, w_out):
    gate, up = jnp.split(h @ w_in, 2, axis=-1)
    return (jax.nn.silu(gate) * up) @ w_out

def second_inputs(seed: int = 0) -> dict:
    key = jax.random.key(seed)
    ks = jax.random.split(key, 14)
    D, F = D_MODEL, D_FF
    n_four = len(range(0, DEPTH_2, N_MIXERS))
    n_ret = len(range(1, DEPTH_2, N_MIXERS))
    ret_in_w = 2 * RET_HEADS * RET_QK_DIM + 2 * RET_HEADS * RET_V_DIM
    ret_v_w = RET_HEADS * RET_V_DIM
    nrm = lambda k, shape, s: jax.random.normal(k, shape, jnp.float32) * s
    return {
        "x": nrm(ks[0], (BATCH, SEQ, D), 1.0),
        "c": nrm(ks[1], (BATCH, D), 1.0),
        "w_ada": nrm(ks[2], (DEPTH_2, D, 6 * D), 0.5 * D ** -0.5),
        "b_ada": nrm(ks[3], (DEPTH_2, 6 * D), 0.01),
        "norm_mix_g": 1.0 + nrm(ks[4], (DEPTH_2, D), 0.02),
        "norm_ffn_g": 1.0 + nrm(ks[5], (DEPTH_2, D), 0.02),
        "w_fourier_out": nrm(ks[6], (n_four, D, D), D ** -0.5),
        "w_ret_in": nrm(ks[7], (n_ret, D, ret_in_w), D ** -0.5),
        "w_ret_out": nrm(ks[8], (n_ret, ret_v_w, D), ret_v_w ** -0.5),
        "w_ffn_in": nrm(ks[9], (DEPTH_2, D, 2 * F), D ** -0.5),
        "w_ffn_out": nrm(ks[10], (DEPTH_2, F, D), F ** -0.5),
        "final_norm_g": 1.0 + nrm(ks[11], (D,), 0.02),
        "w_ada_final": nrm(ks[12], (D, 2 * D), 0.5 * D ** -0.5),
        "b_ada_final": nrm(ks[13], (2 * D,), 0.01),
    }

def second_block(x, c, w_ada, b_ada, norm_mix_g, norm_ffn_g, w_fourier_out, w_ret_in, w_ret_out,
              w_ffn_in, w_ffn_out, final_norm_g, w_ada_final, b_ada_final):
    hidx = jnp.arange(RET_HEADS, dtype=jnp.float32)
    log_g_fwd = jnp.log1p(-jnp.exp2(-5.0 - hidx))
    log_g_bwd = jnp.flip(log_g_fwd)
    c_act = jax.nn.silu(c)
    for i in range(DEPTH_2):
        mod = c_act @ w_ada[i] + b_ada[i]
        sh1, sc1, g1, sh2, sc2, g2 = jnp.split(mod, 6, axis=-1)
        h = modulate(rmsnorm(x, norm_mix_g[i]), sh1, sc1)
        j = i // N_MIXERS
        if i % N_MIXERS == 0:
            m = fourier_mixer(h, w_fourier_out[j])
        else:
            m = retention_mixer(h, w_ret_in[j], w_ret_out[j], log_g_fwd, log_g_bwd)
        x = x + g1[:, None, :] * m
        h = modulate(rmsnorm(x, norm_ffn_g[i]), sh2, sc2)
        x = x + g2[:, None, :] * swiglu(h, w_ffn_in[i], w_ffn_out[i])
    shf, scf = jnp.split(c_act @ w_ada_final + b_ada_final, 2, axis=-1)
    return modulate(rmsnorm(x, final_norm_g), shf, scf)


def setup_inputs(seed=0):
    out = dict(first_inputs(seed))
    for name, value in second_inputs(seed + 1).items():
        if name != "x":
            out[name + "_2"] = value
    return out


def reference(
    x, p, pre_norm_gain, w_in, lambda_q1, lambda_k1, lambda_q2, lambda_k2, subln_gain, conv_w,
    w_out, post_norm_gain, w_ple_proj, ple_norm_gain, w_ple_gate, c_2, w_ada_2, b_ada_2,
    norm_mix_g_2, norm_ffn_g_2, w_fourier_out_2, w_ret_in_2, w_ret_out_2, w_ffn_in_2,
    w_ffn_out_2, final_norm_g_2, w_ada_final_2, b_ada_final_2,
):
    x = first_block(
        x, p, pre_norm_gain, w_in, lambda_q1, lambda_k1, lambda_q2, lambda_k2, subln_gain,
        conv_w, w_out, post_norm_gain, w_ple_proj, ple_norm_gain, w_ple_gate,
    )
    return second_block(
        x, c_2, w_ada_2, b_ada_2, norm_mix_g_2, norm_ffn_g_2, w_fourier_out_2, w_ret_in_2,
        w_ret_out_2, w_ffn_in_2, w_ffn_out_2, final_norm_g_2, w_ada_final_2, b_ada_final_2,
    )


_drawn_inputs = setup_inputs


def setup_inputs(seed=0):
    import zlib

    import numpy as np

    out = dict(_drawn_inputs(seed))
    spreads = {}
    factors = {'lambda_k1': 4.164,
     'lambda_q2': 4.39,
     'subln_gain': 6.354,
     'post_norm_gain': 4.275,
     'ple_norm_gain': 7.597,
     'b_ada_2': 5.312,
     'norm_mix_g_2': 44.333,
     'norm_ffn_g_2': 8.0,
     'final_norm_g_2': 8.049,
     'b_ada_final_2': 4.289}
    for name, (base, spread) in spreads.items():
        noise = np.random.default_rng([zlib.crc32(name.encode()), seed]).standard_normal(out[name].shape)
        drawn = base * np.exp(spread * noise) if base else spread * noise
        out[name] = __import__('jax').numpy.asarray(drawn.astype(out[name].dtype))
    for name, factor in factors.items():
        out[name] = (out[name] * factor).astype(out[name].dtype)
    return out
```

```python
import concourse.bass as bass
from concourse import mybir
from contextlib import ExitStack

P = 128
S = 512
D = 1024
KD = D // P
NH = 4
FF = 2816
FT = FF // P
HALF = (12, FT - 12)
TB = S // P
RING = 4
LAM_INIT = 0.2
N_ADA = 14
ADA_RING = 2
ADA_LAG = 6

COL = {}
NCOL = 0
for _name, _n in (("pre", KD), ("post", KD), ("ple", KD), ("final", KD), ("subln", 1), ("conv", 3 * NH),
                  ("c", KD), ("b_ada", N_ADA * KD), ("mix", 2 * KD), ("ffn", 2 * KD), ("lam", 4 * 64),
                  ("slope", NH), ("ident", P)):
    COL[_name] = NCOL
    NCOL += _n


def gemm_order(K, M, ks=None, first_outer=True):
    ks = list(ks or range(K))
    out = []
    m0 = 0
    if first_outer:
        m0 = 4
        out += [(k, m) for k in ks[:-2] for m in range(4)]
        out += [(k, m) for m in range(4) for k in ks[-2:]]
    return out + [(k, m) for m in range(m0, M) for k in ks]


ATT_KS = (0, 1, 2, 4, 5, 6, 7, 3)
CH = {}
_c = 0
for _name, _n in (("body", 8 * NH), ("out", 8), ("ple", 2), ("gate", 8), ("dft1", 1), ("dft2", 4), ("fout", 8),
                  ("up0a", 24), ("down0a", 12), ("up0b", 20), ("down0b", 10),
                  ("ret", 12), ("retbody", 16 * (NH - 1)), ("retout", 4),
                  ("up1a", 24), ("down1a", 12), ("up1b", 20), ("down1b", 10)):
    CH[_name] = _c
    _c += _n
N_CHUNK = _c

TI = {}
_c = 0
for _name, _n in (("body", 8 * NH), ("out", 8), ("ple", 8), ("gate", 8), ("dft1", 16), ("dft2", 8), ("fout", 8),
                  ("up0a", 24), ("down0a", 8), ("up0b", 20), ("down0b", 8),
                  ("ret", 20), ("retbody", 28 * (NH - 1)), ("retout", 8),
                  ("up1a", 24), ("down1a", 8), ("up1b", 20), ("down1b", 8)):
    TI[_name] = _c
    _c += _n

AUX = {}
_c = 0
for _name, _n in (("pre", 1), ("body", 7 * NH), ("post", 1), ("ada4", 1), ("ple", 1), ("four", 1), ("ada5", 1),
                  ("ada6", 1), ("ffn0", 1), ("ada7", 1), ("ada", 6), ("rnorm", 1),
                  ("ret", 2 * NH), ("ffn1", 1), ("final", 1)):
    AUX[_name] = _c
    _c += _n


class At:

    def __init__(self, i=None, **per):
        self.i, self.per = i, per

    def __call__(self, kind, n):
        return n if self.i is None else self.i * self.per[kind] + n


class Head(At):

    def __call__(self, kind, n):
        ahead = self.per[kind] if kind in ("aux", "four", "three", "one", "sixteen") else 0
        return super().__call__(kind, n + ahead)

    def before(self):
        return At(self.i, **self.per)


def build(nc, W, ADA, XT, PT, COLS, DIST, ROPE, DECAY, OUT):
    fp32, f32r = mybir.dt.float32, mybir.dt.float32r
    ALU, ACT, AX = mybir.AluOpType, mybir.ActivationFunctionType, mybir.AxisListType
    ctx = ExitStack()
    with ctx:
        def sb(name, shape, dt=fp32):
            return ctx.enter_context(nc.sbuf_tensor(name, shape, dt))

        def sem(name):
            return ctx.enter_context(nc.semaphore(name))

        w_raw = sb("w_raw", [P, RING, 1024])
        w_hi = sb("w_hi", [P, RING, 1024], f32r)
        w_lo = sb("w_lo", [P, RING, 1024], f32r)
        ada_raw = sb("ada_raw", [P, ADA_RING, 1024])
        ada_acc = sb("ada_acc", [P, 1024])
        X = sb("X", [P, KD, S])
        a_hi = sb("a_hi", [P, KD, S], f32r)
        a_lo = sb("a_lo", [P, KD, S], f32r)
        b_hi = sb("b_hi", [P, 12, S], f32r)
        b_lo = sb("b_lo", [P, 12, S], f32r)
        sq = sb("sq", [P, 2, S])
        sqsum = sb("sqsum", [P, S])
        rinv = sb("rinv", [P, S])
        tmp = sb("tmp", [P, 2, S])
        cols = sb("cols", [P, NCOL])
        ones = sb("ones", [P, P])
        small = sb("small", [P, 64])
        mod = sb("mod", [P, N_ADA * KD])
        gs = sb("gs", [P, 5 * KD])
        scr = sb("scr", [P, 9216])
        banks = ctx.enter_context(nc.psum_tensor("banks", [P, 8, 512], fp32))
        aux = banks[:, 7, :]

        ident = cols[:, COL["ident"]:COL["ident"] + P]
        zero, eps6, eps5, neglam, gsub = (small[:, n:n + 1] for n in range(5))
        lamv = small[:, 6:8]
        mx, nmx, rsum, rrec, c1 = (small[:, n:n + 2] for n in (8, 10, 12, 14, 16))
        lamp = small[:, 18:20]
        cact = small[:, 24:32]
        ctanh = small[:, 32:40]
        gple = small[:, 40:48]
        cwork = small[:, 48:56]

        def area(n, k=1):
            v = scr[:, n * S:(n + k) * S]
            return v if k == 1 else v.rearrange("p (k s) -> p k s", k=k)

        Q, K, VB, ZA, dist, bias = (area(n) for n in range(6))
        SC = area(6, 4).rearrange("p (u m) s -> p u m s", m=2)
        WT = area(10, 2)
        CG = area(12)
        G = scr[:, 13 * S:14 * S + 2]
        lamt = scr[:, 15 * S:15 * S + 256]
        MIX, E = area(0, 8), area(8, 8)
        PV = scr[:, 16 * S:18 * S]
        T2 = area(0, 2)
        SG = area(2, 2)
        HD = area(4, 2)
        GG, Y = area(0, 4), area(4, 4)
        COS, SIN = area(8), area(9)
        DEC = scr[:, 10 * S:10 * S + 896]
        RT = area(12, 4)

        raw_in = [sem(f"raw_in{s}") for s in range(RING)]
        whi = sem("whi")
        wlo = sem("wlo")
        w_used = sem("w_used")
        ada_in = [sem(f"ada_in{s}") for s in range(ADA_RING)]
        ada_sum = sem("ada_sum")
        x_in, cols_in, p_in, dist_in, rope_in, dec_in = (
            sem(n) for n in ("x_in", "cols_in", "p_in", "dist_in", "rope_in", "dec_in"))
        const = sem("const")
        link_s = sem("dve_link")
        tile_ready = sem("tile_ready")
        bank_read = [sem(f"bank_read{b}") for b in range(4)]
        aux_ready, aux_free = sem("aux_ready"), sem("aux_free")
        sq_ready, sq_added, r_ready = sem("sq_ready"), sem("sq_added"), sem("r_ready")
        h_ready, h_hi, a_ready = sem("h_ready"), sem("h_hi"), sem("a_ready")
        lam_in, lam_e = sem("lam_in"), sem("lam_e")
        za_t, sc_ready, sc_read, nm_ready, ex_ready, w_ready = (
            sem(n) for n in ("za_t", "sc_ready", "sc_read", "nm_ready", "ex_ready", "w_ready"))
        v_hi, wt_hi, pv_ready, o_copied, o_sq, o_r, o_out, mix_hi, mix_ready = (
            sem(n) for n in ("v_hi", "wt_hi", "pv_ready", "o_copied", "o_sq", "o_r", "o_out", "mix_hi",
                             "mix_ready"))
        zc_t, cv_out = sem("zc_t"), sem("cv_out")
        p_hi, p_ready = sem("p_hi"), sem("p_ready")
        x_new, xg_hi, xg_ready, e_copied, e_ready, gt = (
            sem(n) for n in ("x_new", "xg_hi", "xg_ready", "e_copied", "e_ready", "gt"))
        z_hi, f_hi = sem("z_hi"), sem("f_hi")
        hid_t, hid_s, hid_f, hid_hi, hid_ready = (sem(n) for n in ("hid_t", "hid_s", "hid_f", "hid_hi", "hid_ready"))
        x_done = sem("x_done")
        rot, rot_hi, rot_ready, vv_hi, gg_t, pd, pd_hi, y_sum, y_cen, y_sq, y_qs, y_r, y_f, y_hi, y_ready = (
            sem(n) for n in ("rot", "rot_hi", "rot_ready", "vv_hi", "gg_t", "pd", "pd_hi", "y_sum",
                             "y_cen", "y_sq", "y_qs", "y_r", "y_f", "y_hi", "y_ready"))
        out_done = sem("out_done")

        block = ctx.enter_context(nc.Block())
        NORMS = dict(pre=0, post=1, ple=2, four=3, ffn0=4, rnorm=5, ffn1=6, final=7)
        APPLY = dict(pre=0, four=1, ffn0=2, rnorm=3, ffn1=4)

        def col(name, n=0, k=1):
            return cols[:, COL[name] + n:COL[name] + n + k]

        def wait_tile(eng, at, t):
            eng.wait_ge(tile_ready, at("tile", t + 1))

        def read_out(ins, t):
            ins.then_inc(bank_read[t % 4], 1)

        def wait_read(eng, at, t):
            eng.wait_ge(bank_read[t % 4], at("bank", t // 4 + 1))

        flat = At()

        @block.sync
        def _(sp):
            def load_w(at, c, first=False):
                if not first:
                    sp.wait_ge(wlo, at("chunk", c - RING + 1))
                src = W[c] if at.i is None else W[bass.ds(at("chunk", c), 1), :, :].rearrange("a p n -> (a p) n")
                sp.dma_start(w_raw[:, c % RING, :], src).then_inc(raw_in[c % RING], 16)

            def load_ada(at, a, first=False):
                if not first:
                    sp.wait_ge(ada_sum, at("ada", a - ADA_RING + 1))
                src = ADA[a] if at.i is None else ADA[bass.ds(at("ada", a), 1), :, :].rearrange("a p n -> (a p) n")
                sp.dma_start(ada_raw[:, a % ADA_RING, :], src).then_inc(ada_in[a % ADA_RING], 16)

            for c in range(ADA_LAG):
                load_w(flat, c, c < RING)
            for n in range(4):
                load_w(flat, ADA_LAG + n)
                load_ada(flat, n, n < ADA_RING)
            with sp.Fori(0, 15) as i:
                at = At(i, chunk=4, ada=4)
                for n in range(4):
                    load_w(at, ADA_LAG + 4 + n)
                    load_ada(at, 4 + n)
            c0 = ADA_LAG + 64
            with sp.Fori(0, 6) as i:
                at = At(i, chunk=4, ada=8)
                for n in range(4):
                    load_w(at, c0 + n)
                    load_ada(at, 64 + 2 * n)
                    load_ada(at, 65 + 2 * n)
            c0 += 24
            turns = (N_CHUNK - c0) // 4
            with sp.Fori(0, turns) as i:
                at = At(i, chunk=4)
                for n in range(4):
                    load_w(at, c0 + n)
            for c in range(c0 + 4 * turns, N_CHUNK):
                load_w(flat, c)
            for m in range(KD):
                sp.wait_ge(x_done, m + 1)
                sp.dma_start(OUT[:, m, :], X[:, m, :]).then_inc(out_done, 16)
            sp.wait_ge(out_done, 16 * KD)

        @block.gpsimd
        def _(pool):
            def lo_part(at, c, first=False):
                pool.wait_ge(whi, at("chunk", c + 1))
                pool.tensor_tensor(w_lo[:, c % RING, :], w_raw[:, c % RING, :],
                                   w_hi[:, c % RING, :].bitcast(fp32), ALU.subtract).then_inc(wlo, 1)

            n = N_CHUNK // 4
            with pool.Fori(0, n) as i:
                at = At(i, chunk=4)
                for s in range(4):
                    lo_part(at, s)
            for c in range(4 * n, N_CHUNK):
                lo_part(flat, c)

        @block.scalar
        def _(act):
            act.dma_start(cols[:, :], COLS).then_inc(cols_in, 16)
            act.dma_start(X[:, :, :], XT).then_inc(x_in, 16)
            act.dma_start(dist, DIST).then_inc(dist_in, 16)

            def split_w(at, c, first=False):
                if c >= N_CHUNK:
                    return
                act.wait_ge(raw_in[c % RING], at("slot", 16 * (c // RING + 1)))
                if not first:
                    act.wait_ge(w_used, at("chunk", c - RING + 1))
                act.activation(w_hi[:, c % RING, :], w_raw[:, c % RING, :], ACT.Copy).then_inc(whi, 1)

            def square(at, v, m, src):
                if m >= 3:
                    act.wait_ge(sq_added, 7 * v + m - 2)
                dst = sqsum[:, :] if m == 0 else sq[:, m % 2, :]
                act.activation(dst, src, ACT.Square).then_inc(sq_ready, 1)

            def rsqrt(u, n, eps, done, at=flat):
                act.wait_ge(aux_ready, at("aux", u + 1))
                act.activation(rinv[:, :], aux, ACT.Ln, bias=eps, scale=1.0 / n).then_inc(aux_free, 1)
                act.wait_ge(aux_free, at("aux", u + 1))
                act.activation(rinv[:, :], rinv[:, :], ACT.Exp, scale=-0.5).then_inc(done, 1)

            def norm_hi(v, c=None):
                for m in range(KD):
                    if m == 2 and c is not None:
                        split_w(flat, c)
                    act.wait_ge(h_ready, 8 * v + m + 1)
                    act.activation(a_hi[:, m, :], tmp[:, m % 2, :], ACT.Copy).then_inc(h_hi, 1)

            for c in range(RING):
                split_w(flat, c, True)
            act.wait_ge(cols_in, 16)
            act.activation(ctanh, col("c", 0, KD), ACT.Tanh, scale=0.5).then_inc(lam_e, 1)
            act.wait_ge(lam_in, 1)
            act.activation(lamv, lamp, ACT.Exp).then_inc(lam_e, 1)
            act.wait_ge(x_in, 16)
            for m in range(KD):
                square(flat, 0, m, X[:, m, :])
            act.wait_ge(const, 1)
            rsqrt(AUX["pre"], D, eps6, r_ready)
            norm_hi(0)

            t0, c0 = TI["body"], CH["body"]

            def exps(at, b):
                n = (b + 1) * P
                act.wait_ge(nm_ready, at("unit", b + 1))
                for m in range(2):
                    act.activation(SC[:, b % 2, m, 0:n], SC[:, b % 2, m, 0:n], ACT.Exp, bias=nmx[:, m:m + 1],
                                   accum_out=rsum[:, m:m + 1]).then_inc(ex_ready, 1)

            def weights_hi(at, b):
                n = (b + 1) * P
                act.wait_ge(aux_ready, at("aux", AUX["body"] + 1 + b + 1))
                act.activation(b_hi[:, 9 + b % 2, 0:n], aux[:, 0:n], ACT.Copy).then_inc(wt_hi, 1)

            with act.Fori(0, NH) as i:
                at = At(i, chunk=8, slot=32, tile=8, bank=2, aux=7, unit=4, one=1, two=2, eight=8)
                for n, dst in ((0, Q), (1, K), (2, VB)):
                    split_w(at, c0 + n + 4)
                    wait_tile(act, at, t0 + n)
                    read_out(act.activation(dst, banks[:, n, :], ACT.Copy), n)
                split_w(at, c0 + 7)
                wait_tile(act, at, t0 + 3)
                act.activation(tmp[:, 1, :], banks[:, 3, :], ACT.Tanh, scale=0.5).then_inc(za_t, 1)
                exps(at, 0)
                exps(at, 1)
                act.wait_ge(aux_ready, at("aux", AUX["body"] + 1))
                act.activation(b_hi[:, 8, :], aux, ACT.Copy).then_inc(v_hi, 1)
                split_w(at, c0 + 8)
                wait_tile(act, at, t0 + 4)
                read_out(act.activation(VB, banks[:, 0, :], ACT.Copy), t0 + 4)
                weights_hi(at, 0)
                exps(at, 2)
                split_w(at, c0 + 9)
                wait_tile(act, at, t0 + 5)
                read_out(act.activation(CG, banks[:, 1, :], ACT.Copy), t0 + 5)
                weights_hi(at, 1)
                exps(at, 3)
                split_w(at, c0 + 10)
                weights_hi(at, 2)
                weights_hi(at, 3)
                wait_tile(act, at, t0 + 7)
                act.activation(tmp[:, 1, :], banks[:, 3, :], ACT.Tanh, scale=0.5).then_inc(zc_t, 1)
                act.wait_ge(pv_ready, at("one", 1))
                act.activation(sq[:, 0, :], banks[:, 4, :], ACT.Copy).then_inc(o_copied, 1)
                act.activation(sqsum[:, :], banks[:, 4, :], ACT.Square).then_inc(o_sq, 1)
                act.wait_ge(cv_out, at("one", 1))
                act.activation(b_hi[:, bass.ds(i + 4, 1), :].rearrange("p a s -> p (a s)"), tmp[:, 0, :], ACT.Copy,
                               scale=0.5).then_inc(mix_hi, 1)
                split_w(at, c0 + 11)
                rsqrt(AUX["body"] + 6, P, eps5, o_r, at)
                act.wait_ge(o_out, at("one", 1))
                act.activation(b_hi[:, bass.ds(i, 1), :].rearrange("p a s -> p (a s)"), tmp[:, 0, :],
                               ACT.Copy).then_inc(mix_hi, 1)

            act.dma_start(PV, PT).then_inc(p_in, 16)
            act.wait_ge(p_in, 16)
            act.activation(b_hi[:, 8:10, :].rearrange("p k s -> p (k s)"), PV, ACT.Copy).then_inc(p_hi, 1)
            c0, t0 = CH["out"], TI["out"]
            for n in range(8):
                if n != 3:
                    split_w(flat, c0 + n + 4)
                if n >= 3:
                    for m in ((0, 1, 2, 3) if n == 3 else (n,)):
                        wait_tile(act, flat, t0 + m)
                        square(flat, 1, m, banks[:, m % 4, :])
                        if n == 3 and m == 0:
                            split_w(flat, c0 + n + 4)

            def e_tile(m):
                t = TI["ple"] + m
                wait_tile(act, flat, t)
                square(flat, 2, m, banks[:, t % 4, :])
                read_out(act.activation(E[:, m, :], banks[:, t % 4, :], ACT.Copy), t)

            for m in range(2):
                if m == 0:
                    rsqrt(AUX["post"], D, eps6, r_ready)
                e_tile(m)
            for m in range(2, KD):
                if m == 4:
                    split_w(flat, CH["ple"] + 4)
                if m == 7:
                    split_w(flat, CH["ple"] + 5)
                e_tile(m)
                if m >= 3:
                    act.wait_ge(x_new, m - 2)
                    act.activation(a_hi[:, m - 3, :], X[:, m - 3, :], ACT.Copy).then_inc(xg_hi, 1)
            for m in range(5, KD):
                act.wait_ge(x_new, m + 1)
                act.activation(a_hi[:, m, :], X[:, m, :], ACT.Copy).then_inc(xg_hi, 1)
            c0, t0 = CH["gate"], TI["gate"]

            def residual_squares(v, t0, ms):
                for m in ms:
                    wait_read(act, flat, t0 + m)
                    square(flat, v, m, X[:, m, :])

            def gate_tile(m):
                wait_tile(act, flat, t0 + m)
                if m >= 2:
                    act.wait_ge(x_new, KD + m - 1)
                read_out(act.activation(tmp[:, m % 2, :], banks[:, (t0 + m) % 4, :], ACT.Tanh, scale=0.5), t0 + m)

            def gate_square(m):
                act.wait_ge(x_new, KD + m + 1)
                square(flat, 3, m, X[:, m, :])

            for n in range(8):
                if n not in (3, 7):
                    split_w(flat, c0 + n + 4)
                if n == 1:
                    rsqrt(AUX["ple"], D, eps6, r_ready)
                if n >= 3:
                    for m in ((0, 1, 2, 3) if n == 3 else (n,)):
                        gate_tile(m)
                        if n == 3 and m == 0:
                            split_w(flat, c0 + n + 4)
                        if m:
                            gate_square(m - 1)
            gate_square(7)
            rsqrt(AUX["four"], D, eps6, r_ready)
            norm_hi(1, c0 + 11)

            c0, t0 = CH["dft1"], TI["dft1"]
            for z in range(16):
                wait_tile(act, flat, t0 + z)
                dst = b_hi[:, z, :] if z < 12 else a_hi[:, z - 12, :]
                act.activation(dst, banks[:, (t0 + z) % 4, :], ACT.Copy).then_inc(z_hi, 1)
            split_w(flat, c0 + 4)
            c0, t0 = CH["dft2"], TI["dft2"]
            for m in range(KD):
                if m == KD - 1:
                    for n in range(3):
                        split_w(flat, c0 + n + 4)
                wait_tile(act, flat, t0 + m)
                dst = a_hi[:, 4 + m, :] if m < 4 else b_hi[:, m - 4, :]
                act.activation(dst, banks[:, (t0 + m) % 4, :], ACT.Copy).then_inc(f_hi, 1)
            split_w(flat, c0 + 3 + 4)
            c0, t0 = CH["fout"], TI["fout"]
            for n in range(8):
                if n < 7:
                    split_w(flat, c0 + n + 4)
                if n >= 3:
                    residual_squares(4, t0, (0, 1, 2, 3) if n == 3 else (n,))

            def up_body(at, c, t, j):
                for n in range(2):
                    split_w(at, c + 2 * n + 4)
                    wait_tile(act, at, t + 2 * n)
                    act.activation(T2[:, n, :], banks[:, (t + 2 * n) % 4, :], ACT.Tanh, scale=0.5).then_inc(hid_t, 1)
                    split_w(at, c + 2 * n + 5)
                    act.wait_ge(hid_f, at("hid", j + n + 1))
                    if at.i is None:
                        dst = b_hi[:, j % FT % HALF[0] + n, :]
                    else:
                        dst = b_hi[:, bass.ds(at("hid", j % FT % HALF[0] + n), 1), :].rearrange("p a s -> p (a s)")
                    act.activation(dst, HD[:, n, :], ACT.Copy, scale=0.5).then_inc(hid_hi, 1)

            def swiglu(layer, v):
                rsqrt(AUX[f"ffn{layer}"], D, eps6, r_ready)
                norm_hi(2 + 2 * layer, CH[f"up{layer}a"] + 3)
                for part, n_hid in zip("ab", HALF):
                    c, t = CH[f"up{layer}{part}"], TI[f"up{layer}{part}"]
                    j = layer * FT + (0 if part == "a" else HALF[0])
                    first = 1 if part == "a" else 0
                    if first:
                        up_body(flat, c, t, j)
                    with act.Fori(0, n_hid // 2 - first) as i:
                        at = At(i, chunk=4, slot=16, tile=4, hid=2)
                        up_body(at, c + 4 * first, t + 4 * first, j + 2 * first)
                    c, t = CH[f"down{layer}{part}"], TI[f"down{layer}{part}"]
                    for n in range(n_hid):
                        if part == "a" or n < n_hid - 1:
                            split_w(flat, c + n + 4)
                        if part == "b":
                            done = [m for m in range(KD) if down_last(n_hid, m) == n]
                            residual_squares(v, t, done)

            def down_last(K, m):
                order = gemm_order(K, KD)
                return max(n for n, (k, mm) in enumerate(order) if mm == m) // 8

            swiglu(0, 5)

            act.dma_start(scr[:, 8 * S:10 * S], ROPE).then_inc(rope_in, 16)
            rsqrt(AUX["rnorm"], D, eps6, r_ready)
            norm_hi(3, CH["ret"] + 3)

            def rot_parts(at):
                for n in range(4):
                    act.wait_ge(rot, at("four", n + 1))
                    act.activation(b_hi[:, n, :], RT[:, 1 + 2 * (n % 2), :], ACT.Copy).then_inc(rot_hi, 1)

            def head(at, c, t, with_out):
                act.dma_start(DEC, DECAY[0] if with_out is None else
                              DECAY[bass.ds(with_out + 1, 1), :, :].rearrange("a p n -> (a p) n")).then_inc(dec_in, 16)
                for n in range(4):
                    split_w(at, c + n + 4)
                rot_parts(at)
                c, t = c + 4, t + 4
                if with_out is not None:
                    for n in range(4):
                        split_w(at, c + n + 4)
                    c, t = c + 4, t + 8
                for n in range(3):
                    split_w(at, c + n + 4)
                for n in range(4):
                    wait_tile(act, at, t + n)
                    act.activation(b_hi[:, 4 + n, :], banks[:, (t + n) % 4, :], ACT.Copy).then_inc(vv_hi, 1)
                split_w(at, c + 3 + 4)
                c, t = c + 4, t + 4
                for n in range(3):
                    if n < 2:
                        split_w(at, c + n + 4)
                    wait_tile(act, at, t + n)
                    act.activation(RT[:, n, :], banks[:, (t + n) % 4, :], ACT.Tanh, scale=0.5).then_inc(gg_t, 1)
                for n in range(4):
                    act.wait_ge(pd, at("four", n + 1))
                    act.activation(b_hi[:, 8 + n, :], tmp[:, n % 2, :], ACT.Copy).then_inc(pd_hi, 1)
                split_w(at, c + 2 + 4)
                t += 7
                wait_tile(act, at, t)
                act.activation(RT[:, 3, :], banks[:, t % 4, :], ACT.Tanh, scale=0.5).then_inc(gg_t, 1)
                t += 1
                for n in range(4):
                    act.wait_ge(y_cen, at("four", n + 1))
                    if n >= 3:
                        act.wait_ge(y_qs, at("three", n - 2))
                    act.activation(sqsum[:, :] if n == 0 else sq[:, n % 2, :], Y[:, n, :],
                                   ACT.Square).then_inc(y_sq, 1)
                rsqrt(AUX["ret"] + 1, 4 * P, eps6, y_r, at)
                for n in range(4):
                    act.wait_ge(y_f, at("four", n + 1))
                    act.activation(b_hi[:, 8 + n, :], Y[:, n, :], ACT.Copy, scale=0.5).then_inc(y_hi, 1)
                split_w(at, c + 3 + 4)

            head(At(), CH["ret"], TI["ret"], None)
            RB = dict(chunk=16, slot=64, tile=28, bank=7, aux=2, four=4, three=3, one=1)

            with act.Fori(0, NH - 1) as i:
                head(Head(i, **RB), CH["retbody"], TI["retbody"], i)
            c0, t0 = CH["retout"], TI["retout"]
            order = gemm_order(4, KD)
            for n in range(4):
                if n < 3:
                    split_w(flat, c0 + n + 4)
                residual_squares(6, t0, [m for m in range(KD)
                                         if max(q for q, (k, mm) in enumerate(order) if mm == m) // 8 == n])
            swiglu(1, 7)
            rsqrt(AUX["final"], D, eps6, r_ready)

        @block.vector
        def _(dve):
            linked = [0]

            def link(ins, at=flat):
                linked[0] += 1
                ins.then_inc(link_s, 1)
                dve.wait_ge(link_s, at("link", linked[0]))

            steps = [0]

            def ada(at=flat, k=1):
                for _ in range(k):
                    a = steps[0]
                    steps[0] += 1
                    f = a % KD
                    dve.wait_ge(ada_in[a % ADA_RING], at("adaslot", 16 * (a // ADA_RING + 1)))
                    src = ada_raw[:, a % ADA_RING, :]
                    if f == 0:
                        ins = dve.tensor_scalar(ada_acc[:, :], src, cact[:, 0:1], None, ALU.mult)
                    else:
                        dve.wait_ge(ada_sum, at("ada", a))
                        ins = dve.scalar_tensor_tensor(out=ada_acc[:, :], in0=src, scalar=cact[:, f:f + 1],
                                                       in1=ada_acc[:, :], op0=ALU.mult, op1=ALU.add)
                    ins.then_inc(ada_sum, 1)

            def ada_out(u, g, at=flat):
                dve.wait_ge(aux_ready, at("aux", u + 1))
                if at.i is None:
                    dst, b = mod[:, KD * g:KD * g + KD], col("b_ada", KD * g, KD)
                else:
                    dst = mod[:, bass.ds(at("eight", KD * g), KD)]
                    b = cols[:, bass.ds(at("eight", COL["b_ada"] + KD * g), KD)]
                dve.tensor_tensor(dst, aux[:, 0:KD], b, ALU.add).then_inc(aux_free, 1)

            def add_square(v, m):
                if m == 0:
                    return
                dve.wait_ge(sq_ready, 8 * v + m + 1)
                if m >= 2:
                    dve.wait_ge(sq_added, 7 * v + m - 1)
                dve.tensor_tensor(sqsum[:, :], sqsum[:, :], sq[:, m % 2, :], ALU.add).then_inc(sq_added, 1)

            def norm_apply(v, a, g, sh):
                dve.wait_ge(r_ready, v + 1)

                def lo(m):
                    dve.wait_ge(h_hi, 8 * a + m + 1)
                    dve.tensor_tensor(a_lo[:, m, :], tmp[:, m % 2, :], a_hi[:, m, :].bitcast(fp32),
                                      ALU.subtract).then_inc(a_ready, 1)

                for m in range(KD):
                    if m >= 2:
                        dve.wait_ge(a_ready, 8 * a + m - 1)
                    link(dve.tensor_tensor(tmp[:, m % 2, :], X[:, m, :], rinv[:, :], ALU.mult))
                    dve.tensor_scalar(tmp[:, m % 2, :], tmp[:, m % 2, :], g(m), sh(m), ALU.mult,
                                      ALU.add).then_inc(h_ready, 1)
                    if m:
                        lo(m - 1)
                lo(KD - 1)

            def scale_columns(n, gain, g):
                link(dve.scalar_tensor_tensor(out=gs[:, KD * n:KD * n + KD], in0=mod[:, KD * g:KD * g + KD],
                                              scalar=1.0, in1=gain, op0=ALU.add, op1=ALU.mult))

            def residual(at, t, m, g):
                wait_tile(dve, at, t)
                read_out(dve.scalar_tensor_tensor(out=X[:, m, :], in0=banks[:, t % 4, :],
                                                  scalar=mod[:, KD * g + m:KD * g + m + 1], in1=X[:, m, :],
                                                  op0=ALU.mult, op1=ALU.add), t)

            dve.memset(zero, 0.0)
            dve.memset(eps6, 1e-6)
            dve.memset(eps5, 1e-5)
            dve.memset(G[:, 0:2], 0.0)
            dve.memset(ones[:, :], 1.0).then_inc(const, 1)
            dve.wait_ge(cols_in, 16)
            lt = lamt.rearrange("p (a n) -> p a n", a=4)
            lc = col("lam", 0, 256).rearrange("p (a n) -> p a n", a=4)
            link(dve.tensor_tensor(lt[:, 0:2, :], lc[:, 0:2, :], lc[:, 2:4, :], ALU.mult))
            dve.tensor_reduce(lamp, lt[:, 0:2, :], AX.X, ALU.add).then_inc(lam_in, 1)
            dve.wait_ge(lam_e, 1)
            link(dve.tensor_scalar(ctanh, ctanh, 1.0, 0.5, ALU.add, ALU.mult))
            link(dve.tensor_tensor(cact, ctanh, col("c", 0, KD), ALU.mult))
            dve.wait_ge(lam_e, 2)
            link(dve.tensor_tensor(neglam, lamv[:, 1:2], lamv[:, 0:1], ALU.subtract))
            link(dve.tensor_scalar(neglam, neglam, -LAM_INIT, None, ALU.add))
            link(dve.tensor_scalar(gsub, col("subln"), 0.5 * (1.0 - LAM_INIT), None, ALU.mult))
            link(dve.tensor_scalar(gple, col("ple", 0, KD), 0.5, None, ALU.mult))
            for m in range(1, KD):
                add_square(0, m)
            norm_apply(0, 0, lambda m: col("pre", m), lambda m: zero)

            dve.wait_ge(dist_in, 16)
            t0 = TI["body"]
            A0 = AUX["body"]

            def softmax_a(at, b):
                n = (b + 1) * P
                dve.wait_ge(sc_ready, at("unit", b + 1))
                for m in range(2):
                    dve.scalar_tensor_tensor(out=SC[:, b % 2, m, 0:n], in0=banks[:, 5 + m, 0:n], scalar=0.125,
                                             in1=bias[:, 3 * P - P * b:S], op0=ALU.mult,
                                             op1=ALU.add).then_inc(sc_read, 1)
                dve.wait_ge(sc_read, at("eight", 2 * b + 2))
                link(dve.tensor_reduce(mx, SC[:, b % 2, :, 0:n], AX.X, ALU.max), at)
                dve.tensor_scalar(nmx, mx, -1.0, None, ALU.mult).then_inc(nm_ready, 1)

            def softmax_b(at, b):
                n = (b + 1) * P
                dve.wait_ge(ex_ready, at("eight", 2 * b + 2))
                link(dve.reciprocal(rrec, rsum), at)
                link(dve.tensor_scalar(c1[:, 0:1], rrec[:, 1:2], neglam, None, ALU.mult), at)
                if b >= 2:
                    dve.wait_ge(aux_ready, at("aux", A0 + 1 + b - 2 + 1))
                link(dve.tensor_scalar(WT[:, b % 2, 0:n], SC[:, b % 2, 0, 0:n], rrec[:, 0:1], None, ALU.mult), at)
                dve.scalar_tensor_tensor(out=WT[:, b % 2, 0:n], in0=SC[:, b % 2, 1, 0:n], scalar=c1[:, 0:1],
                                         in1=WT[:, b % 2, 0:n], op0=ALU.mult, op1=ALU.add).then_inc(w_ready, 1)

            def weights_lo(at, b):
                n = (b + 1) * P
                dve.wait_ge(wt_hi, at("unit", b + 1))
                dve.tensor_tensor(b_lo[:, 9 + b % 2, 0:n], aux[:, 0:n], b_hi[:, 9 + b % 2, 0:n].bitcast(fp32),
                                  ALU.subtract).then_inc(aux_free, 1)

            base = linked[0]
            per_link = 1 + 4 * 4 + 4 + 1
            with dve.Fori(0, NH) as i:
                at = At(i, chunk=8, tile=8, bank=2, aux=7, unit=4, one=1, two=2, eight=8, link=per_link,
                        ada=8, adaslot=64)
                link(dve.tensor_scalar(bias, dist, cols[:, bass.ds(i + COL["slope"], 1)], None, ALU.mult), at)
                ada(at, 3)
                softmax_a(at, 0)
                wait_tile(dve, at, t0 + 3)
                dve.wait_ge(za_t, at("one", 1))
                read_out(dve.scalar_tensor_tensor(out=ZA, in0=tmp[:, 1, :], scalar=1.0, in1=banks[:, 3, :],
                                                  op0=ALU.add, op1=ALU.mult), 3)
                softmax_b(at, 0)
                softmax_a(at, 1)
                dve.wait_ge(v_hi, at("one", 1))
                dve.tensor_tensor(b_lo[:, 8, :], aux, b_hi[:, 8, :].bitcast(fp32), ALU.subtract).then_inc(aux_free, 1)
                softmax_b(at, 1)
                ada(at, 1)
                softmax_a(at, 2)
                weights_lo(at, 0)
                softmax_b(at, 2)
                ada(at, 1)
                softmax_a(at, 3)
                weights_lo(at, 1)
                softmax_b(at, 3)
                wait_tile(dve, at, t0 + 6)
                wait_read(dve, at, t0 + 5)
                read_out(dve.tensor_tensor(G[:, 2:2 + S], banks[:, 2, :], CG, ALU.mult), t0 + 6)
                wait_read(dve, at, t0 + 6)
                tap = [cols[:, bass.ds(i * 3 + (COL["conv"] + j), 1)] for j in range(3)]
                link(dve.tensor_scalar(tmp[:, 0, :], G[:, 0:S], tap[0], None, ALU.mult), at)
                for j in (1, 2):
                    link(dve.scalar_tensor_tensor(out=tmp[:, 0, :], in0=G[:, j:j + S], scalar=tap[j],
                                                  in1=tmp[:, 0, :], op0=ALU.mult, op1=ALU.add), at)
                wait_read(dve, at, t0 + 4)
                link(dve.tensor_tensor(tmp[:, 0, :], tmp[:, 0, :], VB, ALU.mult), at)
                weights_lo(at, 2)
                ada(at, 2)
                weights_lo(at, 3)
                dve.wait_ge(zc_t, at("one", 1))
                read_out(dve.scalar_tensor_tensor(out=sq[:, 1, :], in0=tmp[:, 1, :], scalar=1.0, in1=banks[:, 3, :],
                                                  op0=ALU.add, op1=ALU.mult), t0 + 7)
                wait_read(dve, at, t0 + 7)
                dve.tensor_tensor(tmp[:, 0, :], tmp[:, 0, :], sq[:, 1, :], ALU.mult).then_inc(cv_out, 1)
                ada(at, 1)
                dve.wait_ge(mix_hi, at("two", 1))
                dve.wait_ge(cv_out, at("one", 1))
                dve.scalar_tensor_tensor(out=b_lo[:, bass.ds(i + 4, 1), :].rearrange("p a s -> p (a s)"),
                                         in0=tmp[:, 0, :], scalar=0.5,
                                         in1=b_hi[:, bass.ds(i + 4, 1), :].rearrange("p a s -> p (a s)").bitcast(fp32),
                                         op0=ALU.mult, op1=ALU.subtract).then_inc(mix_ready, 1)
                ada_out(A0 + 5, 0, at)
                dve.wait_ge(o_r, at("one", 1))
                dve.wait_ge(o_copied, at("one", 1))
                dve.wait_ge(mix_ready, at("two", 1))
                link(dve.tensor_tensor(tmp[:, 0, :], sq[:, 0, :], rinv[:, :], ALU.mult), at)
                dve.scalar_tensor_tensor(out=tmp[:, 0, :], in0=tmp[:, 0, :], scalar=gsub, in1=ZA,
                                         op0=ALU.mult, op1=ALU.mult).then_inc(o_out, 1)
                dve.wait_ge(mix_hi, at("two", 2))
                dve.wait_ge(o_out, at("one", 1))
                dve.tensor_tensor(b_lo[:, bass.ds(i, 1), :].rearrange("p a s -> p (a s)"), tmp[:, 0, :],
                                  b_hi[:, bass.ds(i, 1), :].rearrange("p a s -> p (a s)").bitcast(fp32),
                                  ALU.subtract).then_inc(mix_ready, 1)
            got = linked[0] - base
            assert got == per_link, got
            linked[0] = base + per_link * NH
            steps[0] = 8 * NH

            dve.wait_ge(p_hi, 1)
            dve.tensor_tensor(b_lo[:, 8:10, :].rearrange("p k s -> p (k s)"), PV,
                              b_hi[:, 8:10, :].rearrange("p k s -> p (k s)").bitcast(fp32),
                              ALU.subtract).then_inc(p_ready, 1)
            t0 = TI["out"]
            for n in range(8):
                ada()
                if n >= 3:
                    for m in ((0, 1, 2, 3) if n == 3 else (n,)):
                        dve.wait_ge(sq_ready, 8 + m + 1)
                        read_out(dve.tensor_copy(MIX[:, m, :], banks[:, m % 4, :]), t0 + m)
                        add_square(1, m)
            t1 = TI["ple"]

            def xg_lo(m):
                dve.wait_ge(xg_hi, m + 1)
                dve.tensor_tensor(a_lo[:, m, :], X[:, m, :], a_hi[:, m, :].bitcast(fp32),
                                  ALU.subtract).then_inc(xg_ready, 1)

            dve.wait_ge(r_ready, 2)
            for m in range(KD):
                if m == 0:
                    for b in range(4):
                        wait_read(dve, flat, t0 + 4 + b)
                link(dve.tensor_tensor(tmp[:, m % 2, :], MIX[:, m, :], rinv[:, :], ALU.mult))
                dve.scalar_tensor_tensor(out=X[:, m, :], in0=tmp[:, m % 2, :], scalar=col("post", m), in1=X[:, m, :],
                                         op0=ALU.mult, op1=ALU.add).then_inc(x_new, 1)
                dve.wait_ge(sq_ready, 16 + m + 1)
                add_square(2, m)
                dve.wait_ge(x_new, m + 1)
                if m >= 3:
                    xg_lo(m - 3)
                if m == 2:
                    ada_out(AUX["ada4"], 4)
            for m in range(KD - 3, KD):
                xg_lo(m)
            t0 = TI["gate"]
            dve.wait_ge(r_ready, 3)
            for m in range(4, KD):
                wait_read(dve, flat, t1 + m)
            for m in range(KD):
                dve.scalar_tensor_tensor(out=E[:, m, :], in0=E[:, m, :], scalar=gple[:, m:m + 1], in1=rinv[:, :],
                                         op0=ALU.mult, op1=ALU.mult).then_inc(e_ready, 1)
            for n in range(8):
                ada()
                if n >= 3:
                    for m in ((0, 1, 2, 3) if n == 3 else (n,)):
                        wait_read(dve, flat, t0 + m)
                        dve.wait_ge(e_ready, m + 1)
                        link(dve.scalar_tensor_tensor(out=E[:, m, :], in0=tmp[:, m % 2, :], scalar=1.0,
                                                      in1=E[:, m, :], op0=ALU.add, op1=ALU.mult))
                        dve.tensor_tensor(X[:, m, :], X[:, m, :], E[:, m, :], ALU.add).then_inc(x_new, 1)
                        if m:
                            add_square(3, m - 1)
            add_square(3, 7)
            dve.wait_ge(aux_free, AUX["body"] + 7 * NH)
            scale_columns(0, col("mix", 0, KD), 1)
            norm_apply(3, 1, lambda m: gs[:, m:m + 1], lambda m: mod[:, m:m + 1])
            ada_out(AUX["ada5"], 5)

            t0 = TI["dft1"]
            for z in range(16):
                dve.wait_ge(z_hi, z + 1)
                hi, lo = (b_hi[:, z, :], b_lo[:, z, :]) if z < 12 else (a_hi[:, z - 12, :], a_lo[:, z - 12, :])
                read_out(dve.tensor_tensor(lo, banks[:, (t0 + z) % 4, :], hi.bitcast(fp32), ALU.subtract), t0 + z)
            t0 = TI["dft2"]
            for m in range(KD):
                ada()
                dve.wait_ge(f_hi, m + 1)
                hi, lo = (a_hi[:, 4 + m, :], a_lo[:, 4 + m, :]) if m < 4 else (b_hi[:, m - 4, :], b_lo[:, m - 4, :])
                read_out(dve.tensor_tensor(lo, banks[:, (t0 + m) % 4, :], hi.bitcast(fp32), ALU.subtract), t0 + m)
            ada_out(AUX["ada6"], 6)
            t0 = TI["fout"]
            for n in range(8):
                ada()
                if n >= 3:
                    for m in ((0, 1, 2, 3) if n == 3 else (n,)):
                        residual(flat, t0 + m, m, 2)
                        if m:
                            add_square(4, m - 1)
            add_square(4, 7)

            def up_body(at, t, j):
                for n in range(2):
                    dve.wait_ge(hid_t, at("hid", j + n + 1))
                    g, u = (t + 2 * n) % 4, (t + 2 * n + 1) % 4
                    read_out(dve.scalar_tensor_tensor(out=SG[:, n, :], in0=T2[:, n, :], scalar=1.0,
                                                      in1=banks[:, g, :], op0=ALU.add, op1=ALU.mult), g)
                    wait_tile(dve, at, t + 2 * n + 1)
                    wait_read(dve, at, t + 2 * n)
                    dve.tensor_tensor(HD[:, n, :], SG[:, n, :], banks[:, u, :], ALU.mult).then_inc(hid_f, 1)
                    dve.wait_ge(hid_hi, at("hid", j + n + 1))
                    k = j % FT % HALF[0] + n
                    if at.i is None:
                        hi, lo = b_hi[:, k, :], b_lo[:, k, :]
                    else:
                        hi, lo = (b[:, bass.ds(at("hid", k), 1), :].rearrange("p a s -> p (a s)") for b in (b_hi, b_lo))
                    read_out(dve.scalar_tensor_tensor(out=lo, in0=HD[:, n, :], scalar=0.5, in1=hi.bitcast(fp32),
                                                      op0=ALU.mult, op1=ALU.subtract), u)

            def swiglu(layer, v, a_in, with_ada, u):
                g0 = 6 * layer
                dve.wait_ge(aux_free, u + 1)
                scale_columns(a_in, col("ffn", KD * layer, KD), g0 + 4)
                norm_apply(v - 1, a_in, lambda m: gs[:, KD * a_in + m:KD * a_in + m + 1],
                           lambda m: mod[:, KD * (g0 + 3) + m:KD * (g0 + 3) + m + 1])
                for part, n_hid in zip("ab", HALF):
                    t = TI[f"up{layer}{part}"]
                    j = layer * FT + (0 if part == "a" else HALF[0])
                    first = 1 if part == "a" else 0
                    if first:
                        if with_ada:
                            ada_out(AUX["ada7"], 7)
                        up_body(flat, t, j)
                        if with_ada:
                            ada(flat, 8)
                    with dve.Fori(0, n_hid // 2 - first) as i:
                        at = At(i, tile=4, bank=1, hid=2, ada=8, adaslot=64, aux=1, eight=8)
                        up_body(at, t + 4 * first, j + 2 * first)
                        if first and with_ada:
                            ada_out(AUX["ada"], 8, at)
                            ada(at, 8)
                    if first and with_ada:
                        ada_out(AUX["ada"] + 5, 13)
                    t = TI[f"down{layer}{part}"]
                    for m in range(KD):
                        residual(flat, t + m, m, g0 + 5)
                        if part == "b" and m:
                            add_square(v, m - 1)
                add_square(v, 7)

            swiglu(0, 5, 2, True, AUX["ada5"])

            dve.wait_ge(aux_free, AUX["ada"] + 6)
            scale_columns(3, col("mix", KD, KD), 7)
            norm_apply(5, 3, lambda m: gs[:, 3 * KD + m:3 * KD + m + 1], lambda m: mod[:, 6 * KD + m:6 * KD + m + 1])
            dve.wait_ge(rope_in, 16)

            def head(at, t, with_out):
                def rot_lo(n):
                    dve.wait_ge(rot_hi, at("four", n + 1))
                    dve.tensor_tensor(b_lo[:, n, :], RT[:, 1 + 2 * (n % 2), :], b_hi[:, n, :].bitcast(fp32),
                                      ALU.subtract).then_inc(rot_ready, 1)

                for n in range(2):
                    x1, x2 = banks[:, (t + 2 * n) % 4, :], banks[:, (t + 2 * n + 1) % 4, :]
                    wait_tile(dve, at, t + 2 * n + 1)
                    if n:
                        rot_lo(0)
                    dve.tensor_tensor(RT[:, 0, :], x1, COS, ALU.mult)
                    if n:
                        dve.wait_ge(rot_ready, at("four", 1))
                    link(dve.tensor_tensor(RT[:, 1, :], x2, SIN, ALU.mult), at)
                    dve.tensor_tensor(RT[:, 1, :], RT[:, 0, :], RT[:, 1, :], ALU.subtract).then_inc(rot, 1)
                    if n:
                        rot_lo(1)
                    read_out(dve.tensor_tensor(RT[:, 2, :], x1, SIN, ALU.mult), t + 2 * n)
                    if n:
                        dve.wait_ge(rot_ready, at("four", 2))
                    read_out(dve.tensor_tensor(RT[:, 3, :], x2, COS, ALU.mult), t + 2 * n + 1)
                    wait_read(dve, at, t + 2 * n)
                    wait_read(dve, at, t + 2 * n + 1)
                    dve.tensor_tensor(RT[:, 3, :], RT[:, 2, :], RT[:, 3, :], ALU.add).then_inc(rot, 1)
                rot_lo(2)
                rot_lo(3)
                t += 4
                if with_out:
                    for m in range(KD):
                        residual(at, t + m, m, 8)
                    t += 8
                for n in range(4):
                    dve.wait_ge(vv_hi, at("four", n + 1))
                    read_out(dve.tensor_tensor(b_lo[:, 4 + n, :], banks[:, (t + n) % 4, :],
                                               b_hi[:, 4 + n, :].bitcast(fp32), ALU.subtract), t + n)
                t += 4

                def gate(n, tt):
                    dve.wait_ge(gg_t, at("four", n + 1))
                    read_out(dve.scalar_tensor_tensor(out=GG[:, n, :], in0=RT[:, n, :], scalar=1.0,
                                                      in1=banks[:, tt % 4, :], op0=ALU.add, op1=ALU.mult), tt)

                for n in range(3):
                    gate(n, t + n)
                t += 3
                dve.wait_ge(dec_in, at("sixteen", 16))

                def score_lo(n):
                    dve.wait_ge(pd_hi, at("four", n + 1))
                    read_out(dve.tensor_tensor(b_lo[:, 8 + n, :], tmp[:, n % 2, :], b_hi[:, 8 + n, :].bitcast(fp32),
                                               ALU.subtract), t + n)

                for n in range(4):
                    wait_tile(dve, at, t + n)
                    if n >= 2:
                        wait_read(dve, at, t + n - 2)
                    dve.tensor_tensor(tmp[:, n % 2, :], banks[:, (t + n) % 4, :], DEC[:, 3 * P - P * n:3 * P - P * n + S],
                                      ALU.mult).then_inc(pd, 1)
                    dve.wait_ge(pd, at("four", n + 1))
                    if n:
                        score_lo(n - 1)
                score_lo(3)
                t += 4
                gate(3, t)
                t += 1
                for n in range(4):
                    wait_tile(dve, at, t + n)
                    read_out(dve.tensor_copy(Y[:, n, :], banks[:, (t + n) % 4, :]), t + n)
                    wait_read(dve, at, t + n)
                    if n == 1:
                        link(dve.tensor_tensor(sqsum[:, :], Y[:, 0, :], Y[:, 1, :], ALU.add), at)
                    elif n == 2:
                        link(dve.tensor_tensor(sqsum[:, :], sqsum[:, :], Y[:, 2, :], ALU.add), at)
                    elif n == 3:
                        dve.tensor_tensor(sqsum[:, :], sqsum[:, :], Y[:, 3, :], ALU.add).then_inc(y_sum, 1)
                dve.wait_ge(aux_ready, at("aux", AUX["ret"] + 1))
                dve.tensor_scalar(rinv[:, :], aux, 1.0 / (4 * P), None, ALU.mult).then_inc(aux_free, 1)
                dve.wait_ge(aux_free, at("aux", AUX["ret"] + 1))
                for n in range(4):
                    dve.tensor_tensor(Y[:, n, :], Y[:, n, :], rinv[:, :], ALU.subtract).then_inc(y_cen, 1)
                for n in range(1, 4):
                    dve.wait_ge(y_sq, at("four", n + 1))
                    if n >= 2:
                        dve.wait_ge(y_qs, at("three", n - 1))
                    dve.tensor_tensor(sqsum[:, :], sqsum[:, :], sq[:, n % 2, :], ALU.add).then_inc(y_qs, 1)
                dve.wait_ge(y_r, at("one", 1))
                for n in range(4):
                    dve.wait_ge(y_cen, at("four", n + 1))
                    link(dve.tensor_tensor(Y[:, n, :], Y[:, n, :], rinv[:, :], ALU.mult), at)
                    if n == 0:
                        for q in range(4):
                            wait_read(dve, at, t - 8 + q if q < 3 else t - 1)
                    dve.tensor_tensor(Y[:, n, :], Y[:, n, :], GG[:, n, :], ALU.mult).then_inc(y_f, 1)
                for n in range(4):
                    dve.wait_ge(y_hi, at("four", n + 1))
                    dve.wait_ge(y_f, at("four", n + 1))
                    dve.scalar_tensor_tensor(out=b_lo[:, 8 + n, :], in0=Y[:, n, :], scalar=0.5,
                                             in1=b_hi[:, 8 + n, :].bitcast(fp32), op0=ALU.mult,
                                             op1=ALU.subtract).then_inc(y_ready, 1)

            per_link = 2 + 2 + 4
            base = linked[0]
            head(flat, TI["ret"], False)
            assert linked[0] - base == per_link, linked[0] - base
            base = linked[0]
            with dve.Fori(0, NH - 1) as i:
                head(Head(i, tile=28, bank=7, aux=2, four=4, three=3, one=1, sixteen=16, link=per_link),
                     TI["retbody"], True)
            assert linked[0] - base == per_link
            linked[0] = base + per_link * (NH - 1)
            t0 = TI["retout"]
            for m in range(KD):
                residual(flat, t0 + m, m, 8)
                if m:
                    add_square(6, m - 1)
            add_square(6, 7)
            swiglu(1, 7, 4, False, AUX["ada"] + 5)
            link(dve.scalar_tensor_tensor(out=gs[:, 0:KD], in0=mod[:, 13 * KD:14 * KD], scalar=1.0,
                                          in1=col("final", 0, KD), op0=ALU.add, op1=ALU.mult))
            dve.wait_ge(r_ready, 8)
            for m in range(KD):
                link(dve.tensor_tensor(tmp[:, m % 2, :], X[:, m, :], rinv[:, :], ALU.mult))
                dve.tensor_scalar(X[:, m, :], tmp[:, m % 2, :], gs[:, m:m + 1], mod[:, 12 * KD + m:12 * KD + m + 1],
                                  ALU.mult, ALU.add).then_inc(x_done, 1)

        @block.tensor
        def _(pe):
            pos = [0, 0]

            def chunk_begins(at, width):
                c, q = pos
                slot = c % RING
                begins = q == 0
                if begins:
                    pe.wait_ge(wlo, at("chunk", c + 1))
                ap = slice(q * P, q * P + width)
                pos[1] += width // P
                if pos[1] == 8:
                    pos[0], pos[1] = c + 1, 0
                return begins and c > 0, w_hi[:, slot, ap], w_lo[:, slot, ap]

            def mul(at, bank, x_hi, x_lo, first, last, done=False):
                begins, hi, lo = chunk_begins(at, P)
                out = banks[:, bank, :]
                mm = pe.matmul(out, lo, x_hi, start=first, stop=False)
                if begins:
                    mm.then_inc(w_used, 1)
                pe.matmul(out, hi, x_lo, start=False, stop=False)
                mm = pe.matmul(out, hi, x_hi, start=False, stop=last)
                if done:
                    mm.then_inc(tile_ready, 1)

            def wait_bank(at, t):
                if t >= 4:
                    pe.wait_ge(bank_read[t % 4], at("bank", t // 4))

            def gemm(at, t0, M, ks, rhs, ready=None, first_outer=True, hook=None):
                seen, opened = set(), set()
                order = gemm_order(len(ks), M, ks, first_outer)
                n_of = {}
                for n, (k, m) in enumerate(order):
                    if ready and k not in seen:
                        seen.add(k)
                        ready(k)
                    if m not in opened:
                        opened.add(m)
                        wait_bank(at, t0 + m)
                        n_of[m] = 0
                    hi, lo = rhs(k)
                    n_of[m] += 1
                    mul(at, (t0 + m) % 4, hi, lo, n_of[m] == 1, n_of[m] == len(ks), n_of[m] == len(ks))
                    if hook:
                        hook(n)

            def rhs_a(k):
                return a_hi[:, k, :], a_lo[:, k, :]

            def rhs_b(k):
                return b_hi[:, k, :], b_lo[:, k, :]

            def stats(at, u):
                if u > 0:
                    pe.wait_ge(aux_free, at("aux", u))
                pe.matmul(aux, ones[:, :], sqsum[:, :], start=True, stop=True).then_inc(aux_ready, 1)

            def norm_stats(v, name):
                pe.wait_ge(sq_added, 7 * v + 7)
                stats(flat, AUX[name])

            def ada_reduce(at, u, g):
                pe.wait_ge(ada_sum, at("ada", KD * (g + 1)))
                pe.wait_ge(aux_free, at("aux", u))
                for f in range(KD):
                    mm = pe.matmul(aux[:, f:f + 1], ada_acc[:, f * P:(f + 1) * P], ones[:, 0:1], start=True, stop=True)
                mm.then_inc(aux_ready, 1)

            pe.wait_ge(const, 1)
            norm_stats(0, "pre")
            A0, t0 = AUX["body"], TI["body"]

            def scores(at, b):
                n = (b + 1) * P
                if b == 0:
                    wait_read(pe, at, t0)
                    wait_read(pe, at, t0 + 1)
                else:
                    pe.wait_ge(sc_read, at("eight", 2 * b))
                for m in range(2):
                    p = slice(64 * m, 64 * m + 64)
                    mm = pe.matmul(banks[:, 5 + m, 0:n], Q[p, b * P:(b + 1) * P], K[p, 0:n], start=True, stop=True)
                mm.then_inc(sc_ready, 1)

            def transpose_v(at):
                wait_read(pe, at, t0 + 2)
                pe.wait_ge(aux_free, at("aux", A0))
                for s in range(TB):
                    mm = pe.transpose(aux[:, s * P:(s + 1) * P], VB[:, s * P:(s + 1) * P], ident)
                mm.then_inc(aux_ready, 1)

            def transpose_w(at, b):
                pe.wait_ge(w_ready, at("unit", b + 1))
                pe.wait_ge(aux_free, at("aux", A0 + 1 + b))
                for s in range(b + 1):
                    mm = pe.transpose(aux[:, s * P:(s + 1) * P], WT[:, b % 2, s * P:(s + 1) * P], ident)
                mm.then_inc(aux_ready, 1)

            def values(at, b):
                pe.wait_ge(aux_free, at("aux", A0 + 2 + b))
                out = banks[:, 4, b * P:(b + 1) * P]
                for s in range(b + 1):
                    c = slice(s * P, (s + 1) * P)
                    v1, v2 = b_hi[:, 8, c], b_lo[:, 8, c]
                    w1, w2 = b_hi[:, 9 + b % 2, c], b_lo[:, 9 + b % 2, c]
                    pe.matmul(out, v2, w1, start=(s == 0), stop=False)
                    pe.matmul(out, v1, w2, start=False, stop=False)
                    mm = pe.matmul(out, v1, w1, start=False, stop=(s == b))
                if b == TB - 1:
                    mm.then_inc(pv_ready, 1)

            pe.wait_ge(a_ready, KD)
            pe.wait_ge(cols_in, 16)

            def body_head(at, n):
                gemm(at, t0 + n, 1, range(KD), rhs_a, None, False)

            def body_rest(at):
                scores(at, 1)
                transpose_v(at)
                gemm(at, t0 + 4, 1, range(KD), rhs_a, None, False)
                scores(at, 2)
                transpose_w(at, 0)
                gemm(at, t0 + 5, 1, range(KD), rhs_a, None, False)
                scores(at, 3)
                transpose_w(at, 1)
                values(at, 0)
                gemm(at, t0 + 6, 1, range(KD), rhs_a, None, False)
                transpose_w(at, 2)
                values(at, 1)

                def middle(n):
                    if n == 3:
                        transpose_w(at, 3)
                        values(at, 2)
                gemm(at, t0 + 7, 1, range(KD), rhs_a, None, False, middle)
                values(at, 3)
                ada_reduce(at, A0 + 5, 0)
                pe.wait_ge(o_sq, at("one", 1))
                stats(at, A0 + 6)

            per = dict(chunk=8, tile=8, bank=2, aux=7, unit=4, one=1, two=2, eight=8, ada=8)
            for n in range(3):
                body_head(flat, n)
            scores(flat, 0)
            body_head(flat, 3)
            with pe.Fori(0, NH - 1) as i:
                at = At(i, **per)
                body_rest(at)
                for n in range(8, 12):
                    body_head(at, n)
                    if n == 10:
                        nxt = At(i, **per)
                        for q in (8, 9):
                            wait_read(pe, nxt, t0 + q)
                        for m in range(2):
                            p = slice(64 * m, 64 * m + 64)
                            mm = pe.matmul(banks[:, 5 + m, 0:P], Q[p, 0:P], K[p, 0:P], start=True, stop=True)
                        mm.then_inc(sc_ready, 1)
            last = At(NH - 1, **per)
            pos[0] = CH["body"] + 4
            body_rest(last)
            pos[0] = CH["out"]

            def mix_wait(k):
                pe.wait_ge(mix_ready, 8 if k == 3 else 7)
            gemm(flat, TI["out"], KD, ATT_KS, rhs_b, mix_wait)
            pe.wait_ge(p_ready, 1)

            def gemm_e(t0):
                for m in range(KD):
                    wait_bank(flat, t0 + m)
                    for k in range(2):
                        mul(flat, (t0 + m) % 4, b_hi[:, 8 + k, :], b_lo[:, 8 + k, :], k == 0, k == 1, k == 1)
                    if m == 1:
                        norm_stats(1, "post")
                    if m == 3:
                        ada_reduce(flat, AUX["ada4"], 4)
            gemm_e(TI["ple"])
            def gate_wait(k):
                pe.wait_ge(xg_ready, k + 1)

            def gate_hook(n):
                if n == 15:
                    norm_stats(2, "ple")
            gemm(flat, TI["gate"], KD, range(KD), rhs_a, gate_wait, True, gate_hook)
            norm_stats(3, "four")
            ada_reduce(flat, AUX["ada5"], 5)
            t0 = TI["dft1"]
            slot = CH["dft1"] % RING
            for g in range(NH):
                pe.wait_ge(a_ready, KD + 2 * g + 2)
                for tt in range(TB):
                    t = t0 + g * 4 + tt
                    wait_bank(flat, t)
                    for k in range(2):
                        if g == 0 and tt == 0 and k == 0:
                            pe.wait_ge(wlo, CH["dft1"] + 1)
                        xh, xl = (a[:, 2 * g + k, tt * P:(tt + 1) * P] for a in (a_hi, a_lo))
                        wh, wl = (w[:, slot, k * S:(k + 1) * S] for w in (w_hi, w_lo))
                        out = banks[:, t % 4, :]
                        mm = pe.matmul(out, xh, wl, start=(k == 0), stop=False)
                        if g == 0 and tt == 0 and k == 0:
                            mm.then_inc(w_used, 1)
                        pe.matmul(out, xl, wh, start=False, stop=False)
                        mm = pe.matmul(out, xh, wh, start=False, stop=(k == 1))
                    mm.then_inc(tile_ready, 1)
            t1 = TI["dft2"]
            c0 = CH["dft2"]
            for b in range(4):
                wait_bank(flat, t1 + b)
            begun = set()
            for m in range(KD):
                t = t1 + m
                wait_bank(flat, t)
                g, half = divmod(m, 2)
                for n in range(8):
                    part, tt = divmod(n, 4)
                    c = c0 + n // 2
                    z = g * 4 + tt
                    Zh, Zl = (b_hi[:, z, :], b_lo[:, z, :]) if z < 12 else (a_hi[:, z - 12, :], a_lo[:, z - 12, :])
                    lc = slice(part * 256 + half * P, part * 256 + half * P + P)
                    wc = slice((n % 2) * S, (n % 2 + 1) * S)
                    wh, wl = w_hi[:, c % RING, wc], w_lo[:, c % RING, wc]
                    new = c not in begun
                    if new:
                        begun.add(c)
                        pe.wait_ge(wlo, c + 1)
                    out = banks[:, t % 4, :]
                    mm = pe.matmul(out, Zh[:, lc], wl, start=(n == 0), stop=False)
                    if c == c0 and new:
                        mm.then_inc(w_used, 1)
                    elif m == KD - 1 and n in (2, 4, 6):
                        mm.then_inc(w_used, 1)
                    pe.matmul(out, Zl[:, lc], wh, start=False, stop=False)
                    mm = pe.matmul(out, Zh[:, lc], wh, start=False, stop=(n == 7))
                mm.then_inc(tile_ready, 1)
            ada_reduce(flat, AUX["ada6"], 6)
            pos[0] = CH["fout"]

            def f_rhs(k):
                return (a_hi[:, 4 + k, :], a_lo[:, 4 + k, :]) if k < 4 else (b_hi[:, k - 4, :], b_lo[:, k - 4, :])
            gemm(flat, TI["fout"], KD, range(KD), f_rhs, lambda k: wait_read(pe, flat, t1 + k))
            norm_stats(4, "ffn0")
            ada_reduce(flat, AUX["ada7"], 7)

            def swiglu(layer, a_in, with_ada):
                for part, n_hid in zip("ab", HALF):
                    c, t = CH[f"up{layer}{part}"], TI[f"up{layer}{part}"]
                    assert pos[0] == c
                    first = 1 if part == "a" else 0
                    if first:
                        gemm(flat, t, 4, range(KD), rhs_a, lambda k: pe.wait_ge(a_ready, KD * a_in + k + 1))
                    with pe.Fori(0, n_hid // 2 - first) as i:
                        at = At(i, chunk=4, tile=4, bank=1, ada=8, aux=1)
                        gemm(at, t + 4 * first, 4, range(KD), rhs_a, None, False)
                        if first and with_ada:
                            ada_reduce(at, AUX["ada"], 8)
                    pos[0] = CH[f"down{layer}{part}"]
                    base_t = TI[f"down{layer}{part}"]
                    def last_ada(n):
                        if n == 23:
                            ada_reduce(flat, AUX["ada"] + 5, 13)
                    gemm(flat, base_t, KD, range(n_hid), rhs_b, lambda k: wait_read(pe, flat, t + 2 * k + 1),
                         hook=last_ada if first and with_ada else None)

            swiglu(0, 2, True)
            norm_stats(5, "rnorm")

            def token_major(at, t0):
                for k in range(KD):
                    for tt in range(TB):
                        if k == 0:
                            wait_bank(at, t0 + tt)
                        if tt == 0:
                            begins, wh, wl = chunk_begins(at, S)
                        c = slice(tt * P, (tt + 1) * P)
                        out = banks[:, (t0 + tt) % 4, :]
                        mm = pe.matmul(out, a_hi[:, k, c], wl, start=(k == 0), stop=False)
                        if begins and tt == 0:
                            mm.then_inc(w_used, 1)
                        pe.matmul(out, a_lo[:, k, c], wh, start=False, stop=False)
                        mm = pe.matmul(out, a_hi[:, k, c], wh, start=False, stop=(k == KD - 1))
                        if k == KD - 1:
                            mm.then_inc(tile_ready, 1)

            def head(at, t, with_out, first_wait):
                gemm(at, t, 4, range(KD), rhs_a, first_wait)
                tk = t
                t += 4
                if with_out:
                    prev = at.before()
                    gemm(at, t, KD, range(4), lambda k: rhs_b(8 + k),
                         lambda k: pe.wait_ge(y_ready, prev("four", k + 1)))
                    t += 8
                token_major(at, t)
                tv = t
                t += 4
                for n in range(3):
                    gemm(at, t + n, 1, range(KD), rhs_a, None, False)
                t += 3
                for s in range(TB):
                    wait_bank(at, t + s)
                    if s == 0:
                        pe.wait_ge(rot_ready, at("four", 4))
                    out = banks[:, (t + s) % 4, :]
                    for d in range(2):
                        c = slice(s * P, (s + 1) * P)
                        pe.matmul(out, b_lo[:, d, c], b_hi[:, 2 + d, :], start=(d == 0), stop=False)
                        pe.matmul(out, b_hi[:, d, c], b_lo[:, 2 + d, :], start=False, stop=False)
                        mm = pe.matmul(out, b_hi[:, d, c], b_hi[:, 2 + d, :], start=False, stop=(d == 1))
                    mm.then_inc(tile_ready, 1)
                ts = t
                t += 4
                gemm(at, t, 1, range(KD), rhs_a, None, False)
                t += 1
                for s in range(TB):
                    wait_read(pe, at, tv + s)
                for n in range(4):
                    wait_bank(at, t + n)
                    out = banks[:, (t + n) % 4, :]
                    for s in range(TB):
                        if n == 0:
                            wait_read(pe, at, ts + s)
                        c = slice(n * P, (n + 1) * P)
                        pe.matmul(out, b_lo[:, 4 + s, c], b_hi[:, 8 + s, :], start=(s == 0), stop=False)
                        pe.matmul(out, b_hi[:, 4 + s, c], b_lo[:, 8 + s, :], start=False, stop=False)
                        mm = pe.matmul(out, b_hi[:, 4 + s, c], b_hi[:, 8 + s, :], start=False, stop=(s == 3))
                    mm.then_inc(tile_ready, 1)
                pe.wait_ge(y_sum, at("one", 1))
                stats(at, AUX["ret"])
                pe.wait_ge(y_qs, at("three", 3))
                stats(at, AUX["ret"] + 1)

            head(flat, TI["ret"], False, lambda k: pe.wait_ge(a_ready, 3 * KD + k + 1))
            with pe.Fori(0, NH - 1) as i:
                head(Head(i, chunk=16, tile=28, bank=7, aux=2, four=4, three=3, one=1), TI["retbody"], True, None)
            pos[0] = CH["retout"]
            gemm(flat, TI["retout"], KD, range(4), lambda k: rhs_b(8 + k),
                 lambda k: pe.wait_ge(y_ready, 4 * (NH - 1) + k + 1))
            norm_stats(6, "ffn1")
            swiglu(1, 4, False)
            norm_stats(7, "final")


def weight_stream(w_in, w_out, w_ple_proj, w_ple_gate, w_fourier_out, w_ret_in, w_ret_out, w_ffn_in, w_ffn_out, dfts):
    import numpy as np
    tiles = []

    def tile(w, k, c):
        tiles.append(w[k * P:(k + 1) * P, c:c + P])

    def gemm(w, K, M, ks=None, first_outer=True, k0=0, cols=None):
        for k, m in gemm_order(K, M, ks, first_outer):
            tile(w, k0 + k, cols[m] if cols else m * P)

    for j in range(NH):
        gemm(w_in, KD, 8, None, False, 0, [part * 512 + j * P for part in range(8)])
    gemm(w_out, KD, KD, ATT_KS)
    gemm(w_ple_proj, 2, KD, None, False)
    gemm(w_ple_gate, KD, KD)
    for w in dfts:
        for k in range(w.shape[0] // P):
            for c in range(4):
                tile(w, k, c * P)
    gemm(w_fourier_out, KD, KD)

    def swiglu(layer):
        k0 = 0
        for n_hid in HALF:
            for b in range(n_hid // 2):
                f = k0 + 2 * b
                cols = [f * P, FF + f * P, (f + 1) * P, FF + (f + 1) * P]
                gemm(w_ffn_in[layer], KD, 4, None, k0 == 0 and b == 0, 0, cols)
            gemm(w_ffn_out[layer], n_hid, KD, None, True, k0)
            k0 += n_hid

    swiglu(0)
    for h in range(NH + 1):
        if h < NH:
            gemm(w_ret_in, KD, 4, None, True, 0, [1024 + h * 256, 1024 + h * 256 + P, h * 256, h * 256 + P])
        if h:
            gemm(w_ret_out, 4, KD, None, True, 4 * (h - 1))
        if h < NH:
            for k in range(KD):
                for c in range(4):
                    tile(w_ret_in, k, 2048 + h * 512 + c * P)
            gemm(w_ret_in, KD, 4, None, False, 0, [4096 + h * 512 + n * P for n in range(4)])
    swiglu(1)
    assert len(tiles) == 8 * N_CHUNK, (len(tiles), 8 * N_CHUNK)
    out = np.empty((N_CHUNK, P, 8, P), np.float32)
    for n, t in enumerate(tiles):
        out[n // 8, :, n % 8] = t
    return out.reshape(N_CHUNK, P, 1024)


def tables():
    import numpy as np
    j = np.arange(256)
    ang = 2 * np.pi * (np.outer(j, j) % 256) / 256
    scale = (S * 256) ** -0.5
    feat = np.concatenate([np.cos(ang), np.sin(ang)], 1) * scale
    t = np.arange(S)
    ang = 2 * np.pi * (np.outer(t, t) % S) / S
    dfts = [a.astype(np.float32) for a in (feat, np.cos(ang), -np.sin(ang))]
    p, u = np.arange(P)[:, None], np.arange(S)[None, :] - 3 * P
    dist = np.where(u // 64 <= p // 64, -np.abs(p - u).astype(np.float64), -1e30).astype(np.float32)
    inv = np.float32(10000.0) ** (-np.arange(P, dtype=np.float32) / np.float32(P))
    a = (inv[:, None] * t[None, :].astype(np.float32)).astype(np.float32)
    rope = np.concatenate([np.cos(a), np.sin(a)], 1).astype(np.float32)
    h = np.arange(NH)[:, None, None]
    d = np.arange(896)[None, None, :] - 3 * P - np.arange(P)[None, :, None]
    fwd, bwd = np.log1p(-2.0 ** (-5.0 - h)), np.log1p(-2.0 ** (-5.0 - (NH - 1 - h)))
    decay = (np.where(d >= 0, np.exp(d * fwd), np.exp(-d * bwd)) / 16).astype(np.float32)
    return dfts, dist, rope, decay


def kernel(**inputs):
    import numpy as np
    import concourse.bacc as bacc
    from concourse.bass_utils import run_bass_kernel_spmd as run
    a = {k: np.asarray(v) for k, v in inputs.items()}
    dfts, dist, rope, decay = tables()
    stream = weight_stream(a["w_in"][0], a["w_out"][0], a["w_ple_proj"][0], a["w_ple_gate"][0],
                           a["w_fourier_out_2"][0], a["w_ret_in_2"][0], a["w_ret_out_2"][0], a["w_ffn_in_2"],
                           a["w_ffn_out_2"], dfts)

    def tokens(x):
        return np.ascontiguousarray(x.T.reshape(-1, P, S).transpose(1, 0, 2)).reshape(P, -1)

    def vec(v):
        return v.reshape(-1, P).T

    def groups(w):
        return w.reshape(KD, P, -1, D).transpose(2, 0, 1, 3).reshape(-1, P, D)

    ada = np.concatenate([groups(a["w_ada_2"][0]), groups(a["w_ada_2"][1]), groups(a["w_ada_final_2"])])
    conv = a["conv_w"][0].reshape(3, NH, P).transpose(2, 1, 0).reshape(P, 3 * NH)
    lam = np.concatenate([a[n][0] for n in ("lambda_q1", "lambda_q2", "lambda_k1", "lambda_k2")])
    slopes = np.float32(2.0) ** (-2.0 * np.arange(1, NH + 1, dtype=np.float32))
    cols = np.concatenate([
        vec(a["pre_norm_gain"][0]), vec(a["post_norm_gain"][0]), vec(a["ple_norm_gain"][0]),
        vec(a["final_norm_g_2"]), vec(a["subln_gain"][0]), conv, vec(a["c_2"][0]), vec(a["b_ada_2"].reshape(-1)),
        vec(a["b_ada_final_2"]), vec(a["norm_mix_g_2"].reshape(-1)), vec(a["norm_ffn_g_2"].reshape(-1)),
        np.broadcast_to(lam, (P, 256)), np.broadcast_to(slopes, (P, NH)), np.eye(P, dtype=np.float32),
    ], 1)
    assert cols.shape == (P, NCOL)
    data = dict(W=stream, ADA=np.ascontiguousarray(ada), XT=tokens(a["x"][0]), PT=tokens(a["p"][0, 0]),
                COLS=np.ascontiguousarray(cols), DIST=dist, ROPE=rope, DECAY=decay)
    nc = bacc.Bacc("TRN2", target_bir_lowering=False, num_devices=1)
    aps = {k: nc.dram_tensor(f"in_{k}", v.shape, mybir.dt.float32, kind="ExternalInput").ap() for k, v in data.items()}
    out = nc.dram_tensor("out", (P, KD, S), mybir.dt.float32, kind="ExternalOutput").ap()
    aps["XT"] = aps["XT"].rearrange("p (k s) -> p k s", s=S)
    build(nc, OUT=out, **aps)
    r = run(nc, [{f"in_{k}": v for k, v in data.items()}], core_ids=[0])
    return r.results[0]["out"].transpose(2, 1, 0).reshape(1, S, D)
```

```python
import concourse.bass as bass
from concourse import mybir
from contextlib import ExitStack

P = 128
S = 512
D = 1024
KD = D // P
NH = 4
FF = 2816
FT = FF // P
HALF = (12, FT - 12)
TB = S // P
RING = 4
LAM_INIT = 0.2
N_ADA = 14
ADA_RING = 2
ADA_LAG = 6

COL = {}
NCOL = 0
for _name, _n in (("pre", KD), ("post", KD), ("ple", KD), ("final", KD), ("subln", 1), ("conv", 3 * NH),
                  ("c", KD), ("b_ada", N_ADA * KD), ("mix", 2 * KD), ("ffn", 2 * KD), ("lam", 4 * 64),
                  ("slope", NH), ("ident", P)):
    COL[_name] = NCOL
    NCOL += _n


def gemm_order(K, M, ks=None, first_outer=True):
    ks = list(ks or range(K))
    out = []
    m0 = 0
    if first_outer:
        m0 = 4
        out += [(k, m) for k in ks[:-2] for m in range(4)]
        out += [(k, m) for m in range(4) for k in ks[-2:]]
    return out + [(k, m) for m in range(m0, M) for k in ks]


ATT_KS = (0, 1, 2, 4, 5, 6, 7, 3)
CH = {}
_c = 0
for _name, _n in (("body", 8 * NH), ("out", 8), ("ple", 2), ("gate", 8), ("dft1", 1), ("dft2", 4), ("fout", 8),
                  ("up0a", 24), ("down0a", 12), ("up0b", 20), ("down0b", 10),
                  ("ret", 12), ("retbody", 16 * (NH - 1)), ("retout", 4),
                  ("up1a", 24), ("down1a", 12), ("up1b", 20), ("down1b", 10)):
    CH[_name] = _c
    _c += _n
N_CHUNK = _c

TI = {}
_c = 0
for _name, _n in (("body", 8 * NH), ("out", 8), ("ple", 8), ("gate", 8), ("dft1", 16), ("dft2", 8), ("fout", 8),
                  ("up0a", 24), ("down0a", 8), ("up0b", 20), ("down0b", 8),
                  ("ret", 20), ("retbody", 28 * (NH - 1)), ("retout", 8),
                  ("up1a", 24), ("down1a", 8), ("up1b", 20), ("down1b", 8)):
    TI[_name] = _c
    _c += _n

AUX = {}
_c = 0
for _name, _n in (("pre", 1), ("body", 7 * NH), ("post", 1), ("ada4", 1), ("ple", 1), ("four", 1), ("ada5", 1),
                  ("ada6", 1), ("ffn0", 1), ("ada7", 1), ("ada", 6), ("rnorm", 1),
                  ("ret", 2 * NH), ("ffn1", 1), ("final", 1)):
    AUX[_name] = _c
    _c += _n


class At:

    def __init__(self, i=None, **per):
        self.i, self.per = i, per

    def __call__(self, kind, n):
        return n if self.i is None else self.i * self.per[kind] + n


class Head(At):

    def __call__(self, kind, n):
        ahead = self.per[kind] if kind in ("aux", "four", "three", "one", "sixteen") else 0
        return super().__call__(kind, n + ahead)

    def before(self):
        return At(self.i, **self.per)


def build(nc, W, ADA, XT, PT, COLS, DIST, ROPE, DECAY, OUT):
    fp32, f32r = mybir.dt.float32, mybir.dt.float32r
    ALU, ACT, AX = mybir.AluOpType, mybir.ActivationFunctionType, mybir.AxisListType
    ctx = ExitStack()
    with ctx:
        def sb(name, shape, dt=fp32):
            return ctx.enter_context(nc.sbuf_tensor(name, shape, dt))

        def sem(name):
            return ctx.enter_context(nc.semaphore(name))

        w_raw = sb("w_raw", [P, RING, 1024])
        w_hi = sb("w_hi", [P, RING, 1024], f32r)
        w_lo = sb("w_lo", [P, RING, 1024], f32r)
        ada_raw = sb("ada_raw", [P, ADA_RING, 1024])
        ada_acc = sb("ada_acc", [P, 1024])
        X = sb("X", [P, KD, S])
        a_hi = sb("a_hi", [P, KD, S], f32r)
        a_lo = sb("a_lo", [P, KD, S], f32r)
        b_hi = sb("b_hi", [P, 12, S], f32r)
        b_lo = sb("b_lo", [P, 12, S], f32r)
        sq = sb("sq", [P, 2, S])
        sqsum = sb("sqsum", [P, S])
        rinv = sb("rinv", [P, S])
        tmp = sb("tmp", [P, 2, S])
        cols = sb("cols", [P, NCOL])
        ones = sb("ones", [P, P])
        small = sb("small", [P, 64])
        mod = sb("mod", [P, N_ADA * KD])
        gs = sb("gs", [P, 5 * KD])
        scr = sb("scr", [P, 9216])
        banks = ctx.enter_context(nc.psum_tensor("banks", [P, 8, 512], fp32))
        aux = banks[:, 7, :]

        ident = cols[:, COL["ident"]:COL["ident"] + P]
        zero, eps6, eps5, neglam, gsub = (small[:, n:n + 1] for n in range(5))
        lamv = small[:, 6:8]
        mx, nmx, rsum, rrec, c1 = (small[:, n:n + 2] for n in (8, 10, 12, 14, 16))
        lamp = small[:, 18:20]
        cact = small[:, 24:32]
        ctanh = small[:, 32:40]
        gple = small[:, 40:48]
        cwork = small[:, 48:56]

        def area(n, k=1):
            v = scr[:, n * S:(n + k) * S]
            return v if k == 1 else v.rearrange("p (k s) -> p k s", k=k)

        Q, K, VB, ZA, dist, bias = (area(n) for n in range(6))
        SC = area(6, 4).rearrange("p (u m) s -> p u m s", m=2)
        WT = area(10, 2)
        CG = area(12)
        G = scr[:, 13 * S:14 * S + 2]
        lamt = scr[:, 15 * S:15 * S + 256]
        MIX, E = area(0, 8), area(8, 8)
        PV = scr[:, 16 * S:18 * S]
        GT = [tmp[:, 0, :], tmp[:, 1, :], area(16), area(17)]
        XG = {"pre": area(6, 8), "four": area(0, 8), "ffn0": area(10, 8), "rnorm": area(10, 8), "ffn1": area(10, 8)}
        KQ = ada_raw[:, :, :].rearrange("p a (b s) -> p (a b) s", s=S)
        T2 = area(0, 2)
        SG = area(2, 2)
        HD = area(4, 2)
        GG, Y = area(0, 4), area(4, 4)
        COS, SIN = area(8), area(9)
        DEC = scr[:, 10 * S:10 * S + 896]
        RT = area(12, 4)

        raw_in = [sem(f"raw_in{s}") for s in range(RING)]
        whi = sem("whi")
        wlo = sem("wlo")
        w_used = sem("w_used")
        ada_in = [sem(f"ada_in{s}") for s in range(ADA_RING)]
        ada_sum = sem("ada_sum")
        x_in = [sem(f"x_in{m}") for m in range(KD)]
        cols_in, p_in, dist_in, rope_in, dec_in = (
            sem(n) for n in ("cols_in", "p_in", "dist_in", "rope_in", "dec_in"))
        const = sem("const")
        link_s = sem("dve_link")
        tile_ready = sem("tile_ready")
        bank_read = [sem(f"bank_read{b}") for b in range(4)]
        aux_ready, aux_free = sem("aux_ready"), sem("aux_free")
        sq_ready, sq_added, r_ready = sem("sq_ready"), sem("sq_added"), sem("r_ready")
        xg_s = sem("xg_s")
        h_ready, h_hi, a_ready = sem("h_ready"), sem("h_hi"), sem("a_ready")
        lam_in, lam_e = sem("lam_in"), sem("lam_e")
        za_t, sc_ready, sc_read, nm_ready, ex_ready, w_ready = (
            sem(n) for n in ("za_t", "sc_ready", "sc_read", "nm_ready", "ex_ready", "w_ready"))
        v_hi, wt_hi, pv_ready, o_copied, o_sq, o_r, o_out, mix_hi, mix_ready = (
            sem(n) for n in ("v_hi", "wt_hi", "pv_ready", "o_copied", "o_sq", "o_r", "o_out", "mix_hi",
                             "mix_ready"))
        zc_t, cv_out = sem("zc_t"), sem("cv_out")
        p_hi, p_ready = sem("p_hi"), sem("p_ready")
        x_new, xg_hi, xg_ready, e_copied, e_ready, gt = (
            sem(n) for n in ("x_new", "xg_hi", "xg_ready", "e_copied", "e_ready", "gt"))
        z_hi, f_hi = sem("z_hi"), sem("f_hi")
        hid_t, hid_s, hid_f, hid_hi, hid_ready = (sem(n) for n in ("hid_t", "hid_s", "hid_f", "hid_hi", "hid_ready"))
        x_done = sem("x_done")
        rot, rot_hi, rot_ready, vv_hi, gg_t, pd, pd_hi, y_sum, y_cen, y_sq, y_qs, y_r, y_f, y_hi, y_ready = (
            sem(n) for n in ("rot", "rot_hi", "rot_ready", "vv_hi", "gg_t", "pd", "pd_hi", "y_sum",
                             "y_cen", "y_sq", "y_qs", "y_r", "y_f", "y_hi", "y_ready"))
        out_done = sem("out_done")

        block = ctx.enter_context(nc.Block())
        NORMS = dict(pre=0, post=1, ple=2, four=3, ffn0=4, rnorm=5, ffn1=6, final=7)
        APPLY = dict(pre=0, four=1, ffn0=2, rnorm=3, ffn1=4)

        def col(name, n=0, k=1):
            return cols[:, COL[name] + n:COL[name] + n + k]

        def wait_tile(eng, at, t):
            eng.wait_ge(tile_ready, at("tile", t + 1))

        def read_out(ins, t):
            ins.then_inc(bank_read[t % 4], 1)

        def wait_read(eng, at, t):
            eng.wait_ge(bank_read[t % 4], at("bank", t // 4 + 1))

        flat = At()

        @block.sync
        def _(sp):
            def load_w(at, c, first=False):
                if not first:
                    sp.wait_ge(wlo, at("chunk", c - RING + 1))
                src = W[c] if at.i is None else W[bass.ds(at("chunk", c), 1), :, :].rearrange("a p n -> (a p) n")
                sp.dma_start(w_raw[:, c % RING, :], src).then_inc(raw_in[c % RING], 16)

            def load_ada(at, a, first=False):
                if not first:
                    sp.wait_ge(ada_sum, at("ada", a - ADA_RING + 1))
                src = ADA[a] if at.i is None else ADA[bass.ds(at("ada", a), 1), :, :].rearrange("a p n -> (a p) n")
                sp.dma_start(ada_raw[:, a % ADA_RING, :], src).then_inc(ada_in[a % ADA_RING], 16)

            for m in range(KD):
                sp.dma_start(X[:, m, :], XT[:, m, :]).then_inc(x_in[m], 16)
            pos = [0, 0]

            def load(at, k):
                load_w(at, pos[0], at.i is None and pos[0] < RING)
                pos[0] += 1
                for _ in range(k):
                    load_ada(at, pos[1], at.i is None and pos[1] < ADA_RING)
                    pos[1] += 1

            for turns, chunks, k in ((0, ADA_LAG, 0), (0, 4, 1), (9, 4, 1), (0, 2, 0), (2, 4, 1), (0, 3, 2), (0, 2, 1),
                                     (2, 4, 1), (6, 4, 2), ((N_CHUNK - 93) // 4, 4, 0), (0, (N_CHUNK - 93) % 4, 0)):
                if turns:
                    with sp.Fori(0, turns) as i:
                        for _ in range(chunks):
                            load(At(i, chunk=chunks, ada=chunks * k), k)
                    pos[0] += (turns - 1) * chunks
                    pos[1] += (turns - 1) * chunks * k
                else:
                    for _ in range(chunks):
                        load(flat, k)
            assert pos == [N_CHUNK, N_ADA * KD], pos
            for m in range(KD):
                sp.wait_ge(x_done, m + 1)
                sp.dma_start(OUT[:, m, :], X[:, m, :]).then_inc(out_done, 16)
            sp.wait_ge(out_done, 16 * KD)

        @block.gpsimd
        def _(pool):
            def lo_part(at, c, first=False):
                pool.wait_ge(whi, at("chunk", c + 1))
                pool.tensor_tensor(w_lo[:, c % RING, :], w_raw[:, c % RING, :],
                                   w_hi[:, c % RING, :].bitcast(fp32), ALU.subtract).then_inc(wlo, 1)

            n = N_CHUNK // 4
            with pool.Fori(0, n) as i:
                at = At(i, chunk=4)
                for s in range(4):
                    lo_part(at, s)
            for c in range(4 * n, N_CHUNK):
                lo_part(flat, c)

        @block.scalar
        def _(act):
            act.dma_start(cols[:, :], COLS).then_inc(cols_in, 16)
            act.dma_start(dist, DIST).then_inc(dist_in, 16)

            def split_w(at, c, first=False):
                if c >= N_CHUNK:
                    return
                act.wait_ge(raw_in[c % RING], at("slot", 16 * (c // RING + 1)))
                if not first:
                    act.wait_ge(w_used, at("chunk", c - RING + 1))
                act.activation(w_hi[:, c % RING, :], w_raw[:, c % RING, :], ACT.Copy).then_inc(whi, 1)

            def square(at, v, m, src):
                if m >= 3:
                    act.wait_ge(sq_added, 6 * v + m - 2)
                dst = sqsum[:, :] if m == 0 else sq[:, m % 2, :]
                act.activation(dst, src, ACT.Square).then_inc(sq_ready, 1)

            def rsqrt(u, n, eps, done, at=flat):
                act.preload_act_table_set("natural_log_exp_and_others")
                act.wait_ge(aux_ready, at("aux", u + 1))
                act.activation(rinv[:, :], aux, ACT.Ln, bias=eps, scale=1.0 / n).then_inc(aux_free, 1)
                act.wait_ge(aux_free, at("aux", u + 1))
                act.activation(rinv[:, :], rinv[:, :], ACT.Exp, scale=-0.5).then_inc(done, 1)

            def norm_hi(v, shift, c=None, first_chunks=False, after=None):
                for m in range(KD):
                    if first_chunks and m in (1, 2, 3):
                        split_w(flat, m, True)
                    if m == 2 and c is not None:
                        split_w(flat, c)
                    act.wait_ge(h_ready, 8 * v + m + 1)
                    act.activation(a_hi[:, m, :], tmp[:, m % 2, :], ACT.Identity, bias=shift(m)).then_inc(h_hi, 1)
                    if after:
                        after(m)

            def vector(g):
                return lambda m: mod[:, KD * g + m:KD * g + m + 1]

            act.wait_ge(cols_in, 16)
            for m in range(KD):
                act.wait_ge(x_in[m], 16)
                square(flat, 0, m, X[:, m, :])
            split_w(flat, 0, True)
            act.wait_ge(const, 1)
            rsqrt(AUX["pre"], D, eps6, r_ready)
            norm_hi(0, lambda m: zero, first_chunks=True)
            act.activation(ctanh, col("c", 0, KD), ACT.Tanh, scale=0.5).then_inc(lam_e, 1)
            act.wait_ge(lam_in, 1)
            act.activation(lamv, lamp, ACT.Exp).then_inc(lam_e, 1)

            t0, c0 = TI["body"], CH["body"]

            def exps(at, b):
                n = (b + 1) * P
                act.wait_ge(nm_ready, at("unit", b + 1))
                for m in range(2):
                    act.activation(SC[:, b % 2, m, 0:n], SC[:, b % 2, m, 0:n], ACT.Exp, bias=nmx[:, m:m + 1],
                                   accum_out=rsum[:, m:m + 1]).then_inc(ex_ready, 1)

            def weights_hi(at, b):
                n = (b + 1) * P
                act.wait_ge(aux_ready, at("aux", AUX["body"] + 1 + b + 1))
                act.activation(b_hi[:, 9 + b % 2, 0:n], aux[:, 0:n], ACT.Copy).then_inc(wt_hi, 1)

            with act.Fori(0, NH) as i:
                at = At(i, chunk=8, slot=32, tile=8, bank=2, aux=7, unit=4, one=1, two=2, eight=8)
                for n, dst in ((0, Q), (1, K), (2, VB)):
                    split_w(at, c0 + n + 4)
                    wait_tile(act, at, t0 + n)
                    read_out(act.activation(dst, banks[:, n, :], ACT.Copy), n)
                exps(at, 0)
                split_w(at, c0 + 7)
                wait_tile(act, at, t0 + 3)
                act.activation(tmp[:, 1, :], banks[:, 3, :], ACT.Tanh, scale=0.5).then_inc(za_t, 1)
                exps(at, 1)
                act.wait_ge(aux_ready, at("aux", AUX["body"] + 1))
                act.activation(b_hi[:, 8, :], aux, ACT.Copy).then_inc(v_hi, 1)
                split_w(at, c0 + 8)
                wait_tile(act, at, t0 + 4)
                read_out(act.activation(VB, banks[:, 0, :], ACT.Copy), t0 + 4)
                weights_hi(at, 0)
                exps(at, 2)
                split_w(at, c0 + 9)
                wait_tile(act, at, t0 + 5)
                read_out(act.activation(CG, banks[:, 1, :], ACT.Copy), t0 + 5)
                weights_hi(at, 1)
                exps(at, 3)
                split_w(at, c0 + 10)
                weights_hi(at, 2)
                weights_hi(at, 3)
                wait_tile(act, at, t0 + 7)
                act.activation(tmp[:, 1, :], banks[:, 3, :], ACT.Tanh, scale=0.5).then_inc(zc_t, 1)
                act.wait_ge(pv_ready, at("one", 1))
                act.activation(sq[:, 0, :], banks[:, 4, :], ACT.Copy).then_inc(o_copied, 1)
                act.activation(sqsum[:, :], banks[:, 4, :], ACT.Square).then_inc(o_sq, 1)
                act.wait_ge(cv_out, at("one", 1))
                act.activation(b_hi[:, bass.ds(i + 4, 1), :].rearrange("p a s -> p (a s)"), tmp[:, 0, :], ACT.Copy,
                               scale=0.5).then_inc(mix_hi, 1)
                split_w(at, c0 + 11)
                rsqrt(AUX["body"] + 5, P, eps5, o_r, at)
                act.wait_ge(o_out, at("one", 1))
                act.activation(b_hi[:, bass.ds(i, 1), :].rearrange("p a s -> p (a s)"), tmp[:, 0, :],
                               ACT.Copy).then_inc(mix_hi, 1)

            act.dma_start(PV, PT).then_inc(p_in, 16)
            act.wait_ge(p_in, 16)
            act.activation(b_hi[:, 8:10, :].rearrange("p k s -> p (k s)"), PV, ACT.Copy).then_inc(p_hi, 1)
            c0, t0 = CH["out"], TI["out"]
            for n in range(8):
                if n != 3:
                    split_w(flat, c0 + n + 4)
                if n >= 3:
                    for m in ((0, 1, 2, 3) if n == 3 else (n,)):
                        wait_tile(act, flat, t0 + m)
                        square(flat, 1, m, banks[:, m % 4, :])
                        if n == 3 and m == 0:
                            split_w(flat, c0 + n + 4)

            def e_tile(m):
                t = TI["ple"] + m
                wait_tile(act, flat, t)
                square(flat, 2, m, banks[:, t % 4, :])
                read_out(act.activation(E[:, m, :], banks[:, t % 4, :], ACT.Copy), t)

            for m in range(2):
                if m == 0:
                    rsqrt(AUX["post"], D, eps6, r_ready)
                e_tile(m)
            for m in range(2, KD):
                if m == 4:
                    split_w(flat, CH["ple"] + 4)
                if m == 7:
                    split_w(flat, CH["ple"] + 5)
                e_tile(m)
                if m >= 3:
                    act.wait_ge(x_new, m - 2)
                    act.activation(a_hi[:, m - 3, :], X[:, m - 3, :], ACT.Copy).then_inc(xg_hi, 1)
            for m in range(5, KD):
                act.wait_ge(x_new, m + 1)
                act.activation(a_hi[:, m, :], X[:, m, :], ACT.Copy).then_inc(xg_hi, 1)
            c0, t0 = CH["gate"], TI["gate"]

            def residual_squares(v, t0, ms):
                for m in ms:
                    wait_read(act, flat, t0 + m)
                    square(flat, v, m, X[:, m, :])

            def gate_tile(m):
                wait_tile(act, flat, t0 + m)
                if m >= 4:
                    act.wait_ge(x_new, KD + m - 3)
                read_out(act.activation(GT[m % 4], banks[:, (t0 + m) % 4, :], ACT.Tanh, scale=0.5), t0 + m)

            def gate_square(m):
                act.wait_ge(x_new, KD + m + 1)
                square(flat, 3, m, X[:, m, :])

            for n in range(8):
                if n not in (3, 7):
                    split_w(flat, c0 + n + 4)
                if n == 1:
                    rsqrt(AUX["ple"], D, eps6, r_ready)
                if n >= 3:
                    for m in ((0, 1, 2, 3) if n == 3 else (n,)):
                        gate_tile(m)
                        if n == 3 and m == 0:
                            split_w(flat, c0 + n + 4)
                        if m:
                            gate_square(m - 1)
            gate_square(7)
            rsqrt(AUX["four"], D, eps6, r_ready)

            t1 = TI["dft1"]

            def z_group(g):
                for z in range(4 * g, 4 * g + 4):
                    wait_tile(act, flat, t1 + z)
                    dst = b_hi[:, z, :] if z < 12 else a_hi[:, z - 12, :]
                    act.activation(dst, banks[:, (t1 + z) % 4, :], ACT.Copy).then_inc(z_hi, 1)

            norm_hi(1, vector(0), c0 + 11, after=lambda m: z_group((m - 3) // 2) if m in (3, 5, 7) else None)
            c0 = CH["dft1"]
            z_group(3)
            split_w(flat, c0 + 4)
            c0, t0 = CH["dft2"], TI["dft2"]
            for m in range(KD):
                if m == KD - 1:
                    for n in range(3):
                        split_w(flat, c0 + n + 4)
                wait_tile(act, flat, t0 + m)
                dst = a_hi[:, 4 + m, :] if m < 4 else b_hi[:, m - 4, :]
                act.activation(dst, banks[:, (t0 + m) % 4, :], ACT.Copy).then_inc(f_hi, 1)
            split_w(flat, c0 + 3 + 4)
            c0, t0 = CH["fout"], TI["fout"]
            for n in range(8):
                if n < 7:
                    split_w(flat, c0 + n + 4)
                if n >= 3:
                    residual_squares(4, t0, (0, 1, 2, 3) if n == 3 else (n,))

            def up_body(at, c, t, j):
                for n in range(2):
                    split_w(at, c + 2 * n + 4)
                    wait_tile(act, at, t + 2 * n)
                    act.activation(T2[:, n, :], banks[:, (t + 2 * n) % 4, :], ACT.Tanh, scale=0.5).then_inc(hid_t, 1)
                    split_w(at, c + 2 * n + 5)
                    act.wait_ge(hid_f, at("hid", j + n + 1))
                    if at.i is None:
                        dst = b_hi[:, j % FT % HALF[0] + n, :]
                    else:
                        dst = b_hi[:, bass.ds(at("hid", j % FT % HALF[0] + n), 1), :].rearrange("p a s -> p (a s)")
                    act.activation(dst, HD[:, n, :], ACT.Copy, scale=0.5).then_inc(hid_hi, 1)

            def swiglu(layer, v):
                rsqrt(AUX[f"ffn{layer}"], D, eps6, r_ready)
                norm_hi(2 + 2 * layer, vector(6 * layer + 3), CH[f"up{layer}a"] + 3)
                for part, n_hid in zip("ab", HALF):
                    c, t = CH[f"up{layer}{part}"], TI[f"up{layer}{part}"]
                    j = layer * FT + (0 if part == "a" else HALF[0])
                    first = 1 if part == "a" else 0
                    if first:
                        up_body(flat, c, t, j)
                    with act.Fori(0, n_hid // 2 - first) as i:
                        at = At(i, chunk=4, slot=16, tile=4, hid=2)
                        up_body(at, c + 4 * first, t + 4 * first, j + 2 * first)
                    c, t = CH[f"down{layer}{part}"], TI[f"down{layer}{part}"]
                    for n in range(n_hid):
                        if part == "a" or n < n_hid - 1:
                            split_w(flat, c + n + 4)
                        if part == "b":
                            done = [m for m in range(KD) if down_last(n_hid, m) == n]
                            residual_squares(v, t, done)

            def down_last(K, m):
                order = gemm_order(K, KD)
                return max(n for n, (k, mm) in enumerate(order) if mm == m) // 8

            swiglu(0, 5)

            act.dma_start(scr[:, 8 * S:10 * S], ROPE).then_inc(rope_in, 16)
            rsqrt(AUX["rnorm"], D, eps6, r_ready)
            norm_hi(3, vector(6), CH["ret"] + 3)

            def keys_queries(at, c, t):
                for n in range(3):
                    split_w(at, c + n + 4)
                for n in range(4):
                    wait_tile(act, at, t + n)
                    read_out(act.activation(KQ[:, n, :], banks[:, (t + n) % 4, :], ACT.Copy), t + n)
                split_w(at, c + 3 + 4)
                for n in range(4):
                    act.wait_ge(rot, at("four", n + 1))
                    act.activation(b_hi[:, n, :], RT[:, 1 + 2 * (n % 2), :], ACT.Copy).then_inc(rot_hi, 1)

            def head(at, c, t):
                for n in range(3):
                    split_w(at, c + n + 4)
                for n in range(4):
                    wait_tile(act, at, t + n)
                    act.activation(b_hi[:, 4 + n, :], banks[:, (t + n) % 4, :], ACT.Copy).then_inc(vv_hi, 1)
                split_w(at, c + 3 + 4)
                c, t = c + 4, t + 4
                for n in range(3):
                    if n < 2:
                        split_w(at, c + n + 4)
                    wait_tile(act, at, t + n)
                    act.activation(RT[:, n, :], banks[:, (t + n) % 4, :], ACT.Tanh, scale=0.5).then_inc(gg_t, 1)
                for n in range(4):
                    act.wait_ge(pd, at("four", n + 1))
                    act.activation(b_hi[:, 8 + n, :], tmp[:, n % 2, :], ACT.Copy).then_inc(pd_hi, 1)
                split_w(at, c + 2 + 4)
                t += 7
                wait_tile(act, at, t)
                act.activation(RT[:, 3, :], banks[:, t % 4, :], ACT.Tanh, scale=0.5).then_inc(gg_t, 1)

            def group_norm(at, c, early):
                for n in range(4):
                    act.wait_ge(y_cen, at("four", n + 1))
                    if n >= 3:
                        act.wait_ge(y_qs, at("three", n - 2))
                    act.activation(sqsum[:, :] if n == 0 else sq[:, n % 2, :], Y[:, n, :],
                                   ACT.Square).then_inc(y_sq, 1)
                if early:
                    split_w(at, c)
                rsqrt(AUX["ret"] + 1, 4 * P, eps6, y_r, at)
                for n in range(4):
                    act.wait_ge(y_f, at("four", n + 1))
                    act.activation(b_hi[:, 8 + n, :], Y[:, n, :], ACT.Copy, scale=0.5).then_inc(y_hi, 1)
                if not early:
                    split_w(at, c)

            RB = dict(chunk=16, slot=64, tile=28, bank=7, aux=2, four=4, three=3, one=1)
            act.dma_start(DEC, DECAY[0]).then_inc(dec_in, 16)
            keys_queries(flat, CH["ret"], TI["ret"])
            head(flat, CH["ret"] + 4, TI["ret"] + 4)
            c0, t0 = CH["retbody"], TI["retbody"]
            with act.Fori(0, NH - 1) as i:
                at = Head(i, **RB)
                group_norm(at.before(), c0 + 3, True)
                act.dma_start(DEC, DECAY[bass.ds(i + 1, 1), :, :].rearrange("a p n -> (a p) n")).then_inc(dec_in, 16)
                keys_queries(at, c0, t0)
                for n in range(4):
                    split_w(at, c0 + 4 + n + 4)
                head(at, c0 + 8, t0 + 12)
            group_norm(At(NH - 1, **RB), CH["retout"] + 3 - 16 * (NH - 1), False)
            c0, t0 = CH["retout"], TI["retout"]
            order = gemm_order(4, KD)
            for n in range(4):
                if n < 3:
                    split_w(flat, c0 + n + 4)
                residual_squares(6, t0, [m for m in range(KD)
                                         if max(q for q, (k, mm) in enumerate(order) if mm == m) // 8 == n])
            swiglu(1, 7)
            rsqrt(AUX["final"], D, eps6, r_ready)

        @block.vector
        def _(dve):
            linked = [0]

            def link(ins, at=flat):
                linked[0] += 1
                ins.then_inc(link_s, 1)
                dve.wait_ge(link_s, at("link", linked[0]))

            steps = [0]

            def ada(at=flat, k=1):
                for _ in range(k):
                    a = steps[0]
                    steps[0] += 1
                    f = a % KD
                    dve.wait_ge(ada_in[a % ADA_RING], at("adaslot", 16 * (a // ADA_RING + 1)))
                    src = ada_raw[:, a % ADA_RING, :]
                    if f == 0:
                        ins = dve.tensor_scalar(ada_acc[:, :], src, cact[:, 0:1], None, ALU.mult)
                    else:
                        dve.wait_ge(ada_sum, at("ada", a))
                        ins = dve.scalar_tensor_tensor(out=ada_acc[:, :], in0=src, scalar=cact[:, f:f + 1],
                                                       in1=ada_acc[:, :], op0=ALU.mult, op1=ALU.add)
                    ins.then_inc(ada_sum, 1)

            def ada_out(u, g, at=flat):
                dve.wait_ge(aux_ready, at("aux", u + 1))
                if at.i is None:
                    dst, b = mod[:, KD * g:KD * g + KD], col("b_ada", KD * g, KD)
                else:
                    dst = mod[:, bass.ds(at("eight", KD * g), KD)]
                    b = cols[:, bass.ds(at("eight", COL["b_ada"] + KD * g), KD)]
                dve.tensor_tensor(dst, aux[:, 0:KD], b, ALU.add).then_inc(aux_free, 1)

            def add_square(v, m):
                if m in (0, KD - 1):
                    return
                dve.wait_ge(sq_ready, 8 * v + m + 1)
                if m >= 2:
                    dve.wait_ge(sq_added, 6 * v + m - 1)
                dve.tensor_tensor(sqsum[:, :], sqsum[:, :], sq[:, m % 2, :], ALU.add).then_inc(sq_added, 1)

            def gained(name, m, g):
                dve.tensor_scalar(XG[name][:, m, :], X[:, m, :], g(m), None, ALU.mult).then_inc(xg_s, 1)

            def norm_apply(name, a, shift, after=None):
                dve.wait_ge(r_ready, NORMS[name] + 1)
                dve.wait_ge(xg_s, 8 * a + 8)

                def lo(m):
                    dve.wait_ge(h_hi, 8 * a + m + 1)
                    dve.scalar_tensor_tensor(out=a_lo[:, m, :], in0=tmp[:, m % 2, :], scalar=shift(m),
                                             in1=a_hi[:, m, :].bitcast(fp32), op0=ALU.add,
                                             op1=ALU.subtract).then_inc(a_ready, 1)
                    if after:
                        after(m)

                for m in range(KD):
                    if m >= 2:
                        dve.wait_ge(a_ready, 8 * a + m - 1)
                    dve.tensor_tensor(tmp[:, m % 2, :], XG[name][:, m, :], rinv[:, :], ALU.mult).then_inc(h_ready, 1)
                    if m:
                        lo(m - 1)
                lo(KD - 1)

            def gain(a):
                return lambda m: gs[:, KD * a + m:KD * a + m + 1]

            def vector(g):
                return lambda m: mod[:, KD * g + m:KD * g + m + 1]

            def scale_columns(n, gain, g):
                link(dve.scalar_tensor_tensor(out=gs[:, KD * n:KD * n + KD], in0=mod[:, KD * g:KD * g + KD],
                                              scalar=1.0, in1=gain, op0=ALU.add, op1=ALU.mult))

            def residual(at, t, m, g):
                wait_tile(dve, at, t)
                read_out(dve.scalar_tensor_tensor(out=X[:, m, :], in0=banks[:, t % 4, :],
                                                  scalar=mod[:, KD * g + m:KD * g + m + 1], in1=X[:, m, :],
                                                  op0=ALU.mult, op1=ALU.add), t)

            def residuals(t0, ms, g, v, name=None, a=None):
                for m in ms:
                    residual(flat, t0 + m, m, g)
                    if m:
                        add_square(v, m - 1)
                        if name:
                            wait_read(dve, flat, t0 + m - 1)
                            gained(name, m - 1, gain(a))
                    if m == KD - 1 and name:
                        wait_read(dve, flat, t0 + m)
                        gained(name, m, gain(a))

            dve.memset(zero, 0.0)
            dve.memset(eps6, 1e-6)
            dve.memset(eps5, 1e-5)
            dve.memset(ones[:, :], 1.0).then_inc(const, 1)
            dve.wait_ge(cols_in, 16)
            for m in range(KD):
                dve.wait_ge(x_in[m], 16)
                gained("pre", m, lambda m: col("pre", m))
                add_square(0, m)
            norm_apply("pre", 0, lambda m: zero)
            lt = lamt.rearrange("p (a n) -> p a n", a=4)
            lc = col("lam", 0, 256).rearrange("p (a n) -> p a n", a=4)
            link(dve.tensor_tensor(lt[:, 0:2, :], lc[:, 0:2, :], lc[:, 2:4, :], ALU.mult))
            dve.tensor_reduce(lamp, lt[:, 0:2, :], AX.X, ALU.add).then_inc(lam_in, 1)
            dve.wait_ge(lam_e, 1)
            link(dve.tensor_scalar(ctanh, ctanh, 1.0, 0.5, ALU.add, ALU.mult))
            link(dve.tensor_tensor(cact, ctanh, col("c", 0, KD), ALU.mult))
            dve.wait_ge(lam_e, 2)
            link(dve.tensor_tensor(neglam, lamv[:, 1:2], lamv[:, 0:1], ALU.subtract))
            link(dve.tensor_scalar(neglam, neglam, -LAM_INIT, None, ALU.add))
            link(dve.tensor_scalar(gsub, col("subln"), 0.5 * (1.0 - LAM_INIT), None, ALU.mult))
            link(dve.tensor_scalar(gple, col("ple", 0, KD), 0.5, None, ALU.mult))
            link(dve.memset(G[:, 0:2], 0.0))

            dve.wait_ge(dist_in, 16)
            t0 = TI["body"]
            A0 = AUX["body"]

            def softmax_a(at, b):
                n = (b + 1) * P
                dve.wait_ge(sc_ready, at("unit", b + 1))
                for m in range(2):
                    dve.scalar_tensor_tensor(out=SC[:, b % 2, m, 0:n], in0=banks[:, 5 + m, 0:n], scalar=0.125,
                                             in1=bias[:, 3 * P - P * b:S], op0=ALU.mult,
                                             op1=ALU.add).then_inc(sc_read, 1)
                dve.wait_ge(sc_read, at("eight", 2 * b + 2))
                link(dve.tensor_reduce(mx, SC[:, b % 2, :, 0:n], AX.X, ALU.max), at)
                dve.tensor_scalar(nmx, mx, -1.0, None, ALU.mult).then_inc(nm_ready, 1)

            def softmax_b(at, b):
                n = (b + 1) * P
                dve.wait_ge(ex_ready, at("eight", 2 * b + 2))
                link(dve.reciprocal(rrec, rsum), at)
                link(dve.tensor_scalar(c1[:, 0:1], rrec[:, 1:2], neglam, None, ALU.mult), at)
                if b >= 2:
                    dve.wait_ge(aux_ready, at("aux", A0 + 1 + b - 2 + 1))
                link(dve.tensor_scalar(WT[:, b % 2, 0:n], SC[:, b % 2, 0, 0:n], rrec[:, 0:1], None, ALU.mult), at)
                dve.scalar_tensor_tensor(out=WT[:, b % 2, 0:n], in0=SC[:, b % 2, 1, 0:n], scalar=c1[:, 0:1],
                                         in1=WT[:, b % 2, 0:n], op0=ALU.mult, op1=ALU.add).then_inc(w_ready, 1)

            def weights_lo(at, b):
                n = (b + 1) * P
                dve.wait_ge(wt_hi, at("unit", b + 1))
                dve.tensor_tensor(b_lo[:, 9 + b % 2, 0:n], aux[:, 0:n], b_hi[:, 9 + b % 2, 0:n].bitcast(fp32),
                                  ALU.subtract).then_inc(aux_free, 1)

            base = linked[0]
            per_link = 1 + 4 * 4 + 4 + 1
            with dve.Fori(0, NH) as i:
                at = At(i, chunk=8, tile=8, bank=2, aux=7, unit=4, one=1, two=2, eight=8, link=per_link,
                        ada=8, adaslot=64)
                link(dve.tensor_scalar(bias, dist, cols[:, bass.ds(i + COL["slope"], 1)], None, ALU.mult), at)
                ada(at, 2)
                softmax_a(at, 0)
                ada(at, 1)
                softmax_b(at, 0)
                wait_tile(dve, at, t0 + 3)
                dve.wait_ge(za_t, at("one", 1))
                read_out(dve.scalar_tensor_tensor(out=ZA, in0=tmp[:, 1, :], scalar=1.0, in1=banks[:, 3, :],
                                                  op0=ALU.add, op1=ALU.mult), 3)
                softmax_a(at, 1)
                dve.wait_ge(v_hi, at("one", 1))
                dve.tensor_tensor(b_lo[:, 8, :], aux, b_hi[:, 8, :].bitcast(fp32), ALU.subtract).then_inc(aux_free, 1)
                softmax_b(at, 1)
                softmax_a(at, 2)
                weights_lo(at, 0)
                softmax_b(at, 2)
                softmax_a(at, 3)
                weights_lo(at, 1)
                softmax_b(at, 3)
                wait_tile(dve, at, t0 + 6)
                wait_read(dve, at, t0 + 5)
                read_out(dve.tensor_tensor(G[:, 2:2 + S], banks[:, 2, :], CG, ALU.mult), t0 + 6)
                wait_read(dve, at, t0 + 6)
                tap = [cols[:, bass.ds(i * 3 + (COL["conv"] + j), 1)] for j in range(3)]
                link(dve.tensor_scalar(tmp[:, 0, :], G[:, 0:S], tap[0], None, ALU.mult), at)
                for j in (1, 2):
                    link(dve.scalar_tensor_tensor(out=tmp[:, 0, :], in0=G[:, j:j + S], scalar=tap[j],
                                                  in1=tmp[:, 0, :], op0=ALU.mult, op1=ALU.add), at)
                wait_read(dve, at, t0 + 4)
                link(dve.tensor_tensor(tmp[:, 0, :], tmp[:, 0, :], VB, ALU.mult), at)
                weights_lo(at, 2)
                ada(at, 1)
                weights_lo(at, 3)
                ada(at, 2)
                dve.wait_ge(zc_t, at("one", 1))
                read_out(dve.scalar_tensor_tensor(out=sq[:, 1, :], in0=tmp[:, 1, :], scalar=1.0, in1=banks[:, 3, :],
                                                  op0=ALU.add, op1=ALU.mult), t0 + 7)
                wait_read(dve, at, t0 + 7)
                dve.tensor_tensor(tmp[:, 0, :], tmp[:, 0, :], sq[:, 1, :], ALU.mult).then_inc(cv_out, 1)
                dve.wait_ge(mix_hi, at("two", 1))
                dve.wait_ge(cv_out, at("one", 1))
                dve.scalar_tensor_tensor(out=b_lo[:, bass.ds(i + 4, 1), :].rearrange("p a s -> p (a s)"),
                                         in0=tmp[:, 0, :], scalar=0.5,
                                         in1=b_hi[:, bass.ds(i + 4, 1), :].rearrange("p a s -> p (a s)").bitcast(fp32),
                                         op0=ALU.mult, op1=ALU.subtract).then_inc(mix_ready, 1)
                ada(at, 2)
                dve.wait_ge(o_r, at("one", 1))
                dve.wait_ge(o_copied, at("one", 1))
                dve.wait_ge(mix_ready, at("two", 1))
                link(dve.tensor_tensor(tmp[:, 0, :], sq[:, 0, :], rinv[:, :], ALU.mult), at)
                dve.scalar_tensor_tensor(out=tmp[:, 0, :], in0=tmp[:, 0, :], scalar=gsub, in1=ZA,
                                         op0=ALU.mult, op1=ALU.mult).then_inc(o_out, 1)
                dve.wait_ge(mix_hi, at("two", 2))
                dve.wait_ge(o_out, at("one", 1))
                dve.tensor_tensor(b_lo[:, bass.ds(i, 1), :].rearrange("p a s -> p (a s)"), tmp[:, 0, :],
                                  b_hi[:, bass.ds(i, 1), :].rearrange("p a s -> p (a s)").bitcast(fp32),
                                  ALU.subtract).then_inc(mix_ready, 1)
                ada_out(A0 + 6, 0, at)
            got = linked[0] - base
            assert got == per_link, got
            linked[0] = base + per_link * NH
            steps[0] = 8 * NH

            dve.wait_ge(p_hi, 1)
            dve.tensor_tensor(b_lo[:, 8:10, :].rearrange("p k s -> p (k s)"), PV,
                              b_hi[:, 8:10, :].rearrange("p k s -> p (k s)").bitcast(fp32),
                              ALU.subtract).then_inc(p_ready, 1)
            t0 = TI["out"]
            for n in range(8):
                ada()
                if n >= 3:
                    for m in ((0, 1, 2, 3) if n == 3 else (n,)):
                        dve.wait_ge(sq_ready, 8 + m + 1)
                        read_out(dve.tensor_copy(MIX[:, m, :], banks[:, m % 4, :]), t0 + m)
                        add_square(1, m)
            t1 = TI["ple"]

            def xg_lo(m):
                dve.wait_ge(xg_hi, m + 1)
                dve.tensor_tensor(a_lo[:, m, :], X[:, m, :], a_hi[:, m, :].bitcast(fp32),
                                  ALU.subtract).then_inc(xg_ready, 1)

            dve.wait_ge(r_ready, 2)
            for m in range(KD):
                if m == 0:
                    for b in range(4):
                        wait_read(dve, flat, t0 + 4 + b)
                link(dve.tensor_tensor(tmp[:, m % 2, :], MIX[:, m, :], rinv[:, :], ALU.mult))
                dve.scalar_tensor_tensor(out=X[:, m, :], in0=tmp[:, m % 2, :], scalar=col("post", m), in1=X[:, m, :],
                                         op0=ALU.mult, op1=ALU.add).then_inc(x_new, 1)
                dve.wait_ge(sq_ready, 16 + m + 1)
                add_square(2, m)
                dve.wait_ge(x_new, m + 1)
                if m >= 3:
                    xg_lo(m - 3)
                if m == 2:
                    ada_out(AUX["ada4"], 4)
            for m in range(KD - 3, KD):
                xg_lo(m)
            t0 = TI["gate"]
            dve.wait_ge(r_ready, 3)
            dve.wait_ge(aux_free, AUX["body"] + 7 * NH)
            scale_columns(1, col("mix", 0, KD), 1)
            for m in range(4, KD):
                wait_read(dve, flat, t1 + m)
            for m in range(KD):
                dve.scalar_tensor_tensor(out=E[:, m, :], in0=E[:, m, :], scalar=gple[:, m:m + 1], in1=rinv[:, :],
                                         op0=ALU.mult, op1=ALU.mult).then_inc(e_ready, 1)
            for n in range(8):
                ada()
                if n >= 3:
                    for m in ((0, 1, 2, 3) if n == 3 else (n,)):
                        wait_read(dve, flat, t0 + m)
                        dve.wait_ge(e_ready, m + 1)
                        link(dve.scalar_tensor_tensor(out=E[:, m, :], in0=GT[m % 4], scalar=1.0,
                                                      in1=E[:, m, :], op0=ALU.add, op1=ALU.mult))
                        dve.tensor_tensor(X[:, m, :], X[:, m, :], E[:, m, :], ALU.add).then_inc(x_new, 1)
                        if m:
                            add_square(3, m - 1)
                            gained("four", m - 1, gain(1))
            dve.wait_ge(x_new, 2 * KD)
            gained("four", 7, gain(1))

            td = TI["dft1"]

            def z_group(g):
                for z in range(4 * g, 4 * g + 4):
                    dve.wait_ge(z_hi, z + 1)
                    hi, lo = (b_hi[:, z, :], b_lo[:, z, :]) if z < 12 else (a_hi[:, z - 12, :], a_lo[:, z - 12, :])
                    read_out(dve.tensor_tensor(lo, banks[:, (td + z) % 4, :], hi.bitcast(fp32), ALU.subtract), td + z)

            norm_apply("four", 1, vector(0), lambda m: z_group((m - 3) // 2) if m in (3, 5, 7) else None)
            ada_out(AUX["ada5"], 5)
            z_group(3)
            t0 = TI["dft2"]
            for m in range(KD):
                ada()
                dve.wait_ge(f_hi, m + 1)
                hi, lo = (a_hi[:, 4 + m, :], a_lo[:, 4 + m, :]) if m < 4 else (b_hi[:, m - 4, :], b_lo[:, m - 4, :])
                read_out(dve.tensor_tensor(lo, banks[:, (t0 + m) % 4, :], hi.bitcast(fp32), ALU.subtract), t0 + m)
            ada_out(AUX["ada6"], 6)
            t0 = TI["fout"]
            for n in range(8):
                ada()
                if n >= 3:
                    if n == 3:
                        dve.wait_ge(aux_free, AUX["ada5"] + 1)
                        scale_columns(2, col("ffn", 0, KD), 4)
                    residuals(t0, (0, 1, 2, 3) if n == 3 else (n,), 2, 4, "ffn0", 2)

            def up_body(at, t, j):
                for n in range(2):
                    dve.wait_ge(hid_t, at("hid", j + n + 1))
                    g, u = (t + 2 * n) % 4, (t + 2 * n + 1) % 4
                    read_out(dve.scalar_tensor_tensor(out=SG[:, n, :], in0=T2[:, n, :], scalar=1.0,
                                                      in1=banks[:, g, :], op0=ALU.add, op1=ALU.mult), g)
                    wait_tile(dve, at, t + 2 * n + 1)
                    wait_read(dve, at, t + 2 * n)
                    dve.tensor_tensor(HD[:, n, :], SG[:, n, :], banks[:, u, :], ALU.mult).then_inc(hid_f, 1)
                    dve.wait_ge(hid_hi, at("hid", j + n + 1))
                    k = j % FT % HALF[0] + n
                    if at.i is None:
                        hi, lo = b_hi[:, k, :], b_lo[:, k, :]
                    else:
                        hi, lo = (b[:, bass.ds(at("hid", k), 1), :].rearrange("p a s -> p (a s)") for b in (b_hi, b_lo))
                    read_out(dve.scalar_tensor_tensor(out=lo, in0=HD[:, n, :], scalar=0.5, in1=hi.bitcast(fp32),
                                                      op0=ALU.mult, op1=ALU.subtract), u)

            def swiglu(layer, v, a_in, with_ada):
                g0 = 6 * layer
                norm_apply(f"ffn{layer}", a_in, vector(g0 + 3))
                for part, n_hid in zip("ab", HALF):
                    t = TI[f"up{layer}{part}"]
                    j = layer * FT + (0 if part == "a" else HALF[0])
                    first = 1 if part == "a" else 0
                    if first:
                        if with_ada:
                            ada_out(AUX["ada7"], 7)
                        up_body(flat, t, j)
                        if with_ada:
                            ada(flat, 8)
                    with dve.Fori(0, n_hid // 2 - first) as i:
                        at = At(i, tile=4, bank=1, hid=2, ada=8, adaslot=64, aux=1, eight=8)
                        up_body(at, t + 4 * first, j + 2 * first)
                        if first and with_ada:
                            ada_out(AUX["ada"], 8, at)
                            ada(at, 8)
                    if first and with_ada:
                        ada_out(AUX["ada"] + 5, 13)
                    t = TI[f"down{layer}{part}"]
                    if part == "a":
                        for m in range(KD):
                            residual(flat, t + m, m, g0 + 5)
                    elif layer == 0:
                        dve.wait_ge(aux_free, AUX["ada"] + 6)
                        scale_columns(3, col("mix", KD, KD), 7)
                        residuals(t, range(KD), g0 + 5, v, "rnorm", 3)
                    else:
                        residuals(t, range(KD), g0 + 5, v)

            swiglu(0, 5, 2, True)

            norm_apply("rnorm", 3, vector(6))
            dve.wait_ge(rope_in, 16)

            def rotate(at, t):
                def rot_lo(n):
                    dve.wait_ge(rot_hi, at("four", n + 1))
                    dve.tensor_tensor(b_lo[:, n, :], RT[:, 1 + 2 * (n % 2), :], b_hi[:, n, :].bitcast(fp32),
                                      ALU.subtract).then_inc(rot_ready, 1)

                for n in range(2):
                    x1, x2 = KQ[:, 2 * n, :], KQ[:, 2 * n + 1, :]
                    wait_read(dve, at, t + 2 * n)
                    wait_read(dve, at, t + 2 * n + 1)
                    if n:
                        rot_lo(0)
                    dve.tensor_tensor(RT[:, 0, :], x1, COS, ALU.mult)
                    if n:
                        dve.wait_ge(rot_ready, at("four", 1))
                    link(dve.tensor_tensor(RT[:, 1, :], x2, SIN, ALU.mult), at)
                    dve.tensor_tensor(RT[:, 1, :], RT[:, 0, :], RT[:, 1, :], ALU.subtract).then_inc(rot, 1)
                    if n:
                        rot_lo(1)
                    dve.tensor_tensor(RT[:, 2, :], x1, SIN, ALU.mult)
                    if n:
                        dve.wait_ge(rot_ready, at("four", 2))
                    link(dve.tensor_tensor(RT[:, 3, :], x2, COS, ALU.mult), at)
                    dve.tensor_tensor(RT[:, 3, :], RT[:, 2, :], RT[:, 3, :], ALU.add).then_inc(rot, 1)
                rot_lo(2)
                rot_lo(3)

            def gate(at, n, tt):
                dve.wait_ge(gg_t, at("four", n + 1))
                read_out(dve.scalar_tensor_tensor(out=GG[:, n, :], in0=RT[:, n, :], scalar=1.0,
                                                  in1=banks[:, tt % 4, :], op0=ALU.add, op1=ALU.mult), tt)

            def head(at, t):
                for n in range(4):
                    dve.wait_ge(vv_hi, at("four", n + 1))
                    read_out(dve.tensor_tensor(b_lo[:, 4 + n, :], banks[:, (t + n) % 4, :],
                                               b_hi[:, 4 + n, :].bitcast(fp32), ALU.subtract), t + n)
                t += 4
                for n in range(3):
                    gate(at, n, t + n)
                t += 3
                dve.wait_ge(dec_in, at("sixteen", 16))

                def score_lo(n):
                    dve.wait_ge(pd_hi, at("four", n + 1))
                    read_out(dve.tensor_tensor(b_lo[:, 8 + n, :], tmp[:, n % 2, :], b_hi[:, 8 + n, :].bitcast(fp32),
                                               ALU.subtract), t + n)

                for n in range(4):
                    wait_tile(dve, at, t + n)
                    if n >= 2:
                        wait_read(dve, at, t + n - 2)
                    dve.tensor_tensor(tmp[:, n % 2, :], banks[:, (t + n) % 4, :], DEC[:, 3 * P - P * n:3 * P - P * n + S],
                                      ALU.mult).then_inc(pd, 1)
                    if n:
                        dve.wait_ge(pd, at("four", n))
                        score_lo(n - 1)
                dve.wait_ge(pd, at("four", 4))
                score_lo(3)
                gate(at, 3, t + 4)

            def group_norm(at, t):
                for n in range(4):
                    wait_tile(dve, at, t + n)
                    read_out(dve.tensor_copy(Y[:, n, :], banks[:, (t + n) % 4, :]), t + n)
                    wait_read(dve, at, t + n)
                    if n == 1:
                        link(dve.tensor_tensor(sqsum[:, :], Y[:, 0, :], Y[:, 1, :], ALU.add), at)
                    elif n == 2:
                        link(dve.tensor_tensor(sqsum[:, :], sqsum[:, :], Y[:, 2, :], ALU.add), at)
                    elif n == 3:
                        dve.tensor_tensor(sqsum[:, :], sqsum[:, :], Y[:, 3, :], ALU.add).then_inc(y_sum, 1)
                dve.wait_ge(aux_ready, at("aux", AUX["ret"] + 1))
                dve.tensor_scalar(rinv[:, :], aux, 1.0 / (4 * P), None, ALU.mult).then_inc(aux_free, 1)
                dve.wait_ge(aux_free, at("aux", AUX["ret"] + 1))
                for n in range(4):
                    dve.tensor_tensor(Y[:, n, :], Y[:, n, :], rinv[:, :], ALU.subtract).then_inc(y_cen, 1)
                for n in range(1, 4):
                    dve.wait_ge(y_sq, at("four", n + 1))
                    if n >= 2:
                        dve.wait_ge(y_qs, at("three", n - 1))
                    dve.tensor_tensor(sqsum[:, :], sqsum[:, :], sq[:, n % 2, :], ALU.add).then_inc(y_qs, 1)
                for q in (t - 8, t - 7, t - 6, t - 1):
                    wait_read(dve, at, q)
                for n in range(4):
                    dve.wait_ge(y_cen, at("four", n + 1))
                    link(dve.tensor_tensor(GG[:, n, :], GG[:, n, :], Y[:, n, :], ALU.mult), at)
                dve.wait_ge(y_r, at("one", 1))
                for n in range(4):
                    dve.tensor_tensor(Y[:, n, :], GG[:, n, :], rinv[:, :], ALU.mult).then_inc(y_f, 1)
                for n in range(4):
                    dve.wait_ge(y_hi, at("four", n + 1))
                    dve.scalar_tensor_tensor(out=b_lo[:, 8 + n, :], in0=Y[:, n, :], scalar=0.5,
                                             in1=b_hi[:, 8 + n, :].bitcast(fp32), op0=ALU.mult,
                                             op1=ALU.subtract).then_inc(y_ready, 1)

            PER = dict(tile=28, bank=7, aux=2, four=4, three=3, one=1, sixteen=16)
            first, t0 = TI["ret"], TI["retbody"]
            rotate(flat, first)
            head(flat, first + 4)
            per_link = 2 + 4 + 4
            base = linked[0]
            with dve.Fori(0, NH - 1) as i:
                at = Head(i, link=per_link, **PER)
                group_norm(At(i, link=per_link, **PER), t0 - 4)
                rotate(at, t0)
                for m in range(KD):
                    residual(at, t0 + 4 + m, m, 8)
                head(at, t0 + 12)
            assert linked[0] - base == per_link, linked[0] - base
            linked[0] = base + per_link * (NH - 1)
            group_norm(At(NH - 1, link=0, **PER), t0 - 4)
            t0 = TI["retout"]
            scale_columns(4, col("ffn", KD, KD), 10)
            residuals(t0, range(KD), 8, 6, "ffn1", 4)
            swiglu(1, 7, 4, False)
            link(dve.scalar_tensor_tensor(out=gs[:, 0:KD], in0=mod[:, 13 * KD:14 * KD], scalar=1.0,
                                          in1=col("final", 0, KD), op0=ALU.add, op1=ALU.mult))
            dve.wait_ge(r_ready, 8)
            for m in range(KD):
                link(dve.tensor_tensor(tmp[:, m % 2, :], X[:, m, :], rinv[:, :], ALU.mult))
                dve.tensor_scalar(X[:, m, :], tmp[:, m % 2, :], gs[:, m:m + 1], mod[:, 12 * KD + m:12 * KD + m + 1],
                                  ALU.mult, ALU.add).then_inc(x_done, 1)

        @block.tensor
        def _(pe):
            pos = [0, 0]

            def chunk_begins(at, width):
                c, q = pos
                slot = c % RING
                begins = q == 0
                if begins:
                    pe.wait_ge(wlo, at("chunk", c + 1))
                ap = slice(q * P, q * P + width)
                pos[1] += width // P
                if pos[1] == 8:
                    pos[0], pos[1] = c + 1, 0
                return begins and c > 0, w_hi[:, slot, ap], w_lo[:, slot, ap]

            def mul(at, bank, x_hi, x_lo, first, last, done=False):
                begins, hi, lo = chunk_begins(at, P)
                out = banks[:, bank, :]
                mm = pe.matmul(out, lo, x_hi, start=first, stop=False)
                if begins:
                    mm.then_inc(w_used, 1)
                pe.matmul(out, hi, x_lo, start=False, stop=False)
                mm = pe.matmul(out, hi, x_hi, start=False, stop=last)
                if done:
                    mm.then_inc(tile_ready, 1)

            def wait_bank(at, t):
                if t >= 4:
                    pe.wait_ge(bank_read[t % 4], at("bank", t // 4))

            def gemm(at, t0, M, ks, rhs, ready=None, first_outer=True, hook=None):
                seen, opened = set(), set()
                order = gemm_order(len(ks), M, ks, first_outer)
                n_of = {}
                for n, (k, m) in enumerate(order):
                    if ready and k not in seen:
                        seen.add(k)
                        ready(k)
                    if m not in opened:
                        opened.add(m)
                        wait_bank(at, t0 + m)
                        n_of[m] = 0
                    hi, lo = rhs(k)
                    n_of[m] += 1
                    mul(at, (t0 + m) % 4, hi, lo, n_of[m] == 1, n_of[m] == len(ks), n_of[m] == len(ks))
                    if hook:
                        hook(n)

            def rhs_a(k):
                return a_hi[:, k, :], a_lo[:, k, :]

            def rhs_b(k):
                return b_hi[:, k, :], b_lo[:, k, :]

            def stats(at, u):
                if u > 0:
                    pe.wait_ge(aux_free, at("aux", u))
                pe.matmul(aux, ones[:, :], sqsum[:, :], start=True, stop=True).then_inc(aux_ready, 1)

            def norm_stats(v, name):
                pe.wait_ge(sq_added, 6 * v + 6)
                if AUX[name] > 0:
                    pe.wait_ge(aux_free, AUX[name])
                pe.matmul(aux, ones[:, :], sqsum[:, :], start=True, stop=False)
                pe.wait_ge(sq_ready, 8 * v + 8)
                pe.matmul(aux, ones[:, :], sq[:, 1, :], start=False, stop=True).then_inc(aux_ready, 1)

            def ada_reduce(at, u, g):
                pe.wait_ge(ada_sum, at("ada", KD * (g + 1)))
                pe.wait_ge(aux_free, at("aux", u))
                for f in range(KD):
                    mm = pe.matmul(aux[:, f:f + 1], ada_acc[:, f * P:(f + 1) * P], ones[:, 0:1], start=True, stop=True)
                mm.then_inc(aux_ready, 1)

            pe.wait_ge(const, 1)
            norm_stats(0, "pre")
            A0, t0 = AUX["body"], TI["body"]

            def scores(at, b):
                n = (b + 1) * P
                if b == 0:
                    wait_read(pe, at, t0)
                    wait_read(pe, at, t0 + 1)
                else:
                    pe.wait_ge(sc_read, at("eight", 2 * b))
                for m in range(2):
                    p = slice(64 * m, 64 * m + 64)
                    mm = pe.matmul(banks[:, 5 + m, 0:n], Q[p, b * P:(b + 1) * P], K[p, 0:n], start=True, stop=True)
                mm.then_inc(sc_ready, 1)

            def transpose_v(at):
                wait_read(pe, at, t0 + 2)
                pe.wait_ge(aux_free, at("aux", A0))
                for s in range(TB):
                    mm = pe.transpose(aux[:, s * P:(s + 1) * P], VB[:, s * P:(s + 1) * P], ident)
                mm.then_inc(aux_ready, 1)

            def transpose_w(at, b):
                pe.wait_ge(w_ready, at("unit", b + 1))
                pe.wait_ge(aux_free, at("aux", A0 + 1 + b))
                for s in range(b + 1):
                    mm = pe.transpose(aux[:, s * P:(s + 1) * P], WT[:, b % 2, s * P:(s + 1) * P], ident)
                mm.then_inc(aux_ready, 1)

            def values(at, b):
                pe.wait_ge(aux_free, at("aux", A0 + 2 + b))
                out = banks[:, 4, b * P:(b + 1) * P]
                for s in range(b + 1):
                    c = slice(s * P, (s + 1) * P)
                    v1, v2 = b_hi[:, 8, c], b_lo[:, 8, c]
                    w1, w2 = b_hi[:, 9 + b % 2, c], b_lo[:, 9 + b % 2, c]
                    pe.matmul(out, v2, w1, start=(s == 0), stop=False)
                    pe.matmul(out, v1, w2, start=False, stop=False)
                    mm = pe.matmul(out, v1, w1, start=False, stop=(s == b))
                if b == TB - 1:
                    mm.then_inc(pv_ready, 1)

            pe.wait_ge(cols_in, 16)

            def body_head(at, n, hook=None):
                gemm(at, t0 + n, 1, range(KD), rhs_a, None, False, hook)

            def body_rest(at):
                scores(at, 1)
                transpose_v(at)
                gemm(at, t0 + 4, 1, range(KD), rhs_a, None, False)
                scores(at, 2)
                transpose_w(at, 0)
                gemm(at, t0 + 5, 1, range(KD), rhs_a, None, False)
                scores(at, 3)
                transpose_w(at, 1)
                values(at, 0)
                gemm(at, t0 + 6, 1, range(KD), rhs_a, None, False)
                transpose_w(at, 2)
                values(at, 1)

                def middle(n):
                    if n == 3:
                        transpose_w(at, 3)
                        values(at, 2)
                gemm(at, t0 + 7, 1, range(KD), rhs_a, None, False, middle)
                values(at, 3)

            def body_tail(at, n):
                if n == 3:
                    pe.wait_ge(o_sq, at("one", 1))
                    stats(at, A0 + 5)
                if n == 7:
                    ada_reduce(at, A0 + 6, 0)

            per = dict(chunk=8, tile=8, bank=2, aux=7, unit=4, one=1, two=2, eight=8, ada=8)
            gemm(flat, t0, 4, range(KD), rhs_a, lambda k: pe.wait_ge(a_ready, k + 1))
            scores(flat, 0)
            with pe.Fori(0, NH - 1) as i:
                at = At(i, **per)
                body_rest(at)
                for n in range(8, 12):
                    body_head(at, n, (lambda q: body_tail(at, q)) if n == 8 else None)
                    if n == 10:
                        nxt = At(i, **per)
                        for q in (8, 9):
                            wait_read(pe, nxt, t0 + q)
                        for m in range(2):
                            p = slice(64 * m, 64 * m + 64)
                            mm = pe.matmul(banks[:, 5 + m, 0:P], Q[p, 0:P], K[p, 0:P], start=True, stop=True)
                        mm.then_inc(sc_ready, 1)
            last = At(NH - 1, **per)
            pos[0] = CH["body"] + 4
            body_rest(last)
            pos[0] = CH["out"]

            def mix_wait(k):
                pe.wait_ge(mix_ready, 8 if k == 3 else 7)
            gemm(flat, TI["out"], KD, ATT_KS, rhs_b, mix_wait, hook=lambda n: body_tail(last, n))
            pe.wait_ge(p_ready, 1)

            def gemm_e(t0):
                for m in range(KD):
                    wait_bank(flat, t0 + m)
                    for k in range(2):
                        mul(flat, (t0 + m) % 4, b_hi[:, 8 + k, :], b_lo[:, 8 + k, :], k == 0, k == 1, k == 1)
                    if m == 1:
                        norm_stats(1, "post")
                    if m == 3:
                        ada_reduce(flat, AUX["ada4"], 4)
            gemm_e(TI["ple"])
            def gate_wait(k):
                pe.wait_ge(xg_ready, k + 1)

            def gate_hook(n):
                if n == 15:
                    norm_stats(2, "ple")
            gemm(flat, TI["gate"], KD, range(KD), rhs_a, gate_wait, True, gate_hook)
            norm_stats(3, "four")
            ada_reduce(flat, AUX["ada5"], 5)
            t0 = TI["dft1"]
            slot = CH["dft1"] % RING
            for g in range(NH):
                pe.wait_ge(a_ready, KD + 2 * g + 2)
                for tt in range(TB):
                    t = t0 + g * 4 + tt
                    wait_bank(flat, t)
                    for k in range(2):
                        if g == 0 and tt == 0 and k == 0:
                            pe.wait_ge(wlo, CH["dft1"] + 1)
                        xh, xl = (a[:, 2 * g + k, tt * P:(tt + 1) * P] for a in (a_hi, a_lo))
                        wh, wl = (w[:, slot, k * S:(k + 1) * S] for w in (w_hi, w_lo))
                        out = banks[:, t % 4, :]
                        mm = pe.matmul(out, xh, wl, start=(k == 0), stop=False)
                        if g == 0 and tt == 0 and k == 0:
                            mm.then_inc(w_used, 1)
                        pe.matmul(out, xl, wh, start=False, stop=False)
                        mm = pe.matmul(out, xh, wh, start=False, stop=(k == 1))
                    mm.then_inc(tile_ready, 1)
            t1 = TI["dft2"]
            c0 = CH["dft2"]
            for b in range(4):
                wait_bank(flat, t1 + b)
            begun = set()
            for m in range(KD):
                t = t1 + m
                wait_bank(flat, t)
                g, half = divmod(m, 2)
                for n in range(8):
                    part, tt = divmod(n, 4)
                    c = c0 + n // 2
                    z = g * 4 + tt
                    Zh, Zl = (b_hi[:, z, :], b_lo[:, z, :]) if z < 12 else (a_hi[:, z - 12, :], a_lo[:, z - 12, :])
                    lc = slice(part * 256 + half * P, part * 256 + half * P + P)
                    wc = slice((n % 2) * S, (n % 2 + 1) * S)
                    wh, wl = w_hi[:, c % RING, wc], w_lo[:, c % RING, wc]
                    new = c not in begun
                    if new:
                        begun.add(c)
                        pe.wait_ge(wlo, c + 1)
                    out = banks[:, t % 4, :]
                    mm = pe.matmul(out, Zh[:, lc], wl, start=(n == 0), stop=False)
                    if c == c0 and new:
                        mm.then_inc(w_used, 1)
                    elif m == KD - 1 and n in (2, 4, 6):
                        mm.then_inc(w_used, 1)
                    pe.matmul(out, Zl[:, lc], wh, start=False, stop=False)
                    mm = pe.matmul(out, Zh[:, lc], wh, start=False, stop=(n == 7))
                mm.then_inc(tile_ready, 1)
            pos[0] = CH["fout"]

            def f_rhs(k):
                return (a_hi[:, 4 + k, :], a_lo[:, 4 + k, :]) if k < 4 else (b_hi[:, k - 4, :], b_lo[:, k - 4, :])
            gemm(flat, TI["fout"], KD, range(KD), f_rhs, lambda k: wait_read(pe, flat, t1 + k),
                 hook=lambda n: ada_reduce(flat, AUX["ada6"], 6) if n == 7 else None)
            norm_stats(4, "ffn0")

            def swiglu(layer, a_in, with_ada):
                for part, n_hid in zip("ab", HALF):
                    c, t = CH[f"up{layer}{part}"], TI[f"up{layer}{part}"]
                    assert pos[0] == c
                    first = 1 if part == "a" else 0
                    if first:
                        gemm(flat, t, 4, range(KD), rhs_a, lambda k: pe.wait_ge(a_ready, KD * a_in + k + 1),
                             hook=lambda n: ada_reduce(flat, AUX["ada7"], 7) if n == 15 and with_ada else None)
                    with pe.Fori(0, n_hid // 2 - first) as i:
                        at = At(i, chunk=4, tile=4, bank=1, ada=8, aux=1)
                        gemm(at, t + 4 * first, 4, range(KD), rhs_a, None, False)
                        if first and with_ada:
                            ada_reduce(at, AUX["ada"], 8)
                    pos[0] = CH[f"down{layer}{part}"]
                    base_t = TI[f"down{layer}{part}"]
                    def last_ada(n):
                        if n == 39:
                            ada_reduce(flat, AUX["ada"] + 5, 13)
                    gemm(flat, base_t, KD, range(n_hid), rhs_b, lambda k: wait_read(pe, flat, t + 2 * k + 1),
                         hook=last_ada if first and with_ada else None)

            swiglu(0, 2, True)
            norm_stats(5, "rnorm")

            def token_major(at, t0):
                for k in range(KD):
                    for tt in range(TB):
                        if k == 0:
                            wait_bank(at, t0 + tt)
                        if tt == 0:
                            begins, wh, wl = chunk_begins(at, S)
                        c = slice(tt * P, (tt + 1) * P)
                        out = banks[:, (t0 + tt) % 4, :]
                        mm = pe.matmul(out, a_hi[:, k, c], wl, start=(k == 0), stop=False)
                        if begins and tt == 0:
                            mm.then_inc(w_used, 1)
                        pe.matmul(out, a_lo[:, k, c], wh, start=False, stop=False)
                        mm = pe.matmul(out, a_hi[:, k, c], wh, start=False, stop=(k == KD - 1))
                        if k == KD - 1:
                            mm.then_inc(tile_ready, 1)

            def group_stats(at, n):
                if n == 0:
                    pe.wait_ge(y_sum, at("one", 1))
                else:
                    pe.wait_ge(y_qs, at("three", 3))
                stats(at, AUX["ret"] + n)

            def head(at, t):
                token_major(at, t)
                tv = t
                t += 4
                for n in range(3):
                    gemm(at, t + n, 1, range(KD), rhs_a, None, False)
                t += 3
                for s in range(TB):
                    wait_bank(at, t + s)
                    if s == 0:
                        pe.wait_ge(rot_ready, at("four", 4))
                    out = banks[:, (t + s) % 4, :]
                    for d in range(2):
                        c = slice(s * P, (s + 1) * P)
                        pe.matmul(out, b_lo[:, d, c], b_hi[:, 2 + d, :], start=(d == 0), stop=False)
                        pe.matmul(out, b_hi[:, d, c], b_lo[:, 2 + d, :], start=False, stop=False)
                        mm = pe.matmul(out, b_hi[:, d, c], b_hi[:, 2 + d, :], start=False, stop=(d == 1))
                    mm.then_inc(tile_ready, 1)
                ts = t
                t += 4
                gemm(at, t, 1, range(KD), rhs_a, None, False)
                t += 1
                for s in range(TB):
                    wait_read(pe, at, tv + s)
                for n in range(4):
                    wait_bank(at, t + n)
                    out = banks[:, (t + n) % 4, :]
                    for s in range(TB):
                        if n == 0:
                            wait_read(pe, at, ts + s)
                        c = slice(n * P, (n + 1) * P)
                        pe.matmul(out, b_lo[:, 4 + s, c], b_hi[:, 8 + s, :], start=(s == 0), stop=False)
                        pe.matmul(out, b_hi[:, 4 + s, c], b_lo[:, 8 + s, :], start=False, stop=False)
                        mm = pe.matmul(out, b_hi[:, 4 + s, c], b_hi[:, 8 + s, :], start=False, stop=(s == 3))
                    mm.then_inc(tile_ready, 1)

            gemm(flat, TI["ret"], 4, range(KD), rhs_a, lambda k: pe.wait_ge(a_ready, 3 * KD + k + 1))
            head(flat, TI["ret"] + 4)
            PER = dict(chunk=16, tile=28, bank=7, aux=2, four=4, three=3, one=1)
            t0 = TI["retbody"]
            with pe.Fori(0, NH - 1) as i:
                at, prev = Head(i, **PER), At(i, **PER)
                gemm(at, t0, 4, range(KD), rhs_a,
                     hook=lambda n: group_stats(prev, (5, 13).index(n)) if n in (5, 13) else None)
                gemm(at, t0 + 4, KD, range(4), lambda k: rhs_b(8 + k),
                     lambda k: pe.wait_ge(y_ready, prev("four", k + 1)))
                head(at, t0 + 12)
            for n in range(2):
                group_stats(At(NH - 1, **PER), n)
            pos[0] = CH["retout"]
            gemm(flat, TI["retout"], KD, range(4), lambda k: rhs_b(8 + k),
                 lambda k: pe.wait_ge(y_ready, 4 * (NH - 1) + k + 1))
            norm_stats(6, "ffn1")
            swiglu(1, 4, False)
            norm_stats(7, "final")


def weight_stream(w_in, w_out, w_ple_proj, w_ple_gate, w_fourier_out, w_ret_in, w_ret_out, w_ffn_in, w_ffn_out, dfts):
    import numpy as np
    tiles = []

    def tile(w, k, c):
        tiles.append(w[k * P:(k + 1) * P, c:c + P])

    def gemm(w, K, M, ks=None, first_outer=True, k0=0, cols=None):
        for k, m in gemm_order(K, M, ks, first_outer):
            tile(w, k0 + k, cols[m] if cols else m * P)

    for j in range(NH):
        gemm(w_in, KD, 8, None, j == 0, 0, [part * 512 + j * P for part in range(8)])
    gemm(w_out, KD, KD, ATT_KS)
    gemm(w_ple_proj, 2, KD, None, False)
    gemm(w_ple_gate, KD, KD)
    for w in dfts:
        for k in range(w.shape[0] // P):
            for c in range(4):
                tile(w, k, c * P)
    gemm(w_fourier_out, KD, KD)

    def swiglu(layer):
        k0 = 0
        for n_hid in HALF:
            for b in range(n_hid // 2):
                f = k0 + 2 * b
                cols = [f * P, FF + f * P, (f + 1) * P, FF + (f + 1) * P]
                gemm(w_ffn_in[layer], KD, 4, None, k0 == 0 and b == 0, 0, cols)
            gemm(w_ffn_out[layer], n_hid, KD, None, True, k0)
            k0 += n_hid

    swiglu(0)
    for h in range(NH + 1):
        if h < NH:
            gemm(w_ret_in, KD, 4, None, True, 0, [1024 + h * 256, 1024 + h * 256 + P, h * 256, h * 256 + P])
        if h:
            gemm(w_ret_out, 4, KD, None, True, 4 * (h - 1))
        if h < NH:
            for k in range(KD):
                for c in range(4):
                    tile(w_ret_in, k, 2048 + h * 512 + c * P)
            gemm(w_ret_in, KD, 4, None, False, 0, [4096 + h * 512 + n * P for n in range(4)])
    swiglu(1)
    assert len(tiles) == 8 * N_CHUNK, (len(tiles), 8 * N_CHUNK)
    out = np.empty((N_CHUNK, P, 8, P), np.float32)
    for n, t in enumerate(tiles):
        out[n // 8, :, n % 8] = t
    return out.reshape(N_CHUNK, P, 1024)


def tables():
    import numpy as np
    j = np.arange(256)
    ang = 2 * np.pi * (np.outer(j, j) % 256) / 256
    scale = (S * 256) ** -0.5
    feat = np.concatenate([np.cos(ang), np.sin(ang)], 1) * scale
    t = np.arange(S)
    ang = 2 * np.pi * (np.outer(t, t) % S) / S
    dfts = [a.astype(np.float32) for a in (feat, np.cos(ang), -np.sin(ang))]
    p, u = np.arange(P)[:, None], np.arange(S)[None, :] - 3 * P
    dist = np.where(u // 64 <= p // 64, -np.abs(p - u).astype(np.float64), -1e30).astype(np.float32)
    inv = np.float32(10000.0) ** (-np.arange(P, dtype=np.float32) / np.float32(P))
    a = (inv[:, None] * t[None, :].astype(np.float32)).astype(np.float32)
    rope = np.concatenate([np.cos(a), np.sin(a)], 1).astype(np.float32)
    h = np.arange(NH)[:, None, None]
    d = np.arange(896)[None, None, :] - 3 * P - np.arange(P)[None, :, None]
    fwd, bwd = np.log1p(-2.0 ** (-5.0 - h)), np.log1p(-2.0 ** (-5.0 - (NH - 1 - h)))
    decay = (np.where(d >= 0, np.exp(d * fwd), np.exp(-d * bwd)) / 16).astype(np.float32)
    return dfts, dist, rope, decay


def kernel(**inputs):
    import numpy as np
    import concourse.bacc as bacc
    from concourse.bass_utils import run_bass_kernel_spmd as run
    a = {k: np.asarray(v) for k, v in inputs.items()}
    dfts, dist, rope, decay = tables()
    stream = weight_stream(a["w_in"][0], a["w_out"][0], a["w_ple_proj"][0], a["w_ple_gate"][0],
                           a["w_fourier_out_2"][0], a["w_ret_in_2"][0], a["w_ret_out_2"][0], a["w_ffn_in_2"],
                           a["w_ffn_out_2"], dfts)

    def tokens(x):
        return np.ascontiguousarray(x.T.reshape(-1, P, S).transpose(1, 0, 2)).reshape(P, -1)

    def vec(v):
        return v.reshape(-1, P).T

    def groups(w):
        return w.reshape(KD, P, -1, D).transpose(2, 0, 1, 3).reshape(-1, P, D)

    ada = np.concatenate([groups(a["w_ada_2"][0]), groups(a["w_ada_2"][1]), groups(a["w_ada_final_2"])])
    conv = a["conv_w"][0].reshape(3, NH, P).transpose(2, 1, 0).reshape(P, 3 * NH)
    lam = np.concatenate([a[n][0] for n in ("lambda_q1", "lambda_q2", "lambda_k1", "lambda_k2")])
    slopes = np.float32(2.0) ** (-2.0 * np.arange(1, NH + 1, dtype=np.float32))
    cols = np.concatenate([
        vec(a["pre_norm_gain"][0]), vec(a["post_norm_gain"][0]), vec(a["ple_norm_gain"][0]),
        vec(a["final_norm_g_2"]), vec(a["subln_gain"][0]), conv, vec(a["c_2"][0]), vec(a["b_ada_2"].reshape(-1)),
        vec(a["b_ada_final_2"]), vec(a["norm_mix_g_2"].reshape(-1)), vec(a["norm_ffn_g_2"].reshape(-1)),
        np.broadcast_to(lam, (P, 256)), np.broadcast_to(slopes, (P, NH)), np.eye(P, dtype=np.float32),
    ], 1)
    assert cols.shape == (P, NCOL)
    data = dict(W=stream, ADA=np.ascontiguousarray(ada), XT=tokens(a["x"][0]), PT=tokens(a["p"][0, 0]),
                COLS=np.ascontiguousarray(cols), DIST=dist, ROPE=rope, DECAY=decay)
    nc = bacc.Bacc("TRN2", target_bir_lowering=False, num_devices=1)
    aps = {k: nc.dram_tensor(f"in_{k}", v.shape, mybir.dt.float32, kind="ExternalInput").ap() for k, v in data.items()}
    out = nc.dram_tensor("out", (P, KD, S), mybir.dt.float32, kind="ExternalOutput").ap()
    aps["XT"] = aps["XT"].rearrange("p (k s) -> p k s", s=S)
    build(nc, OUT=out, **aps)
    r = run(nc, [{f"in_{k}": v for k, v in data.items()}], core_ids=[0])
    return r.results[0]["out"].transpose(2, 1, 0).reshape(1, S, D)
```

```python
import concourse.bass as bass
from concourse import mybir
from contextlib import ExitStack

P = 128
S = 512
D = 1024
KD = D // P
NH = 4
FF = 2816
FT = FF // P
NF = S // 2 + 2
HALF = (12, FT - 12)
TB = S // P
RING = 4
LAM_INIT = 0.2
N_ADA = 14
ADA_RING = 2
ADA_LAG = 6

COL = {}
NCOL = 0
for _name, _n in (("pre", KD), ("post", KD), ("ple", KD), ("final", KD), ("subln", 1), ("conv", 3 * NH),
                  ("c", KD), ("b_ada", N_ADA * KD), ("mix", 2 * KD), ("ffn", 2 * KD), ("lam", 4 * 64),
                  ("slope", NH), ("ident", P)):
    COL[_name] = NCOL
    NCOL += _n


def gemm_order(K, M, ks=None, first_outer=True):
    ks = list(ks or range(K))
    out = []
    m0 = 0
    if first_outer:
        m0 = 4
        out += [(k, m) for k in ks[:-2] for m in range(4)]
        out += [(k, m) for m in range(4) for k in ks[-2:]]
    return out + [(k, m) for m in range(m0, M) for k in ks]


ATT_KS = (0, 1, 2, 4, 5, 6, 7, 3)
CH = {}
_c = 0
for _name, _n in (("body", 8 * NH), ("out", 8), ("ple", 2), ("gate", 8), ("dft1", 1), ("dft2", 4), ("fout", 8),
                  ("up0a", 24), ("down0a", 12), ("up0b", 20), ("down0b", 10),
                  ("ret", 12), ("retbody", 16 * (NH - 1)), ("retout", 4),
                  ("up1a", 24), ("down1a", 12), ("up1b", 20), ("down1b", 10)):
    CH[_name] = _c
    _c += _n
N_CHUNK = _c

TI = {}
_c = 0
for _name, _n in (("body", 8 * NH), ("out", 8), ("ple", 8), ("gate", 8), ("dft1", 8), ("dft2", 8), ("fout", 8),
                  ("up0a", 24), ("down0a", 8), ("up0b", 20), ("down0b", 8),
                  ("ret", 20), ("retbody", 28 * (NH - 1)), ("retout", 8),
                  ("up1a", 24), ("down1a", 8), ("up1b", 20), ("down1b", 8)):
    TI[_name] = _c
    _c += _n

AUX = {}
_c = 0
for _name, _n in (("pre", 1), ("body", 7 * NH), ("post", 1), ("ada4", 1), ("ple", 1), ("four", 1), ("ada5", 1),
                  ("ada6", 1), ("ffn0", 1), ("ada7", 1), ("ada", 6), ("rnorm", 1),
                  ("ret", NH), ("ffn1", 1), ("final", 1)):
    AUX[_name] = _c
    _c += _n


class At:

    def __init__(self, i=None, **per):
        self.i, self.per = i, per

    def __call__(self, kind, n):
        return n if self.i is None else self.i * self.per[kind] + n


class Head(At):

    def __call__(self, kind, n):
        ahead = self.per[kind] if kind in ("aux", "four", "three", "one", "sixteen") else 0
        return super().__call__(kind, n + ahead)

    def before(self):
        return At(self.i, **self.per)


def build(nc, W, ADA, XT, PT, COLS, DIST, ROPE, DECAY, OUT):
    fp32, f32r = mybir.dt.float32, mybir.dt.float32r
    ALU, ACT, AX = mybir.AluOpType, mybir.ActivationFunctionType, mybir.AxisListType
    ctx = ExitStack()
    with ctx:
        def sb(name, shape, dt=fp32):
            return ctx.enter_context(nc.sbuf_tensor(name, shape, dt))

        def sem(name):
            return ctx.enter_context(nc.semaphore(name))

        w_raw = sb("w_raw", [P, RING, 1024])
        w_hi = sb("w_hi", [P, RING, 1024], f32r)
        w_lo = sb("w_lo", [P, RING, 1024], f32r)
        ada_raw = sb("ada_raw", [P, ADA_RING, 1024])
        ada_acc = sb("ada_acc", [P, 1024])
        X = sb("X", [P, KD, S])
        a_hi = sb("a_hi", [P, KD, S], f32r)
        a_lo = sb("a_lo", [P, KD, S], f32r)
        b_hi = sb("b_hi", [P, 12, S], f32r)
        b_lo = sb("b_lo", [P, 12, S], f32r)
        sq = sb("sq", [P, 2, S])
        sqsum = sb("sqsum", [P, S])
        rinv = sb("rinv", [P, S])
        tmp = sb("tmp", [P, 2, S])
        cols = sb("cols", [P, NCOL])
        ones = sb("ones", [P, P])
        small = sb("small", [P, 64])
        mod = sb("mod", [P, N_ADA * KD])
        gs = sb("gs", [P, 5 * KD])
        scr = sb("scr", [P, 9216])
        banks = ctx.enter_context(nc.psum_tensor("banks", [P, 8, 512], fp32))
        aux = banks[:, 7, :]

        ident = cols[:, COL["ident"]:COL["ident"] + P]
        zero, eps6, eps5, neglam, gsub = (small[:, n:n + 1] for n in range(5))
        lamv = small[:, 6:8]
        mx, nmx, rsum, rrec, c1 = (small[:, n:n + 2] for n in (8, 10, 12, 14, 16))
        lamp = small[:, 18:20]
        cact = small[:, 24:32]
        ctanh = small[:, 32:40]
        gple = small[:, 40:48]
        vsum, vmean = small[:, 51:55], small[:, 55:59]
        but0, minus_but0, flip = (small[:, n:n + 1] for n in (48, 49, 50))

        def area(n, k=1):
            v = scr[:, n * S:(n + k) * S]
            return v if k == 1 else v.rearrange("p (k s) -> p k s", k=k)

        Q, K, VB, ZA, dist, bias = (area(n) for n in range(6))
        SC = area(6, 4).rearrange("p (u m) s -> p u m s", m=2)
        WT = area(10, 2)
        CG = area(12)
        G = scr[:, 13 * S:14 * S + 2]
        lamt = scr[:, 15 * S:15 * S + 256]
        MIX, E = area(0, 8), area(8, 8)
        PV = scr[:, 16 * S:18 * S]
        GT = [tmp[:, 0, :], tmp[:, 1, :], area(16), area(17)]
        XG = {"pre": area(6, 8), "four": area(0, 8), "ffn0": area(10, 8), "rnorm": area(10, 8), "ffn1": area(10, 8)}
        KQ = ada_raw[:, :, :].rearrange("p a (b s) -> p (a b) s", s=S)
        T2 = area(0, 2)
        SG = area(2, 2)
        HD = area(4, 2)
        FM = area(0, 4)
        FU = area(4, 4)
        GG, Y = area(0, 4), area(4, 4)
        COS, SIN = area(8), area(9)
        DEC = scr[:, 10 * S:10 * S + 896]
        RT = area(12, 4)
        VR = area(16, 2)

        raw_in = [sem(f"raw_in{s}") for s in range(RING)]
        whi = sem("whi")
        wlo = sem("wlo")
        w_used = sem("w_used")
        ada_in = [sem(f"ada_in{s}") for s in range(ADA_RING)]
        ada_sum = sem("ada_sum")
        x_in = [sem(f"x_in{m}") for m in range(KD)]
        cols_in, p_in, dist_in, rope_in, dec_in = (
            sem(n) for n in ("cols_in", "p_in", "dist_in", "rope_in", "dec_in"))
        const = sem("const")
        link_s = sem("dve_link")
        tile_ready = sem("tile_ready")
        bank_read = [sem(f"bank_read{b}") for b in range(4)]
        aux_ready, aux_free = sem("aux_ready"), sem("aux_free")
        sq_ready, sq_added, r_ready = sem("sq_ready"), sem("sq_added"), sem("r_ready")
        xg_s = sem("xg_s")
        h_ready, h_hi, a_ready = sem("h_ready"), sem("h_hi"), sem("a_ready")
        lam_in, lam_e = sem("lam_in"), sem("lam_e")
        za_t, sc_ready, sc_read, nm_ready, ex_ready, w_ready = (
            sem(n) for n in ("za_t", "sc_ready", "sc_read", "nm_ready", "ex_ready", "w_ready"))
        v_hi, wt_hi, pv_ready, o_copied, o_sq, o_r, o_out, mix_hi, mix_ready = (
            sem(n) for n in ("v_hi", "wt_hi", "pv_ready", "o_copied", "o_sq", "o_r", "o_out", "mix_hi",
                             "mix_ready"))
        zc_t, cv_out = sem("zc_t"), sem("cv_out")
        p_hi, p_ready = sem("p_hi"), sem("p_ready")
        x_new, xg_hi, xg_ready, e_ready = (sem(n) for n in ("x_new", "xg_hi", "xg_ready", "e_ready"))
        z_hi, f_sum, f_hi, f_ready = (sem(n) for n in ("z_hi", "f_sum", "f_hi", "f_ready"))
        hid_t, hid_f, hid_hi = (sem(n) for n in ("hid_t", "hid_f", "hid_hi"))
        x_scaled, x_done = sem("x_scaled"), sem("x_done")
        rot, rot_hi, rot_ready, v_mean, vv_hi, v_ready, gg_t, pd, pd_hi, y_sq, y_qs, y_r, y_f, y_hi, y_ready = (
            sem(n) for n in ("rot", "rot_hi", "rot_ready", "v_mean", "vv_hi", "v_ready", "gg_t", "pd", "pd_hi",
                             "y_sq", "y_qs", "y_r", "y_f", "y_hi", "y_ready"))
        out_done = sem("out_done")

        block = ctx.enter_context(nc.Block())
        NORMS = dict(pre=0, post=1, ple=2, four=3, ffn0=4, rnorm=5, ffn1=6, final=7)

        def col(name, n=0, k=1):
            return cols[:, COL[name] + n:COL[name] + n + k]

        def wait_tile(eng, at, t):
            eng.wait_ge(tile_ready, at("tile", t + 1))

        def read_out(ins, t):
            ins.then_inc(bank_read[t % 4], 1)

        def wait_read(eng, at, t):
            eng.wait_ge(bank_read[t % 4], at("bank", t // 4 + 1))

        flat = At()

        @block.sync
        def _(sp):
            def load_w(at, c, first=False):
                if not first:
                    sp.wait_ge(wlo, at("chunk", c - RING + 1))
                src = W[c] if at.i is None else W[bass.ds(at("chunk", c), 1), :, :].rearrange("a p n -> (a p) n")
                sp.dma_start(w_raw[:, c % RING, :], src).then_inc(raw_in[c % RING], 16)

            def load_ada(at, a, first=False):
                if not first:
                    sp.wait_ge(ada_sum, at("ada", a - ADA_RING + 1))
                src = ADA[a] if at.i is None else ADA[bass.ds(at("ada", a), 1), :, :].rearrange("a p n -> (a p) n")
                sp.dma_start(ada_raw[:, a % ADA_RING, :], src).then_inc(ada_in[a % ADA_RING], 16)

            for m in range(KD):
                sp.dma_start(X[:, m, :], XT[:, m, :]).then_inc(x_in[m], 16)
            pos = [0, 0]

            def load(at, k):
                load_w(at, pos[0], at.i is None and pos[0] < RING)
                pos[0] += 1
                for _ in range(k):
                    load_ada(at, pos[1], at.i is None and pos[1] < ADA_RING)
                    pos[1] += 1

            def straight(*steps):
                for k in steps:
                    load(flat, k)

            def turns(n, chunks, k):
                with sp.Fori(0, n) as i:
                    for _ in range(chunks):
                        load(At(i, chunk=chunks, ada=chunks * k), k)
                pos[0] += (n - 1) * chunks
                pos[1] += (n - 1) * chunks * k

            straight(*[0] * ADA_LAG, 1, 1, 1, 1)
            turns(9, 4, 1)
            assert pos == [ADA_LAG + 5 * KD, 5 * KD]
            straight(2, 0, 1, 2, 1, 0, 1, 1, 0, 0)
            straight(1, 1, 2, 1, 1, 1, 1, 2, 2, 0, 0, 2, 2)
            turns(6, 4, 2)
            turns((N_CHUNK - pos[0]) // 4, 4, 0)
            straight(*[0] * (N_CHUNK - pos[0]))
            assert pos == [N_CHUNK, N_ADA * KD], pos
            for m in range(KD):
                sp.wait_ge(x_done, m + 1)
                sp.dma_start(OUT[:, m, :], X[:, m, :]).then_inc(out_done, 16)
            sp.wait_ge(out_done, 16 * KD)

        @block.gpsimd
        def _(pool):
            def lo_part(at, c, first=False):
                pool.wait_ge(whi, at("chunk", c + 1))
                pool.tensor_tensor(w_lo[:, c % RING, :], w_raw[:, c % RING, :],
                                   w_hi[:, c % RING, :].bitcast(fp32), ALU.subtract).then_inc(wlo, 1)

            n = N_CHUNK // 4
            with pool.Fori(0, n) as i:
                at = At(i, chunk=4)
                for s in range(4):
                    lo_part(at, s)
            for c in range(4 * n, N_CHUNK):
                lo_part(flat, c)

        @block.scalar
        def _(act):
            act.dma_start(cols[:, :], COLS).then_inc(cols_in, 16)
            act.dma_start(dist, DIST).then_inc(dist_in, 16)

            def split_w(at, c, first=False):
                if c >= N_CHUNK:
                    return
                act.wait_ge(raw_in[c % RING], at("slot", 16 * (c // RING + 1)))
                if not first:
                    act.wait_ge(w_used, at("chunk", c - RING + 1))
                act.activation(w_hi[:, c % RING, :], w_raw[:, c % RING, :], ACT.Copy).then_inc(whi, 1)

            def square(at, v, m, src):
                if m >= 3:
                    act.wait_ge(sq_added, 6 * v + m - 2)
                dst = sqsum[:, :] if m == 0 else sq[:, m % 2, :]
                act.activation(dst, src, ACT.Square).then_inc(sq_ready, 1)

            def rsqrt(u, n, eps, done, at=flat):
                act.preload_act_table_set("natural_log_exp_and_others")
                act.wait_ge(aux_ready, at("aux", u + 1))
                act.activation(rinv[:, :], aux, ACT.Ln, bias=eps, scale=1.0 / n).then_inc(aux_free, 1)
                act.wait_ge(aux_free, at("aux", u + 1))
                act.activation(rinv[:, :], rinv[:, :], ACT.Exp, scale=-0.5).then_inc(done, 1)

            def norm_hi(v, shift, c=None, first_chunks=False, after=None):
                for m in range(KD):
                    if first_chunks and m in (1, 2, 3):
                        split_w(flat, m, True)
                    if m == 4 and c is not None:
                        split_w(flat, c)
                    act.wait_ge(h_ready, 8 * v + m + 1)
                    act.activation(a_hi[:, m, :], tmp[:, m % 2, :], ACT.Identity, bias=shift(m)).then_inc(h_hi, 1)
                    if after:
                        after(m)

            def vector(g):
                return lambda m: mod[:, KD * g + m:KD * g + m + 1]

            act.wait_ge(cols_in, 16)
            for m in range(KD):
                act.wait_ge(x_in[m], 16)
                square(flat, 0, m, X[:, m, :])
            split_w(flat, 0, True)
            act.wait_ge(const, 1)
            rsqrt(AUX["pre"], D, eps6, r_ready)
            norm_hi(0, lambda m: zero, first_chunks=True)
            act.activation(ctanh, col("c", 0, KD), ACT.Tanh, scale=0.5).then_inc(lam_e, 1)
            act.wait_ge(lam_in, 1)
            act.activation(lamv, lamp, ACT.Exp).then_inc(lam_e, 1)

            t0, c0 = TI["body"], CH["body"]

            def exps(at, b):
                n = (b + 1) * P
                act.wait_ge(nm_ready, at("unit", b + 1))
                for m in range(2):
                    act.activation(SC[:, b % 2, m, 0:n], SC[:, b % 2, m, 0:n], ACT.Exp, bias=nmx[:, m:m + 1],
                                   accum_out=rsum[:, m:m + 1]).then_inc(ex_ready, 1)

            def weights_hi(at, b):
                n = (b + 1) * P
                act.wait_ge(aux_ready, at("aux", AUX["body"] + 1 + b + 1))
                act.activation(b_hi[:, 9 + b % 2, 0:n], aux[:, 0:n], ACT.Copy).then_inc(wt_hi, 1)

            with act.Fori(0, NH) as i:
                at = At(i, chunk=8, slot=32, tile=8, bank=2, aux=7, unit=4, one=1, two=2, eight=8)
                for n, dst in ((0, Q), (1, K), (2, VB)):
                    split_w(at, c0 + n + 4)
                    wait_tile(act, at, t0 + n)
                    read_out(act.activation(dst, banks[:, n, :], ACT.Copy), n)
                exps(at, 0)
                split_w(at, c0 + 7)
                wait_tile(act, at, t0 + 3)
                act.activation(tmp[:, 1, :], banks[:, 3, :], ACT.Tanh, scale=0.5).then_inc(za_t, 1)
                exps(at, 1)
                act.wait_ge(aux_ready, at("aux", AUX["body"] + 1))
                act.activation(b_hi[:, 8, :], aux, ACT.Copy).then_inc(v_hi, 1)
                split_w(at, c0 + 8)
                wait_tile(act, at, t0 + 4)
                read_out(act.activation(VB, banks[:, 0, :], ACT.Copy), t0 + 4)
                weights_hi(at, 0)
                exps(at, 2)
                split_w(at, c0 + 9)
                wait_tile(act, at, t0 + 5)
                read_out(act.activation(CG, banks[:, 1, :], ACT.Copy), t0 + 5)
                weights_hi(at, 1)
                exps(at, 3)
                split_w(at, c0 + 10)
                weights_hi(at, 2)
                weights_hi(at, 3)
                wait_tile(act, at, t0 + 7)
                act.activation(tmp[:, 1, :], banks[:, 3, :], ACT.Tanh, scale=0.5).then_inc(zc_t, 1)
                act.wait_ge(pv_ready, at("one", 1))
                act.activation(sq[:, 0, :], banks[:, 4, :], ACT.Copy).then_inc(o_copied, 1)
                act.activation(sqsum[:, :], banks[:, 4, :], ACT.Square).then_inc(o_sq, 1)
                act.wait_ge(cv_out, at("one", 1))
                act.activation(b_hi[:, bass.ds(i + 4, 1), :].rearrange("p a s -> p (a s)"), tmp[:, 0, :], ACT.Copy,
                               scale=0.5).then_inc(mix_hi, 1)
                split_w(at, c0 + 11)
                rsqrt(AUX["body"] + 5, P, eps5, o_r, at)
                act.wait_ge(o_out, at("one", 1))
                act.activation(b_hi[:, bass.ds(i, 1), :].rearrange("p a s -> p (a s)"), tmp[:, 0, :],
                               ACT.Copy).then_inc(mix_hi, 1)

            act.dma_start(PV, PT).then_inc(p_in, 16)
            act.wait_ge(p_in, 16)
            act.activation(b_hi[:, 8:10, :].rearrange("p k s -> p (k s)"), PV, ACT.Copy).then_inc(p_hi, 1)
            c0, t0 = CH["out"], TI["out"]
            for n in range(8):
                if n != 3:
                    split_w(flat, c0 + n + 4)
                if n >= 3:
                    for m in ((0, 1, 2, 3) if n == 3 else (n,)):
                        wait_tile(act, flat, t0 + m)
                        square(flat, 1, m, banks[:, m % 4, :])
                        if n == 3 and m == 0:
                            split_w(flat, c0 + n + 4)

            def e_tile(m):
                t = TI["ple"] + m
                wait_tile(act, flat, t)
                square(flat, 2, m, banks[:, t % 4, :])
                read_out(act.activation(E[:, m, :], banks[:, t % 4, :], ACT.Copy), t)

            for m in range(2):
                if m == 0:
                    rsqrt(AUX["post"], D, eps6, r_ready)
                e_tile(m)
            for m in range(2, KD):
                if m == 4:
                    split_w(flat, CH["ple"] + 4)
                if m == 7:
                    split_w(flat, CH["ple"] + 5)
                e_tile(m)
                if m >= 3:
                    act.wait_ge(x_new, m - 2)
                    act.activation(a_hi[:, m - 3, :], X[:, m - 3, :], ACT.Copy).then_inc(xg_hi, 1)
            for m in range(5, KD):
                act.wait_ge(x_new, m + 1)
                act.activation(a_hi[:, m, :], X[:, m, :], ACT.Copy).then_inc(xg_hi, 1)
            c0, t0 = CH["gate"], TI["gate"]

            def residual_squares(v, t0, ms):
                for m in ms:
                    wait_read(act, flat, t0 + m)
                    square(flat, v, m, X[:, m, :])

            def gate_tile(m):
                wait_tile(act, flat, t0 + m)
                if m >= 4:
                    act.wait_ge(x_new, KD + m - 3)
                read_out(act.activation(GT[m % 4], banks[:, (t0 + m) % 4, :], ACT.Tanh, scale=0.5), t0 + m)

            def gate_square(m):
                act.wait_ge(x_new, KD + m + 1)
                square(flat, 3, m, X[:, m, :])

            for n in range(8):
                if n not in (3, 7):
                    split_w(flat, c0 + n + 4)
                if n == 1:
                    rsqrt(AUX["ple"], D, eps6, r_ready)
                if n >= 3:
                    for m in ((0, 1, 2, 3) if n == 3 else (n,)):
                        gate_tile(m)
                        if n == 3 and m == 0:
                            split_w(flat, c0 + n + 4)
                        if 0 < m < 4:
                            gate_square(m - 1)
                        if m >= 3:
                            gate_square(m)
            rsqrt(AUX["four"], D, eps6, r_ready)

            t1 = TI["dft1"]

            def z_group(g):
                for z in range(2 * g, 2 * g + 2):
                    wait_tile(act, flat, t1 + z)
                    act.activation(b_hi[:, z, :], banks[:, (t1 + z) % 4, :], ACT.Copy).then_inc(z_hi, 1)

            norm_hi(1, vector(0), c0 + 11, after=lambda m: z_group((m - 3) // 2) if m in (3, 5, 7) else None)
            c0 = CH["dft1"]
            z_group(3)
            split_w(flat, c0 + 4)
            c0, t0 = CH["dft2"], TI["dft2"]
            for g in range(NH):
                if g == NH - 1:
                    for n in range(3):
                        split_w(flat, c0 + n + 4)
                wait_tile(act, flat, t0 + 2 * g)
                src = banks[:, (t0 + 2 * g) % 4, 0:NF]
                act.activation(FU[:, 2 * (g % 2), 0:NF], src, ACT.Copy)
                read_out(act.activation(FU[:, 2 * (g % 2) + 1, 0:NF], src, ACT.Identity, scale=flip, bias=zero), t0 + 2 * g)
                for n in range(2):
                    if n == 0:
                        act.wait_ge(f_sum, g + 1)
                    else:
                        wait_read(act, flat, t0 + 2 * g + 1)
                    act.activation(a_hi[:, 2 * g + n, :], FM[:, 2 * (g % 2) + n, :], ACT.Copy).then_inc(f_hi, 1)
            split_w(flat, c0 + 7)
            c0, t0 = CH["fout"], TI["fout"]
            for n in range(8):
                if n < 7:
                    split_w(flat, c0 + n + 4)
                if n >= 3:
                    residual_squares(4, t0, (0, 1, 2, 3) if n == 3 else (n,))

            def up_body(at, c, t, j):
                for n in range(2):
                    split_w(at, c + 2 * n + 4)
                    wait_tile(act, at, t + 2 * n)
                    act.activation(T2[:, n, :], banks[:, (t + 2 * n) % 4, :], ACT.Tanh, scale=0.5).then_inc(hid_t, 1)
                    split_w(at, c + 2 * n + 5)
                    act.wait_ge(hid_f, at("hid", j + n + 1))
                    if at.i is None:
                        dst = b_hi[:, j % FT % HALF[0] + n, :]
                    else:
                        dst = b_hi[:, bass.ds(at("hid", j % FT % HALF[0] + n), 1), :].rearrange("p a s -> p (a s)")
                    act.activation(dst, HD[:, n, :], ACT.Copy, scale=0.5).then_inc(hid_hi, 1)

            def swiglu(layer, v):
                rsqrt(AUX[f"ffn{layer}"], D, eps6, r_ready)
                norm_hi(2 + 2 * layer, vector(6 * layer + 3), CH[f"up{layer}a"] + 3)
                for part, n_hid in zip("ab", HALF):
                    c, t = CH[f"up{layer}{part}"], TI[f"up{layer}{part}"]
                    j = layer * FT + (0 if part == "a" else HALF[0])
                    first = 1 if part == "a" else 0
                    if first:
                        up_body(flat, c, t, j)
                    with act.Fori(0, n_hid // 2 - first) as i:
                        at = At(i, chunk=4, slot=16, tile=4, hid=2)
                        up_body(at, c + 4 * first, t + 4 * first, j + 2 * first)
                    c, t = CH[f"down{layer}{part}"], TI[f"down{layer}{part}"]
                    for n in range(n_hid):
                        if part == "a" or n < n_hid - 1:
                            split_w(flat, c + n + 4)
                        if part == "b":
                            done = [m for m in range(KD) if down_last(n_hid, m) == n]
                            residual_squares(v, t, done)

            def down_last(K, m):
                order = gemm_order(K, KD)
                return max(n for n, (k, mm) in enumerate(order) if mm == m) // 8

            swiglu(0, 5)

            act.dma_start(scr[:, 8 * S:10 * S], ROPE).then_inc(rope_in, 16)
            rsqrt(AUX["rnorm"], D, eps6, r_ready)
            norm_hi(3, vector(6), CH["ret"] + 3)

            def keys_queries(at, c, t):
                for n in range(3):
                    split_w(at, c + n + 4)
                for n in range(4):
                    wait_tile(act, at, t + n)
                    read_out(act.activation(KQ[:, n, :], banks[:, (t + n) % 4, :], ACT.Copy), t + n)
                split_w(at, c + 3 + 4)
                for n in range(4):
                    act.wait_ge(rot, at("four", n + 1))
                    act.activation(b_hi[:, n, :], RT[:, 1 + 2 * (n % 2), :], ACT.Copy).then_inc(rot_hi, 1)

            def head(at, c, t):
                for n in range(3):
                    split_w(at, c + n + 4)
                for n in range(5):
                    if n < 4:
                        wait_tile(act, at, t + n)
                        if n >= 2:
                            act.wait_ge(v_ready, at("four", n - 1))
                        read_out(act.activation(VR[:, n % 2, :], banks[:, (t + n) % 4, :], ACT.Copy,
                                                accum_out=vsum[:, n:n + 1]), t + n)
                    if n:
                        act.wait_ge(v_mean, at("four", n))
                        act.activation(b_hi[:, 3 + n, :], VR[:, (n - 1) % 2, :], ACT.Identity,
                                       bias=vmean[:, n - 1:n]).then_inc(vv_hi, 1)
                split_w(at, c + 3 + 4)
                c, t = c + 4, t + 4
                for n in range(3):
                    if n < 2:
                        split_w(at, c + n + 4)
                    wait_tile(act, at, t + n)
                    act.activation(RT[:, n, :], banks[:, (t + n) % 4, :], ACT.Tanh, scale=0.5).then_inc(gg_t, 1)
                for n in range(4):
                    act.wait_ge(pd, at("four", n + 1))
                    act.activation(b_hi[:, 8 + n, :], tmp[:, n % 2, :], ACT.Copy).then_inc(pd_hi, 1)
                split_w(at, c + 2 + 4)
                t += 7
                wait_tile(act, at, t)
                act.activation(RT[:, 3, :], banks[:, t % 4, :], ACT.Tanh, scale=0.5).then_inc(gg_t, 1)

            def group_norm(at, t, c, early):
                for n in range(4):
                    wait_read(act, at, t + n)
                    if n >= 3:
                        act.wait_ge(y_qs, at("three", n - 2))
                    act.activation(sqsum[:, :] if n == 0 else sq[:, n % 2, :], Y[:, n, :],
                                   ACT.Square).then_inc(y_sq, 1)
                if early:
                    split_w(at, c)
                rsqrt(AUX["ret"], 4 * P, eps6, y_r, at)
                for n in range(4):
                    act.wait_ge(y_f, at("four", n + 1))
                    act.activation(b_hi[:, 8 + n, :], Y[:, n, :], ACT.Copy, scale=0.5).then_inc(y_hi, 1)
                if not early:
                    split_w(at, c)

            RB = dict(chunk=16, slot=64, tile=28, bank=7, aux=1, four=4, three=3, one=1)
            act.dma_start(DEC, DECAY[0]).then_inc(dec_in, 16)
            keys_queries(flat, CH["ret"], TI["ret"])
            head(flat, CH["ret"] + 4, TI["ret"] + 4)
            c0, t0 = CH["retbody"], TI["retbody"]
            with act.Fori(0, NH - 1) as i:
                at = Head(i, **RB)
                group_norm(at.before(), t0 - 4, c0 + 3, True)
                act.dma_start(DEC, DECAY[bass.ds(i + 1, 1), :, :].rearrange("a p n -> (a p) n")).then_inc(dec_in, 16)
                keys_queries(at, c0, t0)
                for n in range(4):
                    split_w(at, c0 + 4 + n + 4)
                head(at, c0 + 8, t0 + 12)
            group_norm(At(NH - 1, **RB), t0 - 4, CH["retout"] + 3 - 16 * (NH - 1), False)
            c0, t0 = CH["retout"], TI["retout"]
            order = gemm_order(4, KD)
            for n in range(4):
                if n < 3:
                    split_w(flat, c0 + n + 4)
                residual_squares(6, t0, [m for m in range(KD)
                                         if max(q for q, (k, mm) in enumerate(order) if mm == m) // 8 == n])
            swiglu(1, 7)
            rsqrt(AUX["final"], D, eps6, r_ready)
            for m in range(KD):
                act.wait_ge(x_scaled, m + 1)
                act.activation(X[:, m, :], X[:, m, :], ACT.Identity, bias=vector(12)(m)).then_inc(x_done, 1)

        @block.vector
        def _(dve):
            linked = [0]

            def link(ins, at=flat):
                linked[0] += 1
                ins.then_inc(link_s, 1)
                dve.wait_ge(link_s, at("link", linked[0]))

            steps = [0]

            def ada(at=flat, k=1):
                for _ in range(k):
                    a = steps[0]
                    steps[0] += 1
                    f = a % KD
                    dve.wait_ge(ada_in[a % ADA_RING], at("adaslot", 16 * (a // ADA_RING + 1)))
                    src = ada_raw[:, a % ADA_RING, :]
                    if f == 0:
                        ins = dve.tensor_scalar(ada_acc[:, :], src, cact[:, 0:1], None, ALU.mult)
                    else:
                        dve.wait_ge(ada_sum, at("ada", a))
                        ins = dve.scalar_tensor_tensor(out=ada_acc[:, :], in0=src, scalar=cact[:, f:f + 1],
                                                       in1=ada_acc[:, :], op0=ALU.mult, op1=ALU.add)
                    ins.then_inc(ada_sum, 1)

            def ada_out(u, g, at=flat):
                dve.wait_ge(aux_ready, at("aux", u + 1))
                if at.i is None:
                    dst, b = mod[:, KD * g:KD * g + KD], col("b_ada", KD * g, KD)
                else:
                    dst = mod[:, bass.ds(at("eight", KD * g), KD)]
                    b = cols[:, bass.ds(at("eight", COL["b_ada"] + KD * g), KD)]
                dve.tensor_tensor(dst, aux[:, 0:KD], b, ALU.add).then_inc(aux_free, 1)

            def add_square(v, m):
                if m in (-1, 0, KD - 1):
                    return
                dve.wait_ge(sq_ready, 8 * v + m + 1)
                if m >= 2:
                    dve.wait_ge(sq_added, 6 * v + m - 1)
                dve.tensor_tensor(sqsum[:, :], sqsum[:, :], sq[:, m % 2, :], ALU.add).then_inc(sq_added, 1)

            def gained(name, m, g):
                dve.tensor_scalar(XG[name][:, m, :], X[:, m, :], g(m), None, ALU.mult).then_inc(xg_s, 1)

            def norm_apply(name, a, shift, after=None):
                dve.wait_ge(r_ready, NORMS[name] + 1)
                dve.wait_ge(xg_s, 8 * a + 8)

                def lo(m):
                    dve.wait_ge(h_hi, 8 * a + m + 1)
                    dve.scalar_tensor_tensor(out=a_lo[:, m, :], in0=tmp[:, m % 2, :], scalar=shift(m),
                                             in1=a_hi[:, m, :].bitcast(fp32), op0=ALU.add,
                                             op1=ALU.subtract).then_inc(a_ready, 1)
                    if after:
                        after(m)

                for m in range(KD):
                    if m >= 2:
                        dve.wait_ge(a_ready, 8 * a + m - 1)
                    dve.tensor_tensor(tmp[:, m % 2, :], XG[name][:, m, :], rinv[:, :], ALU.mult).then_inc(h_ready, 1)
                    if m:
                        lo(m - 1)
                lo(KD - 1)

            def gain(a):
                return lambda m: gs[:, KD * a + m:KD * a + m + 1]

            def vector(g):
                return lambda m: mod[:, KD * g + m:KD * g + m + 1]

            def scale_columns(n, gain, g):
                link(dve.scalar_tensor_tensor(out=gs[:, KD * n:KD * n + KD], in0=mod[:, KD * g:KD * g + KD],
                                              scalar=1.0, in1=gain, op0=ALU.add, op1=ALU.mult))

            def residual(at, t, m, g):
                wait_tile(dve, at, t)
                read_out(dve.scalar_tensor_tensor(out=X[:, m, :], in0=banks[:, t % 4, :],
                                                  scalar=mod[:, KD * g + m:KD * g + m + 1], in1=X[:, m, :],
                                                  op0=ALU.mult, op1=ALU.add), t)

            def residuals(t0, ms, g, v, name=None, a=None, lag=False):
                for m in ms:
                    residual(flat, t0 + m, m, g)
                    if name:
                        wait_read(dve, flat, t0 + m)
                        gained(name, m, gain(a))
                    if m <= 5 or lag:
                        add_square(v, m - 1)
                    if m >= 5 and not lag:
                        add_square(v, m)

            dve.memset(zero, 0.0)
            dve.memset(eps6, 1e-6)
            dve.memset(eps5, 1e-5)
            dve.memset(ones[:, :], 1.0).then_inc(const, 1)
            for v, row0, rest in ((but0, 0.0, 1.0), (minus_but0, 0.0, -1.0), (flip, 1.0, -1.0)):
                link(dve.memset(v, rest))
                link(dve.memset(v[0:1, :], row0))
            dve.wait_ge(cols_in, 16)
            for m in range(KD):
                dve.wait_ge(x_in[m], 16)
                gained("pre", m, lambda m: col("pre", m))
                add_square(0, m)
            norm_apply("pre", 0, lambda m: zero)
            lt = lamt.rearrange("p (a n) -> p a n", a=4)
            lc = col("lam", 0, 256).rearrange("p (a n) -> p a n", a=4)
            link(dve.tensor_tensor(lt[:, 0:2, :], lc[:, 0:2, :], lc[:, 2:4, :], ALU.mult))
            dve.tensor_reduce(lamp, lt[:, 0:2, :], AX.X, ALU.add).then_inc(lam_in, 1)
            dve.wait_ge(lam_e, 1)
            link(dve.tensor_scalar(ctanh, ctanh, 1.0, 0.5, ALU.add, ALU.mult))
            link(dve.tensor_tensor(cact, ctanh, col("c", 0, KD), ALU.mult))
            dve.wait_ge(lam_e, 2)
            link(dve.tensor_tensor(neglam, lamv[:, 1:2], lamv[:, 0:1], ALU.subtract))
            link(dve.tensor_scalar(neglam, neglam, -LAM_INIT, None, ALU.add))
            link(dve.tensor_scalar(gsub, col("subln"), 0.5 * (1.0 - LAM_INIT), None, ALU.mult))
            link(dve.tensor_scalar(gple, col("ple", 0, KD), 0.5, None, ALU.mult))
            link(dve.memset(G[:, 0:2], 0.0))

            dve.wait_ge(dist_in, 16)
            t0 = TI["body"]
            A0 = AUX["body"]

            def softmax_a(at, b):
                n = (b + 1) * P
                dve.wait_ge(sc_ready, at("unit", b + 1))
                for m in range(2):
                    dve.scalar_tensor_tensor(out=SC[:, b % 2, m, 0:n], in0=banks[:, 5 + m, 0:n], scalar=0.125,
                                             in1=bias[:, 3 * P - P * b:S], op0=ALU.mult,
                                             op1=ALU.add).then_inc(sc_read, 1)
                dve.wait_ge(sc_read, at("eight", 2 * b + 2))
                link(dve.tensor_reduce(mx, SC[:, b % 2, :, 0:n], AX.X, ALU.max), at)
                dve.tensor_scalar(nmx, mx, -1.0, None, ALU.mult).then_inc(nm_ready, 1)

            def softmax_b(at, b):
                n = (b + 1) * P
                dve.wait_ge(ex_ready, at("eight", 2 * b + 2))
                link(dve.reciprocal(rrec, rsum), at)
                link(dve.tensor_scalar(c1[:, 0:1], rrec[:, 1:2], neglam, None, ALU.mult), at)
                if b >= 2:
                    dve.wait_ge(aux_ready, at("aux", A0 + 1 + b - 2 + 1))
                link(dve.tensor_scalar(WT[:, b % 2, 0:n], SC[:, b % 2, 0, 0:n], rrec[:, 0:1], None, ALU.mult), at)
                dve.scalar_tensor_tensor(out=WT[:, b % 2, 0:n], in0=SC[:, b % 2, 1, 0:n], scalar=c1[:, 0:1],
                                         in1=WT[:, b % 2, 0:n], op0=ALU.mult, op1=ALU.add).then_inc(w_ready, 1)

            def weights_lo(at, b):
                n = (b + 1) * P
                dve.wait_ge(wt_hi, at("unit", b + 1))
                dve.tensor_tensor(b_lo[:, 9 + b % 2, 0:n], aux[:, 0:n], b_hi[:, 9 + b % 2, 0:n].bitcast(fp32),
                                  ALU.subtract).then_inc(aux_free, 1)

            base = linked[0]
            per_link = 1 + 4 * 4 + 4 + 1
            with dve.Fori(0, NH) as i:
                at = At(i, chunk=8, tile=8, bank=2, aux=7, unit=4, one=1, two=2, eight=8, link=per_link,
                        ada=8, adaslot=64)
                link(dve.tensor_scalar(bias, dist, cols[:, bass.ds(i + COL["slope"], 1)], None, ALU.mult), at)
                ada(at, 2)
                softmax_a(at, 0)
                ada(at, 1)
                softmax_b(at, 0)
                wait_tile(dve, at, t0 + 3)
                dve.wait_ge(za_t, at("one", 1))
                read_out(dve.scalar_tensor_tensor(out=ZA, in0=tmp[:, 1, :], scalar=1.0, in1=banks[:, 3, :],
                                                  op0=ALU.add, op1=ALU.mult), 3)
                softmax_a(at, 1)
                dve.wait_ge(v_hi, at("one", 1))
                dve.tensor_tensor(b_lo[:, 8, :], aux, b_hi[:, 8, :].bitcast(fp32), ALU.subtract).then_inc(aux_free, 1)
                softmax_b(at, 1)
                softmax_a(at, 2)
                weights_lo(at, 0)
                softmax_b(at, 2)
                softmax_a(at, 3)
                weights_lo(at, 1)
                softmax_b(at, 3)
                wait_tile(dve, at, t0 + 6)
                wait_read(dve, at, t0 + 5)
                read_out(dve.tensor_tensor(G[:, 2:2 + S], banks[:, 2, :], CG, ALU.mult), t0 + 6)
                wait_read(dve, at, t0 + 6)
                tap = [cols[:, bass.ds(i * 3 + (COL["conv"] + j), 1)] for j in range(3)]
                link(dve.tensor_scalar(tmp[:, 0, :], G[:, 0:S], tap[0], None, ALU.mult), at)
                for j in (1, 2):
                    link(dve.scalar_tensor_tensor(out=tmp[:, 0, :], in0=G[:, j:j + S], scalar=tap[j],
                                                  in1=tmp[:, 0, :], op0=ALU.mult, op1=ALU.add), at)
                wait_read(dve, at, t0 + 4)
                link(dve.tensor_tensor(tmp[:, 0, :], tmp[:, 0, :], VB, ALU.mult), at)
                weights_lo(at, 2)
                ada(at, 1)
                weights_lo(at, 3)
                ada(at, 2)
                dve.wait_ge(zc_t, at("one", 1))
                read_out(dve.scalar_tensor_tensor(out=sq[:, 1, :], in0=tmp[:, 1, :], scalar=1.0, in1=banks[:, 3, :],
                                                  op0=ALU.add, op1=ALU.mult), t0 + 7)
                wait_read(dve, at, t0 + 7)
                dve.tensor_tensor(tmp[:, 0, :], tmp[:, 0, :], sq[:, 1, :], ALU.mult).then_inc(cv_out, 1)
                dve.wait_ge(mix_hi, at("two", 1))
                dve.wait_ge(cv_out, at("one", 1))
                dve.scalar_tensor_tensor(out=b_lo[:, bass.ds(i + 4, 1), :].rearrange("p a s -> p (a s)"),
                                         in0=tmp[:, 0, :], scalar=0.5,
                                         in1=b_hi[:, bass.ds(i + 4, 1), :].rearrange("p a s -> p (a s)").bitcast(fp32),
                                         op0=ALU.mult, op1=ALU.subtract).then_inc(mix_ready, 1)
                ada(at, 2)
                dve.wait_ge(o_r, at("one", 1))
                dve.wait_ge(o_copied, at("one", 1))
                dve.wait_ge(mix_ready, at("two", 1))
                link(dve.tensor_tensor(tmp[:, 0, :], sq[:, 0, :], rinv[:, :], ALU.mult), at)
                dve.scalar_tensor_tensor(out=tmp[:, 0, :], in0=tmp[:, 0, :], scalar=gsub, in1=ZA,
                                         op0=ALU.mult, op1=ALU.mult).then_inc(o_out, 1)
                dve.wait_ge(mix_hi, at("two", 2))
                dve.wait_ge(o_out, at("one", 1))
                dve.tensor_tensor(b_lo[:, bass.ds(i, 1), :].rearrange("p a s -> p (a s)"), tmp[:, 0, :],
                                  b_hi[:, bass.ds(i, 1), :].rearrange("p a s -> p (a s)").bitcast(fp32),
                                  ALU.subtract).then_inc(mix_ready, 1)
                ada_out(A0 + 6, 0, at)
            got = linked[0] - base
            assert got == per_link, got
            linked[0] = base + per_link * NH
            steps[0] = 8 * NH

            dve.wait_ge(p_hi, 1)
            dve.tensor_tensor(b_lo[:, 8:10, :].rearrange("p k s -> p (k s)"), PV,
                              b_hi[:, 8:10, :].rearrange("p k s -> p (k s)").bitcast(fp32),
                              ALU.subtract).then_inc(p_ready, 1)
            t0 = TI["out"]
            for n in range(8):
                ada()
                if n >= 3:
                    for m in ((0, 1, 2, 3) if n == 3 else (n,)):
                        dve.wait_ge(sq_ready, 8 + m + 1)
                        read_out(dve.tensor_copy(MIX[:, m, :], banks[:, m % 4, :]), t0 + m)
                        add_square(1, m)
            t1 = TI["ple"]

            def xg_lo(m):
                dve.wait_ge(xg_hi, m + 1)
                dve.tensor_tensor(a_lo[:, m, :], X[:, m, :], a_hi[:, m, :].bitcast(fp32),
                                  ALU.subtract).then_inc(xg_ready, 1)

            dve.wait_ge(r_ready, 2)
            for m in range(KD):
                if m == 0:
                    for b in range(4):
                        wait_read(dve, flat, t0 + 4 + b)
                link(dve.tensor_tensor(tmp[:, m % 2, :], MIX[:, m, :], rinv[:, :], ALU.mult))
                dve.scalar_tensor_tensor(out=X[:, m, :], in0=tmp[:, m % 2, :], scalar=col("post", m), in1=X[:, m, :],
                                         op0=ALU.mult, op1=ALU.add).then_inc(x_new, 1)
                dve.wait_ge(sq_ready, 16 + m + 1)
                add_square(2, m)
                dve.wait_ge(x_new, m + 1)
                if m >= 3:
                    xg_lo(m - 3)
                if m == 2:
                    ada_out(AUX["ada4"], 4)
            for m in range(KD - 3, KD):
                xg_lo(m)
            t0 = TI["gate"]
            ada(k=4)
            dve.wait_ge(r_ready, 3)
            dve.wait_ge(aux_free, AUX["body"] + 7 * NH)
            scale_columns(1, col("mix", 0, KD), 1)
            for m in range(4, KD):
                wait_read(dve, flat, t1 + m)
            for m in range(KD):
                dve.scalar_tensor_tensor(out=E[:, m, :], in0=E[:, m, :], scalar=gple[:, m:m + 1], in1=rinv[:, :],
                                         op0=ALU.mult, op1=ALU.mult).then_inc(e_ready, 1)
            ada(k=2)
            for n in range(8):
                if n >= 3:
                    for m in ((0, 1, 2, 3) if n == 3 else (n,)):
                        wait_read(dve, flat, t0 + m)
                        dve.wait_ge(e_ready, m + 1)
                        link(dve.scalar_tensor_tensor(out=E[:, m, :], in0=GT[m % 4], scalar=1.0,
                                                      in1=E[:, m, :], op0=ALU.add, op1=ALU.mult))
                        dve.tensor_tensor(X[:, m, :], X[:, m, :], E[:, m, :], ALU.add).then_inc(x_new, 1)
                        dve.wait_ge(x_new, KD + m + 1)
                        gained("four", m, gain(1))
                        if m <= 5:
                            add_square(3, m - 1)
                        if m >= 5:
                            add_square(3, m)

            td = TI["dft1"]

            def z_group(g):
                for z in range(2 * g, 2 * g + 2):
                    dve.wait_ge(z_hi, z + 1)
                    read_out(dve.tensor_tensor(b_lo[:, z, :], banks[:, (td + z) % 4, :],
                                               b_hi[:, z, :].bitcast(fp32), ALU.subtract), td + z)

            norm_apply("four", 1, vector(0), lambda m: z_group((m - 3) // 2) if m in (3, 5, 7) else None)
            z_group(3)
            t0 = TI["dft2"]
            def fourier_lo(g):
                for n in range(2):
                    dve.wait_ge(f_hi, 2 * g + n + 1)
                    dve.tensor_tensor(a_lo[:, 2 * g + n, :], FM[:, 2 * (g % 2) + n, :],
                                      a_hi[:, 2 * g + n, :].bitcast(fp32), ALU.subtract).then_inc(f_ready, 1)

            ada(k=2)
            for g in range(NH):
                tz, tc = t0 + 2 * g, t0 + 2 * g + 1
                zs, flipped, cs = FU[:, 2 * (g % 2), :], FU[:, 2 * (g % 2) + 1, :], banks[:, tc % 4, :]
                A, B = FM[:, 2 * (g % 2), :], FM[:, 2 * (g % 2) + 1, :]
                low, mirrored, back = slice(0, S // 2 + 1), slice(S // 2 + 1, S), slice(S // 2 - 1, 0, -1)
                wait_read(dve, flat, tz)
                wait_tile(dve, flat, tc)
                if g >= 2:
                    dve.wait_ge(f_ready, 2 * (g - 1))
                dve.scalar_tensor_tensor(out=A[:, low], in0=zs[:, low], scalar=minus_but0, in1=cs[:, low],
                                         op0=ALU.mult, op1=ALU.add)
                dve.scalar_tensor_tensor(out=A[:, mirrored], in0=zs[:, back], scalar=but0, in1=cs[:, back],
                                         op0=ALU.mult, op1=ALU.add).then_inc(f_sum, 1)
                dve.scalar_tensor_tensor(out=B[:, low], in0=cs[:, low], scalar=but0, in1=zs[:, low],
                                         op0=ALU.mult, op1=ALU.add)
                read_out(dve.scalar_tensor_tensor(out=B[:, mirrored], in0=cs[:, back], scalar=but0,
                                                  in1=flipped[:, back], op0=ALU.mult, op1=ALU.add), tc)
                if g:
                    fourier_lo(g - 1)
                if g == 1:
                    ada_out(AUX["ada5"], 5)
                if 1 <= g < NH - 1:
                    ada(k=2)
            fourier_lo(NH - 1)
            t0 = TI["fout"]
            ada(k=4)
            ada_out(AUX["ada6"], 6)
            ada(k=4)
            for n in range(8):
                if n >= 3:
                    if n == 3:
                        dve.wait_ge(aux_free, AUX["ada5"] + 1)
                        scale_columns(2, col("ffn", 0, KD), 4)
                    residuals(t0, (0, 1, 2, 3) if n == 3 else (n,), 2, 4, "ffn0", 2)

            def up_body(at, t, j):
                for n in range(2):
                    dve.wait_ge(hid_t, at("hid", j + n + 1))
                    g, u = (t + 2 * n) % 4, (t + 2 * n + 1) % 4
                    read_out(dve.scalar_tensor_tensor(out=SG[:, n, :], in0=T2[:, n, :], scalar=1.0,
                                                      in1=banks[:, g, :], op0=ALU.add, op1=ALU.mult), g)
                    wait_tile(dve, at, t + 2 * n + 1)
                    wait_read(dve, at, t + 2 * n)
                    dve.tensor_tensor(HD[:, n, :], SG[:, n, :], banks[:, u, :], ALU.mult).then_inc(hid_f, 1)
                    dve.wait_ge(hid_hi, at("hid", j + n + 1))
                    k = j % FT % HALF[0] + n
                    if at.i is None:
                        hi, lo = b_hi[:, k, :], b_lo[:, k, :]
                    else:
                        hi, lo = (b[:, bass.ds(at("hid", k), 1), :].rearrange("p a s -> p (a s)") for b in (b_hi, b_lo))
                    read_out(dve.scalar_tensor_tensor(out=lo, in0=HD[:, n, :], scalar=0.5, in1=hi.bitcast(fp32),
                                                      op0=ALU.mult, op1=ALU.subtract), u)

            def swiglu(layer, v, a_in, with_ada):
                g0 = 6 * layer
                norm_apply(f"ffn{layer}", a_in, vector(g0 + 3))
                for part, n_hid in zip("ab", HALF):
                    t = TI[f"up{layer}{part}"]
                    j = layer * FT + (0 if part == "a" else HALF[0])
                    first = 1 if part == "a" else 0
                    if first:
                        if with_ada:
                            ada(k=4)
                            ada_out(AUX["ada7"], 7)
                        up_body(flat, t, j)
                        if with_ada:
                            ada(flat, 8)
                    with dve.Fori(0, n_hid // 2 - first) as i:
                        at = At(i, tile=4, bank=1, hid=2, ada=8, adaslot=64, aux=1, eight=8)
                        up_body(at, t + 4 * first, j + 2 * first)
                        if first and with_ada:
                            ada_out(AUX["ada"], 8, at)
                            ada(at, 8)
                    if first and with_ada:
                        ada_out(AUX["ada"] + 5, 13)
                    t = TI[f"down{layer}{part}"]
                    if part == "a":
                        for m in range(KD):
                            residual(flat, t + m, m, g0 + 5)
                    elif layer == 0:
                        dve.wait_ge(aux_free, AUX["ada"] + 6)
                        scale_columns(3, col("mix", KD, KD), 7)
                        residuals(t, range(KD), g0 + 5, v, "rnorm", 3)
                    else:
                        residuals(t, range(KD), g0 + 5, v)

            swiglu(0, 5, 2, True)

            norm_apply("rnorm", 3, vector(6))
            dve.wait_ge(rope_in, 16)

            def rotate(at, t):
                def rot_lo(n):
                    dve.wait_ge(rot_hi, at("four", n + 1))
                    dve.tensor_tensor(b_lo[:, n, :], RT[:, 1 + 2 * (n % 2), :], b_hi[:, n, :].bitcast(fp32),
                                      ALU.subtract).then_inc(rot_ready, 1)

                for n in range(2):
                    x1, x2 = KQ[:, 2 * n, :], KQ[:, 2 * n + 1, :]
                    wait_read(dve, at, t + 2 * n)
                    wait_read(dve, at, t + 2 * n + 1)
                    if n:
                        rot_lo(0)
                    dve.tensor_tensor(RT[:, 0, :], x1, COS, ALU.mult)
                    if n:
                        dve.wait_ge(rot_ready, at("four", 1))
                    link(dve.tensor_tensor(RT[:, 1, :], x2, SIN, ALU.mult), at)
                    dve.tensor_tensor(RT[:, 1, :], RT[:, 0, :], RT[:, 1, :], ALU.subtract).then_inc(rot, 1)
                    if n:
                        rot_lo(1)
                    dve.tensor_tensor(RT[:, 2, :], x1, SIN, ALU.mult)
                    if n:
                        dve.wait_ge(rot_ready, at("four", 2))
                    link(dve.tensor_tensor(RT[:, 3, :], x2, COS, ALU.mult), at)
                    dve.tensor_tensor(RT[:, 3, :], RT[:, 2, :], RT[:, 3, :], ALU.add).then_inc(rot, 1)
                rot_lo(2)
                rot_lo(3)

            def gate(at, n, tt):
                dve.wait_ge(gg_t, at("four", n + 1))
                read_out(dve.scalar_tensor_tensor(out=GG[:, n, :], in0=RT[:, n, :], scalar=1.0,
                                                  in1=banks[:, tt % 4, :], op0=ALU.add, op1=ALU.mult), tt)

            def head(at, t):
                for n in range(5):
                    if n < 4:
                        wait_read(dve, at, t + n)
                        dve.tensor_scalar(vmean[:, n:n + 1], vsum[:, n:n + 1], -1.0 / (4 * P), None,
                                          ALU.mult).then_inc(v_mean, 1)
                    if n:
                        dve.wait_ge(vv_hi, at("four", n))
                        dve.scalar_tensor_tensor(out=b_lo[:, 3 + n, :], in0=VR[:, (n - 1) % 2, :],
                                                 scalar=vmean[:, n - 1:n], in1=b_hi[:, 3 + n, :].bitcast(fp32),
                                                 op0=ALU.add, op1=ALU.subtract).then_inc(v_ready, 1)
                t += 4
                for n in range(3):
                    gate(at, n, t + n)
                t += 3
                dve.wait_ge(dec_in, at("sixteen", 16))

                def score_lo(n):
                    dve.wait_ge(pd_hi, at("four", n + 1))
                    read_out(dve.tensor_tensor(b_lo[:, 8 + n, :], tmp[:, n % 2, :], b_hi[:, 8 + n, :].bitcast(fp32),
                                               ALU.subtract), t + n)

                for n in range(4):
                    wait_tile(dve, at, t + n)
                    if n >= 2:
                        wait_read(dve, at, t + n - 2)
                    dve.tensor_tensor(tmp[:, n % 2, :], banks[:, (t + n) % 4, :], DEC[:, 3 * P - P * n:3 * P - P * n + S],
                                      ALU.mult).then_inc(pd, 1)
                    if n:
                        dve.wait_ge(pd, at("four", n))
                        score_lo(n - 1)
                dve.wait_ge(pd, at("four", 4))
                score_lo(3)
                gate(at, 3, t + 4)

            def group_norm(at, t):
                def add_sq(n):
                    dve.wait_ge(y_sq, at("four", n + 1))
                    if n >= 2:
                        dve.wait_ge(y_qs, at("three", n - 1))
                    dve.tensor_tensor(sqsum[:, :], sqsum[:, :], sq[:, n % 2, :], ALU.add).then_inc(y_qs, 1)

                for n in range(4):
                    wait_tile(dve, at, t + n)
                    read_out(dve.tensor_copy(Y[:, n, :], banks[:, (t + n) % 4, :]), t + n)
                    if n >= 2:
                        add_sq(n - 1)
                add_sq(3)
                for q in (t - 8, t - 7, t - 6, t - 1):
                    wait_read(dve, at, q)
                for n in range(4):
                    link(dve.tensor_tensor(GG[:, n, :], GG[:, n, :], Y[:, n, :], ALU.mult), at)
                dve.wait_ge(y_r, at("one", 1))
                for n in range(4):
                    dve.tensor_tensor(Y[:, n, :], GG[:, n, :], rinv[:, :], ALU.mult).then_inc(y_f, 1)
                for n in range(4):
                    dve.wait_ge(y_hi, at("four", n + 1))
                    dve.scalar_tensor_tensor(out=b_lo[:, 8 + n, :], in0=Y[:, n, :], scalar=0.5,
                                             in1=b_hi[:, 8 + n, :].bitcast(fp32), op0=ALU.mult,
                                             op1=ALU.subtract).then_inc(y_ready, 1)

            PER = dict(tile=28, bank=7, aux=1, four=4, three=3, one=1, sixteen=16)
            first, t0 = TI["ret"], TI["retbody"]
            rotate(flat, first)
            head(flat, first + 4)
            per_link = 4 + 4
            base = linked[0]
            with dve.Fori(0, NH - 1) as i:
                at = Head(i, link=per_link, **PER)
                group_norm(At(i, link=per_link, **PER), t0 - 4)
                rotate(at, t0)
                for m in range(KD):
                    residual(at, t0 + 4 + m, m, 8)
                head(at, t0 + 12)
            assert linked[0] - base == per_link, linked[0] - base
            linked[0] = base + per_link * (NH - 1)
            group_norm(At(NH - 1, link=0, **PER), t0 - 4)
            t0 = TI["retout"]
            scale_columns(4, col("ffn", KD, KD), 10)
            residuals(t0, range(KD), 8, 6, "ffn1", 4, True)
            swiglu(1, 7, 4, False)
            link(dve.scalar_tensor_tensor(out=gs[:, 0:KD], in0=mod[:, 13 * KD:14 * KD], scalar=1.0,
                                          in1=col("final", 0, KD), op0=ALU.add, op1=ALU.mult))
            dve.wait_ge(r_ready, 8)
            for m in range(KD):
                dve.scalar_tensor_tensor(out=X[:, m, :], in0=X[:, m, :], scalar=gs[:, m:m + 1], in1=rinv[:, :],
                                         op0=ALU.mult, op1=ALU.mult).then_inc(x_scaled, 1)

        @block.tensor
        def _(pe):
            pos = [0, 0]

            def chunk_begins(at, width):
                c, q = pos
                slot = c % RING
                begins = q == 0
                if begins:
                    pe.wait_ge(wlo, at("chunk", c + 1))
                ap = slice(q * P, q * P + width)
                pos[1] += width // P
                if pos[1] == 8:
                    pos[0], pos[1] = c + 1, 0
                return begins and c > 0, w_hi[:, slot, ap], w_lo[:, slot, ap]

            def mul(at, bank, x_hi, x_lo, first, last, done=False):
                begins, hi, lo = chunk_begins(at, P)
                out = banks[:, bank, :]
                mm = pe.matmul(out, lo, x_hi, start=first, stop=False)
                if begins:
                    mm.then_inc(w_used, 1)
                pe.matmul(out, hi, x_lo, start=False, stop=False)
                mm = pe.matmul(out, hi, x_hi, start=False, stop=last)
                if done:
                    mm.then_inc(tile_ready, 1)

            def wait_bank(at, t):
                if t >= 4:
                    pe.wait_ge(bank_read[t % 4], at("bank", t // 4))

            def gemm(at, t0, M, ks, rhs, ready=None, first_outer=True, hook=None, norm=None):
                seen, opened = set(), set()
                order = gemm_order(len(ks), M, ks, first_outer)
                n_of = {}
                if norm is not None:
                    pe.wait_ge(h_hi, KD * norm + 1)
                    x_hi, x_lo = rhs(ks[0])
                    his = []
                    for m in range(4):
                        wait_bank(at, t0 + m)
                        begins, hi, lo = chunk_begins(at, P)
                        mm = pe.matmul(banks[:, (t0 + m) % 4, :], lo, x_hi, start=True, stop=False)
                        if begins:
                            mm.then_inc(w_used, 1)
                        pe.matmul(banks[:, (t0 + m) % 4, :], hi, x_hi, start=False, stop=False)
                        his.append(hi)
                        opened.add(m)
                        n_of[m] = 1
                    ready(ks[0])
                    seen.add(ks[0])
                    for m in range(4):
                        pe.matmul(banks[:, (t0 + m) % 4, :], his[m], x_lo, start=False, stop=False)
                for n, (k, m) in enumerate(order):
                    if norm is not None and n < 4:
                        continue
                    if ready and k not in seen:
                        seen.add(k)
                        ready(k)
                    if m not in opened:
                        opened.add(m)
                        wait_bank(at, t0 + m)
                        n_of[m] = 0
                    hi, lo = rhs(k)
                    n_of[m] += 1
                    mul(at, (t0 + m) % 4, hi, lo, n_of[m] == 1, n_of[m] == len(ks), n_of[m] == len(ks))
                    if hook:
                        hook(n)

            def rhs_a(k):
                return a_hi[:, k, :], a_lo[:, k, :]

            def rhs_b(k):
                return b_hi[:, k, :], b_lo[:, k, :]

            def stats(at, u):
                if u > 0:
                    pe.wait_ge(aux_free, at("aux", u))
                pe.matmul(aux, ones[:, :], sqsum[:, :], start=True, stop=True).then_inc(aux_ready, 1)

            def keep_warm(n=1):
                for _ in range(n):
                    pe.matmul(banks[:, 6, :], ones[:, :], cols[:, 0:S], start=True, stop=True)

            def norm_stats(v, name):
                pe.wait_ge(sq_added, 6 * v + 6)
                if AUX[name] > 0:
                    pe.wait_ge(aux_free, AUX[name])
                pe.matmul(aux, ones[:, :], sqsum[:, :], start=True, stop=False)
                pe.wait_ge(sq_ready, 8 * v + 8)
                pe.matmul(aux, ones[:, :], sq[:, 1, :], start=False, stop=True).then_inc(aux_ready, 1)
                if name not in ("post", "ple", "final"):
                    keep_warm(2 if name == "four" else 1)

            def ada_reduce(at, u, g):
                pe.wait_ge(ada_sum, at("ada", KD * (g + 1)))
                pe.wait_ge(aux_free, at("aux", u))
                for f in range(KD):
                    mm = pe.matmul(aux[:, f:f + 1], ada_acc[:, f * P:(f + 1) * P], ones[:, 0:1], start=True, stop=True)
                mm.then_inc(aux_ready, 1)

            pe.wait_ge(const, 1)
            pe.wait_ge(cols_in, 16)
            norm_stats(0, "pre")
            A0, t0 = AUX["body"], TI["body"]

            def scores(at, b):
                n = (b + 1) * P
                if b == 0:
                    wait_read(pe, at, t0)
                    wait_read(pe, at, t0 + 1)
                else:
                    pe.wait_ge(sc_read, at("eight", 2 * b))
                for m in range(2):
                    p = slice(64 * m, 64 * m + 64)
                    mm = pe.matmul(banks[:, 5 + m, 0:n], Q[p, b * P:(b + 1) * P], K[p, 0:n], start=True, stop=True)
                mm.then_inc(sc_ready, 1)

            def transpose_v(at):
                wait_read(pe, at, t0 + 2)
                pe.wait_ge(aux_free, at("aux", A0))
                for s in range(TB):
                    mm = pe.transpose(aux[:, s * P:(s + 1) * P], VB[:, s * P:(s + 1) * P], ident)
                mm.then_inc(aux_ready, 1)

            def transpose_w(at, b):
                pe.wait_ge(w_ready, at("unit", b + 1))
                pe.wait_ge(aux_free, at("aux", A0 + 1 + b))
                for s in range(b + 1):
                    mm = pe.transpose(aux[:, s * P:(s + 1) * P], WT[:, b % 2, s * P:(s + 1) * P], ident)
                mm.then_inc(aux_ready, 1)

            def values(at, b):
                pe.wait_ge(aux_free, at("aux", A0 + 2 + b))
                out = banks[:, 4, b * P:(b + 1) * P]
                for s in range(b + 1):
                    c = slice(s * P, (s + 1) * P)
                    v1, v2 = b_hi[:, 8, c], b_lo[:, 8, c]
                    w1, w2 = b_hi[:, 9 + b % 2, c], b_lo[:, 9 + b % 2, c]
                    pe.matmul(out, v2, w1, start=(s == 0), stop=False)
                    pe.matmul(out, v1, w2, start=False, stop=False)
                    mm = pe.matmul(out, v1, w1, start=False, stop=(s == b))
                if b == TB - 1:
                    mm.then_inc(pv_ready, 1)


            def body_head(at, n, hook=None):
                gemm(at, t0 + n, 1, range(KD), rhs_a, None, False, hook)

            def body_rest(at):
                scores(at, 1)
                transpose_v(at)
                gemm(at, t0 + 4, 1, range(KD), rhs_a, None, False)
                scores(at, 2)
                transpose_w(at, 0)
                gemm(at, t0 + 5, 1, range(KD), rhs_a, None, False)
                scores(at, 3)
                transpose_w(at, 1)
                values(at, 0)
                gemm(at, t0 + 6, 1, range(KD), rhs_a, None, False)
                transpose_w(at, 2)
                values(at, 1)

                def middle(n):
                    if n == 3:
                        transpose_w(at, 3)
                        values(at, 2)
                gemm(at, t0 + 7, 1, range(KD), rhs_a, None, False, middle)
                values(at, 3)

            def body_tail(at, n):
                if n == 3:
                    pe.wait_ge(o_sq, at("one", 1))
                    stats(at, A0 + 5)
                if n == 7:
                    ada_reduce(at, A0 + 6, 0)

            per = dict(chunk=8, tile=8, bank=2, aux=7, unit=4, one=1, two=2, eight=8, ada=8)
            gemm(flat, t0, 4, range(KD), rhs_a, lambda k: pe.wait_ge(a_ready, k + 1), norm=0)
            scores(flat, 0)
            with pe.Fori(0, NH - 1) as i:
                at = At(i, **per)
                body_rest(at)
                for n in range(8, 12):
                    body_head(at, n, (lambda q: body_tail(at, q)) if n == 8 else None)
                    if n == 10:
                        for q in (8, 9):
                            wait_read(pe, at, t0 + q)
                        for m in range(2):
                            p = slice(64 * m, 64 * m + 64)
                            mm = pe.matmul(banks[:, 5 + m, 0:P], Q[p, 0:P], K[p, 0:P], start=True, stop=True)
                        mm.then_inc(sc_ready, 1)
            last = At(NH - 1, **per)
            pos[0] = CH["body"] + 4
            body_rest(last)
            pos[0] = CH["out"]
            keep_warm()

            def mix_wait(k):
                pe.wait_ge(mix_ready, 8 if k == 3 else 7)
            gemm(flat, TI["out"], KD, ATT_KS, rhs_b, mix_wait, hook=lambda n: body_tail(last, n))
            pe.wait_ge(p_ready, 1)

            def gemm_e(t0):
                for m in range(KD):
                    wait_bank(flat, t0 + m)
                    for k in range(2):
                        mul(flat, (t0 + m) % 4, b_hi[:, 8 + k, :], b_lo[:, 8 + k, :], k == 0, k == 1, k == 1)
                    if m == 1:
                        norm_stats(1, "post")
                    if m == 3:
                        ada_reduce(flat, AUX["ada4"], 4)
            gemm_e(TI["ple"])
            def gate_wait(k):
                pe.wait_ge(xg_ready, k + 1)

            def gate_hook(n):
                if n == 15:
                    norm_stats(2, "ple")
            gemm(flat, TI["gate"], KD, range(KD), rhs_a, gate_wait, True, gate_hook)
            norm_stats(3, "four")
            t0 = TI["dft1"]
            slot = CH["dft1"] % RING
            for g in range(NH):
                pe.wait_ge(a_ready, KD + 2 * g + 2)
                for tt in range(TB):
                    t = t0 + 2 * g + tt // 2
                    if tt % 2 == 0:
                        wait_bank(flat, t)
                    for k in range(2):
                        begins = g == 0 and tt == 0 and k == 0
                        if begins:
                            pe.wait_ge(wlo, CH["dft1"] + 1)
                        xh, xl = (a[:, 2 * g + k, tt * P:(tt + 1) * P] for a in (a_hi, a_lo))
                        wh, wl = (w[:, slot, k * S:k * S + 2 * P] for w in (w_hi, w_lo))
                        out = banks[:, t % 4, (tt % 2) * 2 * P:(tt % 2 + 1) * 2 * P]
                        mm = pe.matmul(out, xh, wl, start=(k == 0), stop=False)
                        if begins:
                            mm.then_inc(w_used, 1)
                        pe.matmul(out, xl, wh, start=False, stop=False)
                        mm = pe.matmul(out, xh, wh, start=False, stop=(k == 1))
                    if tt % 2:
                        mm.then_inc(tile_ready, 1)
            td, t1 = t0, TI["dft2"]
            c0 = CH["dft2"]
            begun = set()

            def table(g, tt, cos):
                c = c0 + 2 * cos + tt // 2
                new, last = c not in begun, g == NH - 1 and tt % 2 == 0 and c > c0
                if new:
                    begun.add(c)
                    pe.wait_ge(wlo, c + 1)
                w = slice((tt % 2) * S, (tt % 2) * S + NF)
                return new and c == c0 or last, w_hi[:, c % RING, w], w_lo[:, c % RING, w]

            def token_sums(out, g, tt, cs, used, wh, wl):
                z, o = 2 * g + tt // 2, (tt % 2) * 2 * P
                Zh, Zl = (b[:, z, o + cs.start:o + cs.stop] for b in (b_hi, b_lo))
                mm = pe.matmul(out, Zh, wl, start=(tt == 0), stop=False)
                if used:
                    mm.then_inc(w_used, 1)
                pe.matmul(out, Zl, wh, start=False, stop=False)
                return pe.matmul(out, Zh, wh, start=False, stop=(tt == TB - 1))

            for g in range(NH):
                tz, tc = t1 + 2 * g, t1 + 2 * g + 1
                for n in range(2):
                    wait_read(pe, flat, td + 2 * g + n)
                wait_bank(flat, tz)
                sine, cosine = banks[:, tz % 4, 0:NF], banks[:, tc % 4, 0:NF]
                if g == 2:
                    ada_reduce(flat, AUX["ada5"], 5)
                for tt in range(TB):
                    token_sums(sine, g, tt, slice(P, 2 * P), *table(g, tt, 0))
                wait_bank(flat, tc)
                for tt in range(TB):
                    used, wh, wl = table(g, tt, 1)
                    mm = token_sums(sine[0:1, :], g, tt, slice(P, P + 1), used, wh, wl)
                    if tt == TB - 1:
                        mm.then_inc(tile_ready, 1)
                    mm = token_sums(cosine, g, tt, slice(0, P), False, wh, wl)
                mm.then_inc(tile_ready, 1)
            pos[0] = CH["fout"]
            gemm(flat, TI["fout"], KD, range(KD), rhs_a, lambda k: pe.wait_ge(f_ready, k + 1),
                 hook=lambda n: ada_reduce(flat, AUX["ada6"], 6) if n == 21 else None)
            norm_stats(4, "ffn0")

            def swiglu(layer, a_in, with_ada, v, name):
                for part, n_hid in zip("ab", HALF):
                    c, t = CH[f"up{layer}{part}"], TI[f"up{layer}{part}"]
                    assert pos[0] == c
                    first = 1 if part == "a" else 0
                    if first:
                        gemm(flat, t, 4, range(KD), rhs_a, lambda k: pe.wait_ge(a_ready, KD * a_in + k + 1),
                             hook=lambda n: ada_reduce(flat, AUX["ada7"], 7) if n == 23 and with_ada else None,
                             norm=a_in)
                    with pe.Fori(0, n_hid // 2 - first) as i:
                        at = At(i, chunk=4, tile=4, bank=1, ada=8, aux=1)
                        gemm(at, t + 4 * first, 4, range(KD), rhs_a, None, False)
                        if first and with_ada:
                            ada_reduce(at, AUX["ada"], 8)
                    pos[0] = CH[f"down{layer}{part}"]
                    base_t = TI[f"down{layer}{part}"]
                    def last_ada(n):
                        if n == 39:
                            ada_reduce(flat, AUX["ada"] + 5, 13)
                    gemm(flat, base_t, KD, range(n_hid), rhs_b, lambda k: wait_read(pe, flat, t + 2 * k + 1),
                         hook=last_ada if first and with_ada else None)
                norm_stats(v, name)

            swiglu(0, 2, True, 5, "rnorm")

            def token_major(at, t0):
                for k in range(KD):
                    for tt in range(TB):
                        if k == 0:
                            wait_bank(at, t0 + tt)
                        if tt == 0:
                            begins, wh, wl = chunk_begins(at, S)
                        c = slice(tt * P, (tt + 1) * P)
                        out = banks[:, (t0 + tt) % 4, :]
                        mm = pe.matmul(out, a_hi[:, k, c], wl, start=(k == 0), stop=False)
                        if begins and tt == 0:
                            mm.then_inc(w_used, 1)
                        pe.matmul(out, a_lo[:, k, c], wh, start=False, stop=False)
                        mm = pe.matmul(out, a_hi[:, k, c], wh, start=False, stop=(k == KD - 1))
                        if k == KD - 1:
                            mm.then_inc(tile_ready, 1)

            def group_stats(at):
                pe.wait_ge(y_qs, at("three", 3))
                stats(at, AUX["ret"])

            def head(at, t):
                token_major(at, t)
                t += 4
                for n in range(3):
                    gemm(at, t + n, 1, range(KD), rhs_a, None, False)
                t += 3
                for s in range(TB):
                    wait_bank(at, t + s)
                    if s == 0:
                        pe.wait_ge(rot_ready, at("four", 4))
                    out = banks[:, (t + s) % 4, :]
                    for d in range(2):
                        c = slice(s * P, (s + 1) * P)
                        pe.matmul(out, b_lo[:, d, c], b_hi[:, 2 + d, :], start=(d == 0), stop=False)
                        pe.matmul(out, b_hi[:, d, c], b_lo[:, 2 + d, :], start=False, stop=False)
                        mm = pe.matmul(out, b_hi[:, d, c], b_hi[:, 2 + d, :], start=False, stop=(d == 1))
                    mm.then_inc(tile_ready, 1)
                ts = t
                t += 4
                gemm(at, t, 1, range(KD), rhs_a, None, False)
                t += 1
                pe.wait_ge(v_ready, at("four", 4))
                for n in range(4):
                    wait_bank(at, t + n)
                    out = banks[:, (t + n) % 4, :]
                    for s in range(TB):
                        if n == 0:
                            wait_read(pe, at, ts + s)
                        c = slice(n * P, (n + 1) * P)
                        pe.matmul(out, b_lo[:, 4 + s, c], b_hi[:, 8 + s, :], start=(s == 0), stop=False)
                        pe.matmul(out, b_hi[:, 4 + s, c], b_lo[:, 8 + s, :], start=False, stop=False)
                        mm = pe.matmul(out, b_hi[:, 4 + s, c], b_hi[:, 8 + s, :], start=False, stop=(s == 3))
                    mm.then_inc(tile_ready, 1)

            gemm(flat, TI["ret"], 4, range(KD), rhs_a, lambda k: pe.wait_ge(a_ready, 3 * KD + k + 1),
                 norm=3)
            head(flat, TI["ret"] + 4)
            PER = dict(chunk=16, tile=28, bank=7, aux=1, four=4, three=3, one=1)
            t0 = TI["retbody"]
            with pe.Fori(0, NH - 1) as i:
                at, prev = Head(i, **PER), At(i, **PER)
                gemm(at, t0, 4, range(KD), rhs_a,
                     hook=lambda n: group_stats(prev) if n == 7 else None)
                gemm(at, t0 + 4, KD, range(4), lambda k: rhs_b(8 + k),
                     lambda k: pe.wait_ge(y_ready, prev("four", k + 1)))
                head(at, t0 + 12)
            keep_warm()
            group_stats(At(NH - 1, **PER))
            keep_warm()
            pos[0] = CH["retout"]
            gemm(flat, TI["retout"], KD, range(4), lambda k: rhs_b(8 + k),
                 lambda k: pe.wait_ge(y_ready, 4 * (NH - 1) + k + 1))
            keep_warm()
            norm_stats(6, "ffn1")
            swiglu(1, 4, False, 7, "final")


def weight_stream(w_in, w_out, w_ple_proj, w_ple_gate, w_fourier_out, w_ret_in, w_ret_out, w_ffn_in, w_ffn_out, dfts):
    import numpy as np
    tiles = []
    fourier_rows = np.concatenate([g * 256 + np.r_[0:129, 255:128:-1] for g in range(NH)])

    def tile(w, k, c):
        tiles.append(w[k * P:(k + 1) * P, c:c + P])

    def gemm(w, K, M, ks=None, first_outer=True, k0=0, cols=None):
        for k, m in gemm_order(K, M, ks, first_outer):
            tile(w, k0 + k, cols[m] if cols else m * P)

    for j in range(NH):
        gemm(w_in, KD, 8, None, j == 0, 0, [part * 512 + j * P for part in range(8)])
    gemm(w_out, KD, KD, ATT_KS)
    gemm(w_ple_proj, 2, KD, None, False)
    gemm(w_ple_gate, KD, KD)
    for w in dfts:
        for k in range(w.shape[0] // P):
            for c in range(4):
                tile(w, k, c * P)
    gemm(w_fourier_out[fourier_rows], KD, KD)

    def swiglu(layer):
        k0 = 0
        for n_hid in HALF:
            for b in range(n_hid // 2):
                f = k0 + 2 * b
                cols = [f * P, FF + f * P, (f + 1) * P, FF + (f + 1) * P]
                gemm(w_ffn_in[layer], KD, 4, None, k0 == 0 and b == 0, 0, cols)
            gemm(w_ffn_out[layer], n_hid, KD, None, True, k0)
            k0 += n_hid

    swiglu(0)
    for h in range(NH + 1):
        if h < NH:
            gemm(w_ret_in, KD, 4, None, True, 0, [1024 + h * 256, 1024 + h * 256 + P, h * 256, h * 256 + P])
        if h:
            gemm(w_ret_out, 4, KD, None, True, 4 * (h - 1))
        if h < NH:
            for k in range(KD):
                for c in range(4):
                    tile(w_ret_in, k, 2048 + h * 512 + c * P)
            gemm(w_ret_in, KD, 4, None, False, 0, [4096 + h * 512 + n * P for n in range(4)])
    swiglu(1)
    assert len(tiles) == 8 * N_CHUNK, (len(tiles), 8 * N_CHUNK)
    out = np.empty((N_CHUNK, P, 8, P), np.float32)
    for n, t in enumerate(tiles):
        out[n // 8, :, n % 8] = t
    return out.reshape(N_CHUNK, P, 1024)


def tables():
    import numpy as np
    j = np.arange(256)
    ang = 2 * np.pi * (np.outer(j, j) % 256) / 256
    scale = (S * 256) ** -0.5
    feat = np.zeros((256, S))
    feat[:, :256] = np.concatenate([np.cos(ang[:, :129]), np.sin(ang[:, 1:P])], 1) * scale
    t = np.arange(S)
    ang = 2 * np.pi * (np.outer(t, t) % S) / S
    dfts = [a.astype(np.float32) for a in (feat, np.sin(ang), np.cos(ang))]
    p, u = np.arange(P)[:, None], np.arange(S)[None, :] - 3 * P
    dist = np.where(u // 64 <= p // 64, -np.abs(p - u).astype(np.float64), -1e30).astype(np.float32)
    inv = np.float32(10000.0) ** (-np.arange(P, dtype=np.float32) / np.float32(P))
    a = (inv[:, None] * t[None, :].astype(np.float32)).astype(np.float32)
    rope = np.concatenate([np.cos(a), np.sin(a)], 1).astype(np.float32)
    h = np.arange(NH)[:, None, None]
    d = np.arange(896)[None, None, :] - 3 * P - np.arange(P)[None, :, None]
    fwd, bwd = np.log1p(-2.0 ** (-5.0 - h)), np.log1p(-2.0 ** (-5.0 - (NH - 1 - h)))
    decay = (np.where(d >= 0, np.exp(d * fwd), np.exp(-d * bwd)) / 16).astype(np.float32)
    return dfts, dist, rope, decay


def kernel(**inputs):
    import numpy as np
    import concourse.bacc as bacc
    from concourse.bass_utils import run_bass_kernel_spmd as run
    a = {k: np.asarray(v) for k, v in inputs.items()}
    dfts, dist, rope, decay = tables()
    stream = weight_stream(a["w_in"][0], a["w_out"][0], a["w_ple_proj"][0], a["w_ple_gate"][0],
                           a["w_fourier_out_2"][0], a["w_ret_in_2"][0], a["w_ret_out_2"][0], a["w_ffn_in_2"],
                           a["w_ffn_out_2"], dfts)

    def tokens(x):
        return np.ascontiguousarray(x.T.reshape(-1, P, S).transpose(1, 0, 2)).reshape(P, -1)

    def vec(v):
        return v.reshape(-1, P).T

    def groups(w):
        return w.reshape(KD, P, -1, D).transpose(2, 0, 1, 3).reshape(-1, P, D)

    ada = np.concatenate([groups(a["w_ada_2"][0]), groups(a["w_ada_2"][1]), groups(a["w_ada_final_2"])])
    conv = a["conv_w"][0].reshape(3, NH, P).transpose(2, 1, 0).reshape(P, 3 * NH)
    lam = np.concatenate([a[n][0] for n in ("lambda_q1", "lambda_q2", "lambda_k1", "lambda_k2")])
    slopes = np.float32(2.0) ** (-2.0 * np.arange(1, NH + 1, dtype=np.float32))
    cols = np.concatenate([
        vec(a["pre_norm_gain"][0]), vec(a["post_norm_gain"][0]), vec(a["ple_norm_gain"][0]),
        vec(a["final_norm_g_2"]), vec(a["subln_gain"][0]), conv, vec(a["c_2"][0]), vec(a["b_ada_2"].reshape(-1)),
        vec(a["b_ada_final_2"]), vec(a["norm_mix_g_2"].reshape(-1)), vec(a["norm_ffn_g_2"].reshape(-1)),
        np.broadcast_to(lam, (P, 256)), np.broadcast_to(slopes, (P, NH)), np.eye(P, dtype=np.float32),
    ], 1)
    assert cols.shape == (P, NCOL)
    data = dict(W=stream, ADA=np.ascontiguousarray(ada), XT=tokens(a["x"][0]), PT=tokens(a["p"][0, 0]),
                COLS=np.ascontiguousarray(cols), DIST=dist, ROPE=rope, DECAY=decay)
    nc = bacc.Bacc("TRN2", target_bir_lowering=False, num_devices=1)
    aps = {k: nc.dram_tensor(f"in_{k}", v.shape, mybir.dt.float32, kind="ExternalInput").ap() for k, v in data.items()}
    out = nc.dram_tensor("out", (P, KD, S), mybir.dt.float32, kind="ExternalOutput").ap()
    aps["XT"] = aps["XT"].rearrange("p (k s) -> p k s", s=S)
    build(nc, OUT=out, **aps)
    r = run(nc, [{f"in_{k}": v for k, v in data.items()}], core_ids=[0])
    return r.results[0]["out"].transpose(2, 1, 0).reshape(1, S, D)
```
